# Optimizing a Trainium2 kernel written in Bass

```python
import math
import jax
import jax.numpy as jnp
from jax import lax
import numpy as np
import jax, jax.numpy as jnp

D_MODEL = 1024
BATCH = 1
SEQ = 256
DEPTH = 2

CTX_LEN = 256
GRID_W = 64
QBLK = 128
ROPE_BASE = 10000.0
NORM_EPS = 1e-6
NEG_INF = -1e30

SWA_HEADS = 8
SWA_KV_HEADS = 2
SWA_HEAD_DIM = 64
SWA_WINDOW = 128

MLA_HEADS = 8
MLA_Q_RANK = 256
MLA_KV_RANK = 128
MLA_NOPE_DIM = 64
MLA_ROPE_DIM = 32
MLA_V_DIM = 64

DIFF_HEADS = 8
DIFF_HEAD_DIM = 64
DIFF_EPS = 1e-5

N_GROUPS = 4
EXPERTS_PER_GROUP = 8
N_EXPERTS = N_GROUPS * EXPERTS_PER_GROUP
TOP_K = 2
EXPERT_FF = 512
MOE_BLK = 128

AB_IN_WIDTHS = (SWA_HEADS * SWA_HEAD_DIM, SWA_KV_HEADS * SWA_HEAD_DIM, SWA_KV_HEADS * SWA_HEAD_DIM, MLA_Q_RANK, MLA_KV_RANK, MLA_ROPE_DIM)
AB_IN_WIDTH = 512 + 128 + 128 + 256 + 128 + 32
AB_OUT_WIDTH = SWA_HEADS * SWA_HEAD_DIM + MLA_HEADS * MLA_V_DIM
DIFF_IN_WIDTHS = (DIFF_HEADS * 2 * DIFF_HEAD_DIM, DIFF_HEADS * 2 * DIFF_HEAD_DIM, DIFF_HEADS * 2 * DIFF_HEAD_DIM)
DIFF_IN_WIDTH = 3 * DIFF_HEADS * 2 * DIFF_HEAD_DIM
DIFF_OUT_WIDTH = DIFF_HEADS * 2 * DIFF_HEAD_DIM


def _rmsnorm(x, g, eps=NORM_EPS):
    xf = x.astype(jnp.float32)
    y = xf * lax.rsqrt(jnp.mean(xf * xf, axis=-1, keepdims=True) + eps)
    return (y * g.astype(jnp.float32)).astype(x.dtype)

def _modulate(h, shift, scale):
    return h * (1 + scale) + shift

def _split(x, widths):
    idx = [int(i) for i in np.cumsum(widths)[:-1]]
    return jnp.split(x, idx, axis=-1)

def _axial_rope_tables(n_tokens, dim):
    rows = n_tokens // GRID_W
    row = jnp.repeat(jnp.arange(rows, dtype=jnp.float32), GRID_W)
    col = jnp.tile(jnp.arange(GRID_W, dtype=jnp.float32), rows)
    nf = dim // 4
    inv = ROPE_BASE ** (-jnp.arange(nf, dtype=jnp.float32) / nf)
    ang = jnp.concatenate([row[:, None] * inv, col[:, None] * inv], axis=-1)
    return jnp.cos(ang), jnp.sin(ang)

def _rope(x, tables):
    cos, sin = tables
    cos = cos[None, :, None, :]
    sin = sin[None, :, None, :]
    half = x.shape[-1] // 2
    x1 = x[..., :half].astype(jnp.float32)
    x2 = x[..., half:].astype(jnp.float32)
    return jnp.concatenate([x1 * cos - x2 * sin, x2 * cos + x1 * sin], axis=-1).astype(x.dtype)

def _dense_attention(q, k, v, scale):
    b, sq, h, d = q.shape
    dv = v.shape[-1]
    nb = sq // QBLK
    qb = jnp.moveaxis(q.reshape(b, nb, QBLK, h, d), 1, 0)

    def block(qi):
        s = jnp.einsum('bqhd,bkhd->bhqk', qi, k, preferred_element_type=jnp.float32) * scale
        p = jax.nn.softmax(s, axis=-1).astype(v.dtype)
        return jnp.einsum('bhqk,bkhd->bqhd', p, v)

    out = lax.map(block, qb)
    return jnp.moveaxis(out, 0, 1).reshape(b, sq, h, dv)

def _sink_softmax(s, sink_g):
    sk = jnp.broadcast_to(sink_g.astype(jnp.float32)[None, :, :, None, None], s.shape[:-1] + (1,))
    p = jax.nn.softmax(jnp.concatenate([s, sk], axis=-1), axis=-1)
    return p[..., :-1]

def _window_attention_with_sink(q, k, v, k_ctx, v_ctx, sink):
    b, s_len, hq, d = q.shape
    hkv = k.shape[2]
    g = hq // hkv
    dv = v.shape[-1]
    nb = s_len // QBLK
    kb_len = QBLK + 2 * SWA_WINDOW
    scale = d ** -0.5
    pad = ((0, 0), (SWA_WINDOW, SWA_WINDOW), (0, 0), (0, 0))
    kp = jnp.pad(k, pad)
    vp = jnp.pad(v, pad)
    qb = jnp.moveaxis(q.reshape(b, nb, QBLK, hkv, g, d), 1, 0)
    sink_g = sink.reshape(hkv, g)

    def block(args):
        i, qi = args
        start = i * QBLK
        kb = lax.dynamic_slice_in_dim(kp, start, kb_len, axis=1)
        vb = lax.dynamic_slice_in_dim(vp, start, kb_len, axis=1)
        qpos = start + jnp.arange(QBLK)
        kpos = start - SWA_WINDOW + jnp.arange(kb_len)
        mask = (jnp.abs(qpos[:, None] - kpos[None, :]) <= SWA_WINDOW) & ((kpos >= 0) & (kpos < s_len))[None, :]
        s_loc = jnp.einsum('bqhgd,bkhd->bhgqk', qi, kb, preferred_element_type=jnp.float32) * scale
        s_loc = jnp.where(mask, s_loc, NEG_INF)
        s_ctx = jnp.einsum('bqhgd,bkhd->bhgqk', qi, k_ctx, preferred_element_type=jnp.float32) * scale
        p = _sink_softmax(jnp.concatenate([s_loc, s_ctx], axis=-1), sink_g).astype(v.dtype)
        return (jnp.einsum('bhgqk,bkhd->bqhgd', p[..., :kb_len], vb)
                + jnp.einsum('bhgqk,bkhd->bqhgd', p[..., kb_len:], v_ctx))

    out = lax.map(block, (jnp.arange(nb), qb))
    return jnp.moveaxis(out, 0, 1).reshape(b, s_len, hq * dv)

def _context_sink_attention(q, k, v, sink):
    b, c_len, hq, d = q.shape
    hkv = k.shape[2]
    g = hq // hkv
    qg = q.reshape(b, c_len, hkv, g, d)
    s = jnp.einsum('bqhgd,bkhd->bhgqk', qg, k, preferred_element_type=jnp.float32) * (d ** -0.5)
    p = _sink_softmax(s, sink.reshape(hkv, g)).astype(v.dtype)
    return jnp.einsum('bhgqk,bkhd->bqhgd', p, v).reshape(b, c_len, hq * v.shape[-1])

def _swa_mla_mixer(h_lat, h_ctx, w_in, q_norm, w_uq, kv_norm, w_ukv, sink, w_out, rope_a, rope_b, ctx_out):
    def project(h):
        b, n, _ = h.shape
        aq, ak, av, cq, ckv, kr = _split(h @ w_in, AB_IN_WIDTHS)
        aq = aq.reshape(b, n, SWA_HEADS, SWA_HEAD_DIM)
        ak = ak.reshape(b, n, SWA_KV_HEADS, SWA_HEAD_DIM)
        av = av.reshape(b, n, SWA_KV_HEADS, SWA_HEAD_DIM)
        q = (_rmsnorm(cq, q_norm) @ w_uq).reshape(b, n, MLA_HEADS, MLA_NOPE_DIM + MLA_ROPE_DIM)
        kv = (_rmsnorm(ckv, kv_norm) @ w_ukv).reshape(b, n, MLA_HEADS, MLA_NOPE_DIM + MLA_V_DIM)
        return (aq, ak, av, q[..., :MLA_NOPE_DIM], q[..., MLA_NOPE_DIM:],
                kv[..., :MLA_NOPE_DIM], kr[:, :, None, :], kv[..., MLA_NOPE_DIM:])

    aq_l, ak_l, av_l, qn_l, qr_l, kn_l, kr_l, mv_l = project(h_lat)
    aq_c, ak_c, av_c, qn_c, qr_c, kn_c, kr_c, mv_c = project(h_ctx)
    aq_l = _rope(aq_l, rope_a)
    ak_l = _rope(ak_l, rope_a)
    qr_l = _rope(qr_l, rope_b)
    kr_l = _rope(kr_l, rope_b)

    def mla_qk(qn, qr, kn, kr):
        q = jnp.concatenate([qn, qr], axis=-1)
        k = jnp.concatenate([kn, jnp.broadcast_to(kr, kn.shape[:-1] + (MLA_ROPE_DIM,))], axis=-1)
        return q, k

    q_l, k_l = mla_qk(qn_l, qr_l, kn_l, kr_l)
    q_c, k_c = mla_qk(qn_c, qr_c, kn_c, kr_c)
    mla_scale = (MLA_NOPE_DIM + MLA_ROPE_DIM) ** -0.5
    b, s_len = h_lat.shape[0], h_lat.shape[1]
    o_a = _window_attention_with_sink(aq_l, ak_l, av_l, ak_c, av_c, sink)
    o_b = _dense_attention(q_l, jnp.concatenate([k_l, k_c], axis=1), jnp.concatenate([mv_l, mv_c], axis=1), mla_scale)
    out_lat = jnp.concatenate([o_a, o_b.reshape(b, s_len, -1)], axis=-1) @ w_out
    if not ctx_out:
        return out_lat, None
    c_len = h_ctx.shape[1]
    o_a_c = _context_sink_attention(aq_c, ak_c, av_c, sink)
    o_b_c = _dense_attention(q_c, k_c, mv_c, mla_scale).reshape(b, c_len, -1)
    out_ctx = jnp.concatenate([o_a_c, o_b_c], axis=-1) @ w_out
    return out_lat, out_ctx

def _diff_mixer(h_lat, h_ctx, w_in, lq1, lk1, lq2, lk2, subln, w_out, lambda_init, rope, ctx_out):
    def project(h):
        b, n, _ = h.shape
        q, k, v = _split(h @ w_in, DIFF_IN_WIDTHS)
        q = q.reshape(b, n, DIFF_HEADS, 2, DIFF_HEAD_DIM)
        k = k.reshape(b, n, DIFF_HEADS, 2, DIFF_HEAD_DIM)
        v = v.reshape(b, n, DIFF_HEADS, 2 * DIFF_HEAD_DIM)
        return q[..., 0, :], q[..., 1, :], k[..., 0, :], k[..., 1, :], v

    q1_l, q2_l, k1_l, k2_l, v_l = project(h_lat)
    q1_c, q2_c, k1_c, k2_c, v_c = project(h_ctx)
    q1_l = _rope(q1_l, rope)
    q2_l = _rope(q2_l, rope)
    k1_l = _rope(k1_l, rope)
    k2_l = _rope(k2_l, rope)
    lam = (jnp.exp(jnp.sum(lq1.astype(jnp.float32) * lk1.astype(jnp.float32)))
           - jnp.exp(jnp.sum(lq2.astype(jnp.float32) * lk2.astype(jnp.float32))) + lambda_init)
    scale = DIFF_HEAD_DIM ** -0.5

    def combine(a1, a2):
        o = a1 - lam.astype(a1.dtype) * a2
        o = _rmsnorm(o, subln, DIFF_EPS) * (1.0 - lambda_init)
        return o.reshape(o.shape[0], o.shape[1], -1) @ w_out

    k1_all = jnp.concatenate([k1_l, k1_c], axis=1)
    k2_all = jnp.concatenate([k2_l, k2_c], axis=1)
    v_all = jnp.concatenate([v_l, v_c], axis=1)
    out_lat = combine(_dense_attention(q1_l, k1_all, v_all, scale), _dense_attention(q2_l, k2_all, v_all, scale))
    if not ctx_out:
        return out_lat, None
    out_ctx = combine(_dense_attention(q1_c, k1_c, v_c, scale), _dense_attention(q2_c, k2_c, v_c, scale))
    return out_lat, out_ctx

def _hier_moe(h, w_group, b_group, w_expert, b_expert, w1, w3, w2):
    n_tok, d = h.shape
    g_logits = jnp.dot(h, w_group, preferred_element_type=jnp.float32) + b_group.astype(jnp.float32)
    g_prob = jax.nn.softmax(g_logits, axis=-1)
    grp = jnp.argmax(g_logits, axis=-1).astype(jnp.int32)
    p_grp = jnp.take_along_axis(g_prob, grp[:, None], axis=-1)
    e_logits = (jnp.dot(h, w_expert, preferred_element_type=jnp.float32) + b_expert.astype(jnp.float32)).reshape(n_tok, N_GROUPS, EXPERTS_PER_GROUP)
    e_logits = jnp.take_along_axis(e_logits, grp[:, None, None], axis=1)[:, 0]
    top_p, top_i = lax.top_k(jax.nn.softmax(e_logits, axis=-1), TOP_K)
    gate = p_grp * top_p / jnp.sum(top_p, axis=-1, keepdims=True)
    eid = grp[:, None] * EXPERTS_PER_GROUP + top_i.astype(jnp.int32)

    n_assign = n_tok * TOP_K
    flat_e = eid.reshape(n_assign)
    flat_tok = jnp.repeat(jnp.arange(n_tok, dtype=jnp.int32), TOP_K)
    flat_gate = gate.reshape(n_assign)
    order = jnp.argsort(flat_e)
    se = flat_e[order]
    stok = flat_tok[order]
    sgate = flat_gate[order]
    counts = jnp.zeros((N_EXPERTS,), jnp.int32).at[flat_e].add(1)
    padded = (counts + MOE_BLK - 1) // MOE_BLK * MOE_BLK
    pad_end = jnp.cumsum(padded)
    pad_start = pad_end - padded
    start = jnp.cumsum(counts) - counts
    dest = pad_start[se] + (jnp.arange(n_assign, dtype=jnp.int32) - start[se])
    n_blocks = (n_assign + N_EXPERTS * (MOE_BLK - 1) + MOE_BLK - 1) // MOE_BLK
    n_slots = n_blocks * MOE_BLK
    slot_tok = jnp.full((n_slots,), n_tok, jnp.int32).at[dest].set(stok)
    h_pad = jnp.concatenate([h, jnp.zeros((1, d), h.dtype)], axis=0)
    xb = h_pad[slot_tok].reshape(n_blocks, MOE_BLK, d)
    block_e = jnp.minimum(jnp.searchsorted(pad_end, jnp.arange(n_blocks, dtype=jnp.int32) * MOE_BLK, side='right'), N_EXPERTS - 1)

    def expert_block(args):
        xi, e = args
        return (jax.nn.silu(xi @ w1[e]) * (xi @ w3[e])) @ w2[e]

    yb = lax.map(expert_block, (xb, block_e)).reshape(n_slots, d)
    contrib = yb[dest] * sgate[:, None].astype(yb.dtype)
    return jnp.zeros((n_tok, d), h.dtype).at[stok].add(contrib)

def first_inputs(seed: int = 0) -> dict:
    key = jax.random.key(seed)
    ks = jax.random.split(key, 30)
    d = D_MODEL
    n_even = (DEPTH + 1) // 2
    n_odd = DEPTH // 2

    def nrm(k, shape, scale):
        return jax.random.normal(k, shape, jnp.float32) * scale

    def gain(k, shape):
        return 1.0 + 0.1 * jax.random.normal(k, shape, jnp.float32)

    return {
        'x': nrm(ks[0], (BATCH, SEQ, d), 1.0),
        'c': nrm(ks[1], (BATCH, d), 1.0),
        'ctx': nrm(ks[2], (BATCH, CTX_LEN, d), 1.0),
        'c_ctx': nrm(ks[3], (d,), 1.0),
        'norm_mix': gain(ks[4], (DEPTH, d)),
        'norm_ffn': gain(ks[5], (DEPTH, d)),
        'ada_w': nrm(ks[6], (DEPTH, d, 6 * d), 0.5 * d ** -0.5),
        'ada_b': nrm(ks[7], (DEPTH, 6 * d), 0.02),
        'ab_w_in': nrm(ks[8], (n_even, d, AB_IN_WIDTH), d ** -0.5),
        'mla_q_norm': gain(ks[9], (n_even, MLA_Q_RANK)),
        'mla_w_uq': nrm(ks[10], (n_even, MLA_Q_RANK, MLA_HEADS * (MLA_NOPE_DIM + MLA_ROPE_DIM)), MLA_Q_RANK ** -0.5),
        'mla_kv_norm': gain(ks[11], (n_even, MLA_KV_RANK)),
        'mla_w_ukv': nrm(ks[12], (n_even, MLA_KV_RANK, MLA_HEADS * (MLA_NOPE_DIM + MLA_V_DIM)), MLA_KV_RANK ** -0.5),
        'swa_sink': nrm(ks[13], (n_even, SWA_HEADS), 1.0),
        'ab_w_out': nrm(ks[14], (n_even, AB_OUT_WIDTH, d), AB_OUT_WIDTH ** -0.5),
        'diff_w_in': nrm(ks[15], (n_odd, d, DIFF_IN_WIDTH), d ** -0.5),
        'diff_lambda_q1': nrm(ks[16], (n_odd, DIFF_HEAD_DIM), 0.1),
        'diff_lambda_k1': nrm(ks[17], (n_odd, DIFF_HEAD_DIM), 0.1),
        'diff_lambda_q2': nrm(ks[18], (n_odd, DIFF_HEAD_DIM), 0.1),
        'diff_lambda_k2': nrm(ks[19], (n_odd, DIFF_HEAD_DIM), 0.1),
        'diff_subln': gain(ks[20], (n_odd, 2 * DIFF_HEAD_DIM)),
        'diff_w_out': nrm(ks[21], (n_odd, DIFF_OUT_WIDTH, d), DIFF_OUT_WIDTH ** -0.5),
        'router_group_w': nrm(ks[22], (DEPTH, d, N_GROUPS), d ** -0.5),
        'router_group_b': nrm(ks[23], (DEPTH, N_GROUPS), 0.01),
        'router_expert_w': nrm(ks[24], (DEPTH, d, N_EXPERTS), d ** -0.5),
        'router_expert_b': nrm(ks[25], (DEPTH, N_EXPERTS), 0.01),
        'expert_w1': nrm(ks[26], (DEPTH, N_EXPERTS, d, EXPERT_FF), d ** -0.5),
        'expert_w3': nrm(ks[27], (DEPTH, N_EXPERTS, d, EXPERT_FF), d ** -0.5),
        'expert_w2': nrm(ks[28], (DEPTH, N_EXPERTS, EXPERT_FF, d), EXPERT_FF ** -0.5),
        'final_norm': gain(ks[29], (d,)),
    }

def first_block(x, c, ctx, c_ctx, norm_mix, norm_ffn, ada_w, ada_b, ab_w_in, mla_q_norm, mla_w_uq, mla_kv_norm, mla_w_ukv, swa_sink, ab_w_out, diff_w_in, diff_lambda_q1, diff_lambda_k1, diff_lambda_q2, diff_lambda_k2, diff_subln, diff_w_out, router_group_w, router_group_b, router_expert_w, router_expert_b, expert_w1, expert_w3, expert_w2, final_norm):
    b, s_len, d = x.shape
    rope_64 = _axial_rope_tables(s_len, SWA_HEAD_DIM)
    rope_32 = _axial_rope_tables(s_len, MLA_ROPE_DIM)
    sc = jax.nn.silu(c)
    scc = jax.nn.silu(c_ctx)
    x_lat = x
    x_ctx = ctx
    n_lat = b * s_len
    for l in range(DEPTH):
        last = l == DEPTH - 1
        mod_l = [m[:, None, :] for m in jnp.split(sc @ ada_w[l] + ada_b[l], 6, axis=-1)]
        mod_c = jnp.split(scc @ ada_w[l] + ada_b[l], 6, axis=-1)
        h_lat = _modulate(_rmsnorm(x_lat, norm_mix[l]), mod_l[0], mod_l[1])
        h_ctx = _modulate(_rmsnorm(x_ctx, norm_mix[l]), mod_c[0], mod_c[1])
        j = l // 2
        if l % 2 == 0:
            o_lat, o_ctx = _swa_mla_mixer(h_lat, h_ctx, ab_w_in[j], mla_q_norm[j], mla_w_uq[j], mla_kv_norm[j], mla_w_ukv[j], swa_sink[j], ab_w_out[j], rope_64, rope_32, not last)
        else:
            lambda_init = 0.8 - 0.6 * math.exp(-0.3 * l)
            o_lat, o_ctx = _diff_mixer(h_lat, h_ctx, diff_w_in[j], diff_lambda_q1[j], diff_lambda_k1[j], diff_lambda_q2[j], diff_lambda_k2[j], diff_subln[j], diff_w_out[j], lambda_init, rope_64, not last)
        x_lat = x_lat + mod_l[2] * o_lat
        h_lat = _modulate(_rmsnorm(x_lat, norm_ffn[l]), mod_l[3], mod_l[4])
        if last:
            tokens = h_lat.reshape(n_lat, d)
        else:
            x_ctx = x_ctx + mod_c[2] * o_ctx
            h_ctx = _modulate(_rmsnorm(x_ctx, norm_ffn[l]), mod_c[3], mod_c[4])
            tokens = jnp.concatenate([h_lat.reshape(n_lat, d), h_ctx.reshape(-1, d)], axis=0)
        y = _hier_moe(tokens, router_group_w[l], router_group_b[l], router_expert_w[l], router_expert_b[l], expert_w1[l], expert_w3[l], expert_w2[l])
        x_lat = x_lat + mod_l[5] * y[:n_lat].reshape(b, s_len, d)
        if not last:
            x_ctx = x_ctx + mod_c[5] * y[n_lat:].reshape(x_ctx.shape)
    return _rmsnorm(x_lat, final_norm)


DEPTH_2 = 1

EPS = 1e-6
N_BRANCH = 3
BRANCH_WIDTH = D_MODEL // 2
GLA_HEADS = 4
GLA_DV = BRANCH_WIDTH // GLA_HEADS
GLA_DK = GLA_DV // 2
GLA_RANK = 16
GLA_TAU = 16.0
GLA_CHUNK = 16
GLA_QK = GLA_HEADS * GLA_DK
GLA_V = GLA_HEADS * GLA_DV
SC_WIDTH = BRANCH_WIDTH
CONV_K = 3
DIL_PATTERNS = ((128, 1), (512, 4), (2048, 16))
DIL_GROUPS = len(DIL_PATTERNS)
DIL_HEADS = 4
DIL_HD = BRANCH_WIDTH // DIL_HEADS
DIL_W = DIL_GROUPS * DIL_HEADS * DIL_HD
DIL_BLOCK = 128
ROPE_THETA = 10000.0
D_FF = 2816

IN_SIZES = (GLA_QK, GLA_QK, GLA_V, GLA_V, GLA_RANK,
            SC_WIDTH, SC_WIDTH, SC_WIDTH,
            DIL_W, DIL_W, DIL_W)
IN_COLS = sum(IN_SIZES)


def rmsnorm(x, g):
    xf = x.astype(jnp.float32)
    r = lax.rsqrt(jnp.mean(xf * xf, axis=-1, keepdims=True) + EPS)
    return (xf * r).astype(x.dtype) * g

def causal_dwconv(u, w):
    K = w.shape[0]
    S = u.shape[1]
    up = jnp.pad(u, ((0, 0), (K - 1, 0), (0, 0)))
    y = w[0] * up[:, 0:S]
    for k in range(1, K):
        y = y + w[k] * up[:, k:k + S]
    return y

def rope(x, pos):
    hd = x.shape[-1]
    inv = ROPE_THETA ** (-jnp.arange(0, hd, 2, dtype=jnp.float32) / hd)
    ang = pos.astype(jnp.float32)[..., None] * inv
    cos = jnp.cos(ang)[:, :, None, None, :]
    sin = jnp.sin(ang)[:, :, None, None, :]
    xf = x.astype(jnp.float32)
    x1, x2 = xf[..., :hd // 2], xf[..., hd // 2:]
    return jnp.concatenate([x1 * cos - x2 * sin, x2 * cos + x1 * sin], axis=-1).astype(x.dtype)

def gla_branch(q, k, v, g, a_low, w_a_up, b_a, norm_g):
    B, S, _ = q.shape
    H, C = GLA_HEADS, GLA_CHUNK
    N = S // C
    f32 = jnp.float32
    loga = jax.nn.log_sigmoid((a_low.astype(f32) @ w_a_up.astype(f32)) + b_a.astype(f32)) / GLA_TAU

    def chunks(t, d):
        return t.astype(f32).reshape(B, N, C, H, d).transpose(0, 3, 1, 2, 4)

    qc = chunks(q, GLA_DK) * (GLA_DK ** -0.5)
    kc = chunks(k, GLA_DK)
    vc = chunks(v, GLA_DV)
    lc = jnp.cumsum(chunks(loga, GLA_DK), axis=3)

    causal = jnp.tril(jnp.ones((C, C), dtype=bool))
    rel = lc[..., :, None, :] - lc[..., None, :, :]
    decay = jnp.exp(jnp.where(causal[:, :, None], rel, -jnp.inf))
    scores = jnp.einsum('bhnid,bhnjd,bhnijd->bhnij', qc, kc, decay)
    o_intra = jnp.einsum('bhnij,bhnje->bhnie', scores, vc)

    lend = lc[..., -1:, :]
    q_in = qc * jnp.exp(lc)
    k_in = kc * jnp.exp(lend - lc)
    dec_chunk = jnp.exp(lend[..., 0, :])

    def step(state, xs):
        qn, kn, vn, dn = xs
        o = jnp.einsum('bhid,bhde->bhie', qn, state)
        state = state * dn[..., None] + jnp.einsum('bhjd,bhje->bhde', kn, vn)
        return state, o

    xs = (jnp.moveaxis(q_in, 2, 0), jnp.moveaxis(k_in, 2, 0),
          jnp.moveaxis(vc, 2, 0), jnp.moveaxis(dec_chunk, 2, 0))
    s0 = jnp.zeros((B, H, GLA_DK, GLA_DV), f32)
    _, o_inter = lax.scan(step, s0, xs)
    o = o_intra + jnp.moveaxis(o_inter, 0, 2)
    o = o.transpose(0, 2, 3, 1, 4).reshape(B, S, H, GLA_DV).astype(v.dtype)
    o = rmsnorm(o, norm_g).reshape(B, S, GLA_V)
    return o * jax.nn.silu(g)

def strided_window_attn(q, k, v, span, dil):
    B, S, H, D = q.shape
    L = S // dil
    BLK = DIL_BLOCK
    nb = -(-L // BLK)
    Lp = nb * BLK

    def to_sub(t):
        return t.reshape(B, L, dil, H, D).transpose(0, 2, 3, 1, 4)

    qs, ks, vs = to_sub(q), to_sub(k), to_sub(v)
    qb = jnp.pad(qs, ((0, 0), (0, 0), (0, 0), (0, Lp - L), (0, 0))).reshape(B, dil, H, nb, BLK, D)

    def kv_blocks(t):
        tp = jnp.pad(t, ((0, 0), (0, 0), (0, 0), (BLK, Lp - L), (0, 0)))
        prev = tp[:, :, :, :Lp].reshape(B, dil, H, nb, BLK, D)
        cur = tp[:, :, :, BLK:].reshape(B, dil, H, nb, BLK, D)
        return jnp.concatenate([prev, cur], axis=4)

    kb, vb = kv_blocks(ks), kv_blocks(vs)
    i = jnp.arange(BLK)[:, None]
    m = jnp.arange(2 * BLK)[None, :]
    blk = jnp.arange(nb)[:, None, None]
    dist = i + BLK - m
    key_idx = (blk - 1) * BLK + m
    valid = (dist >= 0) & (dist <= span) & (key_idx >= 0)

    s = jnp.einsum('brhnid,brhnmd->brhnim', qb, kb).astype(jnp.float32) * (D ** -0.5)
    s = jnp.where(valid, s, -jnp.inf)
    mx = jnp.max(s, axis=-1, keepdims=True)
    p = jnp.exp(s - mx)
    den = jnp.sum(p, axis=-1, keepdims=True)
    o = jnp.einsum('brhnim,brhnmd->brhnid', p, vb.astype(jnp.float32)) / den
    lse = (mx + jnp.log(den))[..., 0]

    o = o.reshape(B, dil, H, Lp, D)[:, :, :, :L].transpose(0, 3, 1, 2, 4).reshape(B, S, H, D)
    lse = lse.reshape(B, dil, H, Lp)[:, :, :, :L].transpose(0, 3, 1, 2).reshape(B, S, H)
    return o, lse

def dilated_branch(dq, dk, dv, pos):
    B, S, _ = dq.shape
    shp = (B, S, DIL_GROUPS, DIL_HEADS, DIL_HD)
    q = rope(dq.reshape(shp), pos)
    k = rope(dk.reshape(shp), pos)
    v = dv.reshape(shp)
    outs, lses = [], []
    for gi, (win, dil) in enumerate(DIL_PATTERNS):
        o, lse = strided_window_attn(q[:, :, gi], k[:, :, gi], v[:, :, gi], win // dil, dil)
        outs.append(o)
        lses.append(lse)
    w = jax.nn.softmax(jnp.stack(lses, axis=0), axis=0)
    o = jnp.sum(w[..., None] * jnp.stack(outs, axis=0), axis=0)
    return o.reshape(B, S, DIL_HEADS * DIL_HD).astype(dq.dtype)

def second_inputs(seed: int = 0) -> dict:
    key = jax.random.key(seed)
    ks = jax.random.split(key, 24)
    f32 = jnp.float32

    def nrm(k, shape, scale):
        return jax.random.normal(k, shape, f32) * scale

    def gain(k, shape):
        return 1.0 + 0.02 * jax.random.normal(k, shape, f32)

    x = jax.random.normal(ks[0], (BATCH, SEQ, D_MODEL), f32)
    offset = jax.random.randint(ks[1], (BATCH, 1), 0, 4096, dtype=jnp.int32)
    positions = (offset + jnp.arange(SEQ, dtype=jnp.int32)[None, :]).astype(jnp.int32)
    return {
        "x": x,
        "positions": positions,
        "w_in": nrm(ks[2], (DEPTH_2, D_MODEL, IN_COLS), D_MODEL ** -0.5),
        "w_alpha_up": nrm(ks[3], (DEPTH_2, GLA_RANK, GLA_QK), GLA_RANK ** -0.5),
        "b_alpha": nrm(ks[4], (DEPTH_2, GLA_QK), 0.1),
        "gla_norm_g": gain(ks[5], (DEPTH_2, GLA_DV)),
        "sc_conv_w": nrm(ks[6], (DEPTH_2, CONV_K, SC_WIDTH), CONV_K ** -0.5),
        "w_gate": nrm(ks[7], (DEPTH_2, D_MODEL, N_BRANCH * D_MODEL), D_MODEL ** -0.5),
        "b_gate": nrm(ks[8], (DEPTH_2, N_BRANCH * D_MODEL), 0.02),
        "w_branch": nrm(ks[9], (DEPTH_2, N_BRANCH, BRANCH_WIDTH, D_MODEL), BRANCH_WIDTH ** -0.5),
        "w_mix_out": nrm(ks[10], (DEPTH_2, D_MODEL, D_MODEL), D_MODEL ** -0.5),
        "pre_mix_g": gain(ks[11], (DEPTH_2, D_MODEL)),
        "post_mix_g": gain(ks[12], (DEPTH_2, D_MODEL)),
        "pre_ffn_g": gain(ks[13], (DEPTH_2, D_MODEL)),
        "post_ffn_g": gain(ks[14], (DEPTH_2, D_MODEL)),
        "w_ff_gate": nrm(ks[15], (DEPTH_2, D_MODEL, D_FF), D_MODEL ** -0.5),
        "w_ff_up": nrm(ks[16], (DEPTH_2, D_MODEL, D_FF), D_MODEL ** -0.5),
        "ff_conv_w": nrm(ks[17], (DEPTH_2, CONV_K, D_FF), CONV_K ** -0.5),
        "ff_conv_b": nrm(ks[18], (DEPTH_2, D_FF), 0.02),
        "w_ff_down": nrm(ks[19], (DEPTH_2, D_FF, D_MODEL), D_FF ** -0.5),
    }

def second_block(x, positions, w_in, w_alpha_up, b_alpha, gla_norm_g, sc_conv_w, w_gate, b_gate,
              w_branch, w_mix_out, pre_mix_g, post_mix_g, pre_ffn_g, post_ffn_g,
              w_ff_gate, w_ff_up, ff_conv_w, ff_conv_b, w_ff_down):
    B, S, _ = x.shape
    split_points = np.cumsum(np.array(IN_SIZES))[:-1].tolist()
    for l in range(DEPTH_2):
        h = rmsnorm(x, pre_mix_g[l])
        z = h @ w_in[l]
        (g_q, g_k, g_v, g_o, a_low, sc_b, sc_c, sc_x,
         d_q, d_k, d_v) = jnp.split(z, split_points, axis=-1)

        y_gla = gla_branch(g_q, g_k, g_v, g_o, a_low, w_alpha_up[l], b_alpha[l], gla_norm_g[l])
        y_sc = sc_b * causal_dwconv(sc_c * sc_x, sc_conv_w[l])
        y_dil = dilated_branch(d_q, d_k, d_v, positions)

        br = jnp.stack([y_gla, y_sc, y_dil], axis=2)
        proj = jnp.einsum('bsgc,gcd->bsgd', br, w_branch[l])
        gates = jax.nn.sigmoid(h @ w_gate[l] + b_gate[l]).reshape(B, S, N_BRANCH, D_MODEL)
        merged = jnp.sum(gates * proj, axis=2)
        x = x + rmsnorm(merged @ w_mix_out[l], post_mix_g[l])

        h = rmsnorm(x, pre_ffn_g[l])
        gt = causal_dwconv(h @ w_ff_gate[l], ff_conv_w[l]) + ff_conv_b[l]
        y = (jax.nn.gelu(gt, approximate=True) * (h @ w_ff_up[l])) @ w_ff_down[l]
        x = x + rmsnorm(y, post_ffn_g[l])
    return x


def setup_inputs(seed=0):
    out = dict(first_inputs(seed))
    for name, value in second_inputs(seed + 1).items():
        if name != "x":
            out[name + "_2"] = value
    return out


def reference(
    x, c, ctx, c_ctx, norm_mix, norm_ffn, ada_w, ada_b, ab_w_in, mla_q_norm, mla_w_uq,
    mla_kv_norm, mla_w_ukv, swa_sink, ab_w_out, diff_w_in, diff_lambda_q1, diff_lambda_k1,
    diff_lambda_q2, diff_lambda_k2, diff_subln, diff_w_out, router_group_w, router_group_b,
    router_expert_w, router_expert_b, expert_w1, expert_w3, expert_w2, final_norm, positions_2,
    w_in_2, w_alpha_up_2, b_alpha_2, gla_norm_g_2, sc_conv_w_2, w_gate_2, b_gate_2, w_branch_2,
    w_mix_out_2, pre_mix_g_2, post_mix_g_2, pre_ffn_g_2, post_ffn_g_2, w_ff_gate_2, w_ff_up_2,
    ff_conv_w_2, ff_conv_b_2, w_ff_down_2,
):
    x = first_block(
        x, c, ctx, c_ctx, norm_mix, norm_ffn, ada_w, ada_b, ab_w_in, mla_q_norm, mla_w_uq,
        mla_kv_norm, mla_w_ukv, swa_sink, ab_w_out, diff_w_in, diff_lambda_q1, diff_lambda_k1,
        diff_lambda_q2, diff_lambda_k2, diff_subln, diff_w_out, router_group_w, router_group_b,
        router_expert_w, router_expert_b, expert_w1, expert_w3, expert_w2, final_norm,
    )
    return second_block(
        x, positions_2, w_in_2, w_alpha_up_2, b_alpha_2, gla_norm_g_2, sc_conv_w_2, w_gate_2,
        b_gate_2, w_branch_2, w_mix_out_2, pre_mix_g_2, post_mix_g_2, pre_ffn_g_2, post_ffn_g_2,
        w_ff_gate_2, w_ff_up_2, ff_conv_w_2, ff_conv_b_2, w_ff_down_2,
    )


_drawn_inputs = setup_inputs


def setup_inputs(seed=0):
    import zlib

    import numpy as np

    out = dict(_drawn_inputs(seed))
    spreads = {}
    factors = {'mla_q_norm': 8.0,
     'mla_kv_norm': 2.829,
     'swa_sink': 8.0,
     'router_expert_b': 3.368,
     'b_alpha_2': 2.971,
     'gla_norm_g_2': 6.174,
     'b_gate_2': 8.0,
     'post_mix_g_2': 3.455,
     'pre_ffn_g_2': 3.371,
     'post_ffn_g_2': 4.94,
     'ff_conv_b_2': 4.982}
    for name, (base, spread) in spreads.items():
        noise = np.random.default_rng([zlib.crc32(name.encode()), seed]).standard_normal(out[name].shape)
        drawn = base * np.exp(spread * noise) if base else spread * noise
        out[name] = jnp.asarray(drawn.astype(out[name].dtype))
    for name, factor in factors.items():
        out[name] = (out[name] * factor).astype(out[name].dtype)
    return out
```

```python
import math
from contextlib import ExitStack

import numpy as np
import concourse.bass as bass
from concourse import mybir

F32 = mybir.dt.float32
I32 = mybir.dt.int32
U32 = mybir.dt.uint32
ACT = mybir.ActivationFunctionType
ALU = mybir.AluOpType
AX = mybir.AxisListType

P = 128
D = 1024
DK = D // P
S = 256
T_LAT = S // P
T_ALL = 2 * T_LAT
SLOTS = 8
BANK = 512
NEG = -1.0e30
STOP = None


class Tally:

    def __init__(self, sem):
        self.sem, self.n = sem, 0

    def mark(self, ins, by=1):
        ins.then_inc(self.sem, by)
        self.n += by
        return self.n


class Signal:

    def __init__(self, sem):
        self.sem, self.base = sem, 0

    def at(self, v):
        return self.sem, self.base + v


class Core:

    def __init__(self, nc, ctx):
        self.nc, self.ctx = nc, ctx
        sem = lambda n: ctx.enter_context(nc.semaphore(n))
        self.tensor_done = Tally(sem("tensor_done"))
        self.act_evac = Tally(sem("act_evac"))
        self.dve_evac = Tally(sem("dve_evac"))
        self.dve_step = Tally(sem("dve_step"))
        self.act_step = Tally(sem("act_step"))
        self.pool_step = Tally(sem("pool_step"))
        self.load_done = Tally(sem("load_done"))
        self.store_done = Tally(sem("store_done"))
        self.scores_ready = Signal(sem("scores_ready"))
        self.max_ready = Signal(sem("max_ready"))
        self.probs_ready = Signal(sem("probs_ready"))
        self.turned = Signal(sem("probs_turned"))
        self.turned_copied = Signal(sem("turned_copied"))
        self.mixed = Signal(sem("values_mixed"))
        self.out_done = Signal(sem("out_done"))
        self.slot_full = [Tally(sem(f"slot_full{i}")) for i in range(SLOTS)]
        self.psum = ctx.enter_context(nc.psum_tensor("psum", [P, 8, BANK], F32))
        self.ring = [self.sb(f"ring{i}", [P, 4, BANK]) for i in range(SLOTS)]
        self.chunks, self.issued, self.taken, self.used_at = [], 0, 0, []

    def sb(self, name, shape, dt=F32, where=None):
        return (where or self.ctx).enter_context(self.nc.sbuf_tensor(name, shape, dt))

    def plan(self, w, k_rows, n_cols, n_first=0):
        for n0 in range(n_first, n_first + n_cols, BANK):
            nn = min(BANK, n_first + n_cols - n0)
            for k0 in range(0, k_rows, 4 * P):
                kt = min(4, (k_rows - k0) // P)
                self.chunks.append((w[k0:k0 + kt * P, n0:n0 + nn].rearrange("(j p) n -> p j n", p=P), kt, nn))

    def pump(self, sp):
        while self.issued < len(self.chunks):
            j = self.issued
            if j >= SLOTS:
                if j - SLOTS >= len(self.used_at):
                    break
                sp.wait_ge(self.tensor_done.sem, self.used_at[j - SLOTS])
            src, kt, nn = self.chunks[j]
            self.slot_full[j % SLOTS].mark(sp.dma_start(self.ring[j % SLOTS][:, 0:kt, 0:nn], src), 16)
            self.issued += 1

    def take(self, pe, kt, nn):
        j = self.taken
        self.taken += 1
        assert self.chunks[j][1:] == (kt, nn), (j, self.chunks[j][1:], kt, nn)
        pe.wait_ge(self.slot_full[j % SLOTS].sem, 16 * (j // SLOTS + 1))
        return self.ring[j % SLOTS][:, 0:kt, 0:nn]

    def used(self, at):
        self.used_at.append(at)


def chain(eng, tally, ins):
    eng.wait_ge(tally.sem, tally.mark(ins))


def banks_phase(k, groups, streams=False):
    nc = k.nc
    act0, dve0 = k.act_evac.n, k.dve_evac.n
    filled = []
    with nc.Block(no_gpsimd_drain=True) as block:
        @block.tensor
        def _(pe):
            holder = [None] * 8
            emptied = {"act": act0, "dve": dve0}
            at = 0
            for fill, empties, *after in groups:
                if after and emptied["act"] > act0:
                    pe.wait_ge(k.act_evac.sem, emptied["act"])
                if after and emptied["dve"] > dve0:
                    pe.wait_ge(k.dve_evac.sem, emptied["dve"])
                mine = [(at + i) % 8 for i in range(len(empties))]
                at += len(empties)
                for b in mine:
                    if holder[b] is not None:
                        pe.wait_ge(*holder[b])
                last = None
                for last in fill(pe, [k.psum[:, b, :] for b in mine]):
                    done = k.tensor_done.mark(last)
                filled.append(done)
                for b, (who, _) in zip(mine, empties):
                    emptied[who] += 1
                    holder[b] = (k.act_evac.sem if who == "act" else k.dve_evac.sem, emptied[who])

        def drain(eng, who, tally):
            at = 0
            for g, (_, empties, *_) in enumerate(groups):
                if any(w == who for w, _ in empties):
                    eng.wait_ge(k.tensor_done.sem, filled[g])
                for w, empty in empties:
                    if w == who:
                        tally.mark(empty(k.psum[:, at % 8, :]))
                    at += 1
            eng.wait_ge(tally.sem, tally.n)

        @block.scalar
        def _(act):
            drain(act, "act", k.act_evac)

        @block.vector
        def _(dve):
            drain(dve, "dve", k.dve_evac)

        @block.sync
        def _(sp):
            k.pump(sp)


def copy_by(k, who, out, src):
    return k.nc.scalar.copy(out, src) if who == "act" else k.nc.vector.tensor_copy(out, src)


def turns():
    i = 0
    while True:
        yield ("act", "dve")[i % 2]
        i += 1


def project_groups(k, lhs, k_tiles, rows, n_cols, empty, who=None):
    groups = []
    turn = turns()
    for n0 in range(0, n_cols, BANK):
        nn = min(BANK, n_cols - n0)

        def fill(pe, banks, nn=nn):
            for k0 in range(0, k_tiles, 4):
                kt = min(4, k_tiles - k0)
                w = k.take(pe, kt, nn)
                for r, m in enumerate(rows):
                    for j in range(kt):
                        mm = k.nc.tensor.matmul(banks[r][0:m, 0:nn], lhs(k0 + j, r), w[:, j, :],
                                                start=(k0 + j == 0), stop=(k0 + j == k_tiles - 1))
                yield mm
                k.used(k.tensor_done.n)

        empties = []
        for r, m in enumerate(rows):
            w = who or next(turn)
            empties.append((w, lambda bank, w=w, r=r, n0=n0, nn=nn, m=m: empty(w, r, n0, nn, bank[0:m, 0:nn])))
        groups.append((fill, empties))
    return groups


def project_column_groups(k, rhs, k_tiles, n_rhs, n_cols, empty, who=None):
    groups = []
    turn = turns()
    for n0 in range(0, n_cols, BANK):
        nn = min(BANK, n_cols - n0)
        blocks = [(b, min(P, nn - b)) for b in range(0, nn, P)]

        def fill(pe, banks, nn=nn, blocks=blocks):
            for k0 in range(0, k_tiles, 4):
                kt = min(4, k_tiles - k0)
                w = k.take(pe, kt, nn)
                for i, (b, h) in enumerate(blocks):
                    for j in range(kt):
                        mm = k.nc.tensor.matmul(banks[i][0:h, 0:n_rhs], w[:, j, b:b + h], rhs(k0 + j),
                                                start=(k0 + j == 0), stop=(k0 + j == k_tiles - 1))
                yield mm
                k.used(k.tensor_done.n)

        empties = []
        for b, h in blocks:
            w = who or next(turn)
            empties.append((w, lambda bank, w=w, i=(n0 + b) // P, h=h: empty(w, i, h, bank[0:h, 0:n_rhs])))
        groups.append((fill, empties))
    return groups


def transpose_groups(k, jobs, who=None):
    groups = []
    turn = turns()
    for sources, empty in jobs:
        def fill(pe, banks, sources=sources):
            for i, src in enumerate(sources):
                r, w = src.shape
                mm = k.nc.tensor.transpose(banks[0][0:w, i * P:i * P + r], src, k.ident[0:r, 0:r])
            yield mm
        w = who or next(turn)
        wd = sources[0].shape[1]
        n = len(sources) * P
        groups.append((fill, [(w, lambda bank, w=w, wd=wd, n=n, empty=empty: empty(w, bank[0:wd, 0:n]))]))
    return groups


def vector_phase(k, steps):
    with k.nc.Block(no_gpsimd_drain=True) as block:
        @block.vector
        def _(dve):
            for ins in steps(k.nc.vector):
                chain(dve, k.dve_step, ins)

        @block.sync
        def _(sp):
            k.pump(sp)


def load_phase(k, loads):
    with k.nc.Block(no_gpsimd_drain=True) as block:
        @block.scalar
        def _(act):
            for out, src in loads:
                k.load_done.mark(act.dma_start(out, src), 16)
            act.wait_ge(k.load_done.sem, k.load_done.n)

        @block.sync
        def _(sp):
            k.pump(sp)


def inv_rms(k, xs, width, eps, rs, junk):
    nc, n = k.nc, len(xs)
    with nc.Block(no_gpsimd_drain=True) as block:
        @block.scalar
        def _(act):
            for i, x in enumerate(xs):
                chain(act, k.act_step, nc.scalar.activation(junk, x, ACT.Square, accum_out=rs[:, i:i + 1]))
            sums = k.act_step.n
            k.marks = {"sums": sums}
            act.wait_ge(k.dve_step.sem, k.dve_step.n + 1)
            chain(act, k.act_step, nc.scalar.activation(rs[:, 0:n], rs[:, 0:n], ACT.Sqrt))
            k.marks["root"] = k.act_step.n

        @block.vector
        def _(dve):
            dve.wait_ge(k.act_step.sem, k.marks["sums"])
            k.dve_step.mark(nc.vector.tensor_scalar(rs[:, 0:n], rs[:, 0:n], 1.0 / width, eps, ALU.mult, ALU.add))
            dve.wait_ge(k.act_step.sem, k.marks["root"])
            chain(dve, k.dve_step, nc.vector.reciprocal(rs[:, 0:n], rs[:, 0:n]))

        @block.sync
        def _(sp):
            k.pump(sp)


def norm_to_columns(k, tag, xs, width, eps, out, scale_bias):
    nc = k.nc
    with ExitStack() as tmp:
        n = len(xs)
        rs = k.sb(f"rs_{tag}", [P, n], where=tmp)
        xn = k.sb(f"xn_{tag}", [P, n, width], where=tmp)
        inv_rms(k, xs, width, eps, rs, xn[:, 0, :])
        with nc.Block(no_gpsimd_drain=True) as block:
            @block.scalar
            def _(act):
                for i in range(0, n, 2):
                    k.act_step.mark(nc.scalar.mul(xn[:, i, :], xs[i], rs[:, i:i + 1]))
                act.wait_ge(k.act_step.sem, k.act_step.n)

            @block.vector
            def _(dve):
                for i in range(1, n, 2):
                    k.dve_step.mark(nc.vector.tensor_scalar(xn[:, i, :], xs[i], rs[:, i:i + 1], None, ALU.mult))
                if n > 1:
                    dve.wait_ge(k.dve_step.sem, k.dve_step.n)

            @block.sync
            def _(sp):
                k.pump(sp)

        jobs = []
        for kt in range(width // P):
            def empty(who, bank, kt=kt):
                for t0, tn, sc, bi in scale_bias(kt):
                    o, i = out[:, kt, t0:t0 + tn], bank[:, t0:t0 + tn]
                    if who == "act":
                        ins = nc.scalar.activation(o, i, ACT.Identity, scale=sc, bias=0.0 if bi is None else bi)
                    elif bi is None:
                        ins = nc.vector.tensor_scalar(o, i, sc, None, ALU.mult)
                    else:
                        ins = nc.vector.tensor_scalar(o, i, sc, bi, ALU.mult, ALU.add)
                return ins
            jobs.append(([xn[:, i, kt * P:(kt + 1) * P] for i in range(n)], empty))
        banks_phase(k, transpose_groups(k, jobs))


def attention(k, tag, units, scale, width, dv):
    nc = k.nc
    n = len(units)
    with ExitStack() as tmp:
        masked = k.sb(f"sc_{tag}", [P, 2, width], where=tmp)
        probs = k.sb(f"pr_{tag}", [P, 2, width], where=tmp)
        probs_t = k.sb(f"pt_{tag}", [P, 2, width], where=tmp)
        stat = k.sb(f"st_{tag}", [P, 2, 8], where=tmp)
        scores_ready, max_ready, probs_ready = k.scores_ready, k.max_ready, k.probs_ready
        turned, turned_copied, mixed, out_done = k.turned, k.turned_copied, k.mixed, k.out_done

        def widths(u):
            return sum(kk.shape[-1] for _, kk in u["qk"])

        def s_view(i, w):
            return k.psum[:, 2 * (i % 2):2 * (i % 2) + 2, :].rearrange("p b n -> p (b n)")[:, 0:w]

        def t_view(w):
            return k.psum[:, 4:6, :].rearrange("p b n -> p (b n)")[:, 0:w]

        with nc.Block(no_gpsimd_drain=True) as block:
            @block.tensor
            def _(pe):
                def scores(i):
                    if i >= 2:
                        pe.wait_ge(*probs_ready.at(i - 1))
                    c = 0
                    for q, kk in units[i]["qk"]:
                        w = kk.shape[-1]
                        mm = nc.tensor.matmul(s_view(i, c + w)[:, c:c + w], q, kk, start=(c % BANK == 0), stop=True,
                                              skip_group_check=True)
                        c += w
                    mm.then_inc(scores_ready.sem, 1)

                for i in range(min(2, n)):
                    scores(i)
                for i in range(n):
                    w = widths(units[i])
                    pe.wait_ge(*probs_ready.at(i + 1))
                    if i >= 1:
                        pe.wait_ge(*turned_copied.at(i))
                    for j in range(w // P):
                        mm = nc.tensor.transpose(t_view(w)[:, j * P:(j + 1) * P], probs[:, i % 2, j * P:(j + 1) * P],
                                                 k.ident[:])
                    mm.then_inc(turned.sem, 1)
                    if i + 2 < n:
                        scores(i + 2)
                    pe.wait_ge(*turned_copied.at(i + 1))
                    if i >= 2:
                        pe.wait_ge(*out_done.at(i - 1))
                    for j in range(w // P):
                        mm = nc.tensor.matmul(k.psum[:, 6 + i % 2, 0:dv], probs_t[:, i % 2, j * P:(j + 1) * P],
                                              units[i]["v"][j], start=(j == 0), stop=(j == w // P - 1))
                    mm.then_inc(mixed.sem, 1)

            @block.vector
            def _(dve):
                def finish(i):
                    u, st, w = units[i], stat[:, i % 2, :], widths(units[i])
                    dve.wait_ge(*probs_ready.at(i + 1))
                    if u["sink"] is not None:
                        chain(dve, k.dve_step, nc.vector.tensor_tensor(st[:, 3:4], st[:, 3:4], st[:, 4:5], ALU.add))
                    k.dve_step.mark(nc.vector.reciprocal(st[:, 5:6], st[:, 3:4]))
                    if u["mask"] is None:
                        dve.wait_ge(*turned.at(i + 1))
                        nc.vector.tensor_copy(probs_t[:, i % 2, 0:w], t_view(w)).then_inc(turned_copied.sem, 1)
                    dve.wait_ge(k.dve_step.sem, k.dve_step.n)
                    dve.wait_ge(*mixed.at(i + 1))
                    nc.vector.tensor_scalar(u["out"], k.psum[:, 6 + i % 2, 0:dv], st[:, 5:6], None,
                                            ALU.mult).then_inc(out_done.sem, 1)

                for i in range(n):
                    u, st, w = units[i], stat[:, i % 2, :], widths(units[i])
                    dve.wait_ge(*scores_ready.at(i + 1))
                    src, sc = s_view(i, w), scale
                    if u["mask"] is not None:
                        chain(dve, k.dve_step, nc.vector.scalar_tensor_tensor(
                            out=masked[:, i % 2, 0:w], in0=s_view(i, w), scalar=scale, in1=u["mask"],
                            op0=ALU.mult, op1=ALU.add))
                        src, sc = masked[:, i % 2, 0:w], 1.0
                    chain(dve, k.dve_step, nc.vector.reduce_max(st[:, 0:1], src, AX.X))
                    if u["sink"] is not None:
                        chain(dve, k.dve_step, nc.vector.tensor_scalar(st[:, 1:2], st[:, 0:1], sc, u["sink"],
                                                                       ALU.mult, ALU.max))
                        sc = 1.0
                    else:
                        chain(dve, k.dve_step, nc.vector.tensor_copy(st[:, 1:2], st[:, 0:1]))
                    nc.vector.tensor_scalar(st[:, 2:3], st[:, 1:2], -sc, None, ALU.mult).then_inc(max_ready.sem, 1)
                    if i >= 1:
                        finish(i - 1)
                finish(n - 1)
                dve.wait_ge(*out_done.at(n))

            @block.scalar
            def _(act):
                def turn_copy(i):
                    w = widths(units[i])
                    act.wait_ge(*turned.at(i + 1))
                    nc.scalar.copy(probs_t[:, i % 2, 0:w], t_view(w)).then_inc(turned_copied.sem, 1)

                for i in range(n):
                    u, st, w = units[i], stat[:, i % 2, :], widths(units[i])
                    act.wait_ge(*max_ready.at(i + 1))
                    if i >= 2:
                        act.wait_ge(*out_done.at(i - 1))
                    if u["sink"] is not None:
                        nc.scalar.activation(st[:, 4:5], u["sink"], ACT.Exp, bias=st[:, 2:3])
                    src, sc = (s_view(i, w), scale) if u["mask"] is None else (masked[:, i % 2, 0:w], 1.0)
                    nc.scalar.activation(probs[:, i % 2, 0:w], src, ACT.Exp, scale=sc, bias=st[:, 2:3],
                                         accum_out=st[:, 3:4]).then_inc(probs_ready.sem, 1)
                    if u["mask"] is not None and i >= 1:
                        turn_copy(i - 1)
                if units[n - 1]["mask"] is not None:
                    turn_copy(n - 1)

            @block.sync
            def _(sp):
                k.pump(sp)
        for signal in (scores_ready, max_ready, probs_ready, turned, turned_copied, mixed, out_done):
            signal.base += n


def rope_steps(v, x, out, t1, cos2, sin2, heads, hd):
    h2 = hd // 2
    c = cos2.unsqueeze(1).to_broadcast([P, heads, hd])
    s_lo = sin2[:, 0:h2].unsqueeze(1).to_broadcast([P, heads, h2])
    s_hi = sin2[:, h2:hd].unsqueeze(1).to_broadcast([P, heads, h2])
    yield v.tensor_tensor(t1[:, :, 0:h2], x[:, :, h2:hd], s_lo, ALU.mult)
    yield v.tensor_tensor(t1[:, :, h2:hd], x[:, :, 0:h2], s_hi, ALU.mult)
    yield v.tensor_tensor(out, x, c, ALU.mult)
    yield v.tensor_tensor(out, out, t1, ALU.add)


class Stop(Exception):
    pass


def shape_constants():
    f = np.float32
    tok = np.arange(S)
    row, col = (tok // 64).astype(f), (tok % 64).astype(f)

    def rope_table(dim):
        nf = dim // 4
        inv = (f(10000.0) ** (-np.arange(nf, dtype=f) / f(nf))).astype(f)
        ang = np.concatenate([row[:, None] * inv, col[:, None] * inv], axis=-1)
        c, s = np.cos(ang), np.sin(ang)
        return np.stack([np.concatenate([c, c], -1), np.concatenate([-s, s], -1)], 1).astype(f)

    q, kk = tok[:, None], tok[None, :]
    swa = np.where(np.abs(q - kk) <= 128, 0.0, NEG)
    swa = np.concatenate([swa, np.zeros((S, S))], 1).astype(f)
    dil = np.concatenate([np.where((q >= kk) & ((q - kk) % d == 0) & (q - kk <= 128 * d), 0.0, NEG)
                          for d in (1, 4, 16)], 1).astype(f)
    i16 = np.arange(P) % 16
    lag = (i16[:, None, None] - np.arange(16)[None, :, None] == np.arange(16)[None, None, :]).astype(f)
    sel = np.zeros((2, 2, P), f)
    sel[0, 0], sel[1, 1] = 1.0, 1.0
    inv = (f(10000.0) ** (-np.arange(0, P, 2, dtype=f) / f(P))).astype(f)
    head = np.zeros((P, 2), f)
    head[:64, 0], head[64:, 1] = 1.0, 1.0
    return {
        "ident": np.eye(P, dtype=f), "rope64": rope_table(64), "rope32": rope_table(32), "swa_mask": swa,
        "dil_mask": dil, "row_pick": sel, "inv_freq": np.tile(inv, (P, 1)),
        "lag_is": lag, "chunk_is": (np.arange(P)[:, None] // 16 == np.arange(8)[None, :]).astype(f),
        "head_is": head, "within_chunk": np.tile((tok % 16 != 0).astype(f), (P, 1)),
        "descending": np.tile(np.arange(32, 0, -1, dtype=f), (P, 1)),
    }


def two_blocks(nc, t, out):
    try:
        with ExitStack() as ctx:
            program(Core(nc, ctx), t, out)
    except (Stop, AssertionError):
        if STOP is None:
            raise


def stop_at(name):
    if STOP == name:
        raise Stop()


def program(k, t, out):
    nc = k.nc
    sb = k.sb
    E = (range(32))

    for l in range(2):
        k.plan(t["ada_w"][l], D, 6 * D)
        if l == 0:
            k.plan(t["ab_w_in"][0], D, 1184)
            k.plan(t["mla_w_uq"][0], 256, 768)
            k.plan(t["mla_w_ukv"][0], 128, 1024)
            k.plan(t["ab_w_out"][0], D, D)
        else:
            k.plan(t["diff_w_in"][0], D, 3072)
            k.plan(t["diff_w_out"][0], D, D)
        for e in E:
            k.plan(t["expert_w1"][l, e], D, 512)
            k.plan(t["expert_w3"][l, e], D, 512)
            k.plan(t["expert_w2"][l, e], 512, D)
    w_in = t["w_in_2"][0]
    for first, cols in ((0, 512), (512, 512), (1024, 528), (1552, 1536), (3088, 4608)):
        k.plan(w_in, D, cols, first)
    k.plan(t["w_gate_2"][0], D, 3 * D)
    for g in range(3):
        k.plan(t["w_branch_2"][0, g], 512, D)
    k.plan(t["w_mix_out_2"][0], D, D)
    k.plan(t["w_ff_gate_2"][0], D, 2816)
    k.plan(t["w_ff_up_2"][0], D, 2816)
    k.plan(t["w_ff_down_2"][0], 2816, D)

    k.ident = sb("ident", [P, P])
    x = sb("x", [P, T_ALL, D])
    h_t = sb("h_t", [P, DK, 2 * S])
    cols = sb("cols", [P, 3 * P])
    rope64 = sb("rope64", [P, T_LAT, 2, 64])
    rope32 = sb("rope32", [P, T_LAT, 2, 32])
    row_pick = sb("row_pick", [2, 2, P])
    descending = sb("descending", [P, 32])
    x_dram = t["x"][0].rearrange("(t p) d -> p t d", p=P)
    ctx_dram = t["ctx"][0].rearrange("(t p) d -> p t d", p=P)
    vec = lambda a: a.rearrange("(r c) -> r c", c=P)
    packs = [[("c", t["c"][0]), ("c_ctx", t["c_ctx"]), ("mix0", t["norm_mix"][0]), ("mix1", t["norm_mix"][1]),
              ("ffn0", t["norm_ffn"][0]), ("ffn1", t["norm_ffn"][1]), ("pre_mix", t["pre_mix_g_2"][0]),
              ("pre_ffn", t["pre_ffn_g_2"][0]), ("b_gate", t["b_gate_2"][0])],
             [("ffw0", t["ff_conv_w_2"][0, 0]), ("ffw1", t["ff_conv_w_2"][0, 1]), ("ffw2", t["ff_conv_w_2"][0, 2]),
              ("ff_b", t["ff_conv_b_2"][0]), ("scw0", t["sc_conv_w_2"][0, 0]), ("scw1", t["sc_conv_w_2"][0, 1]),
              ("scw2", t["sc_conv_w_2"][0, 2]), ("b_alpha", t["b_alpha_2"][0]), ("q_norm", t["mla_q_norm"][0]),
              ("kv_norm", t["mla_kv_norm"][0]), ("gla_g", t["gla_norm_g_2"][0])]]
    where = {}
    with ExitStack() as tmp:
        pk = [sb(f"pack{i}", [P, P], where=tmp) for i in range(2)]
        with nc.Block(no_gpsimd_drain=True) as block:
            @block.gpsimd
            def _(pool):
                for p in pk:
                    chain(pool, k.pool_step, nc.gpsimd.memset(p[:], 0.0))
        loads = [(k.ident[:], t["ident"]), (x[:, 0:T_LAT, :], x_dram), (x[:, T_LAT:T_ALL, :], ctx_dram),
                 (rope64[:], t["rope64"].rearrange("(t p) a b -> p t a b", p=P)),
                 (rope32[:], t["rope32"].rearrange("(t p) a b -> p t a b", p=P)),
                 (row_pick[:], t["row_pick"]), (descending[:], t["descending"])]
        for i, pack in enumerate(packs):
            r = 0
            for name, a in pack:
                n = a.shape[0] // P
                loads.append((pk[i][r:r + n, :], vec(a)))
                where[name] = i * P + r
                r += n
        load_phase(k, loads)
        banks_phase(k, transpose_groups(k, [([p[:] for p in pk],
                                             lambda who, bank: copy_by(k, who, cols[:, 0:2 * P], bank))]))
    col = lambda name, i=0, n=1: cols[:, where[name] + i:where[name] + i + n]
    stop_at("setup")

    mod_cols = sb("mod_cols", [P, 4, DK, 2])
    mod_a = sb("mod_a", [P, 2, 2, DK])
    first = ctx_first = ExitStack()
    with first:
        gates = sb("gates", [P, 2, 2, D], where=first)
        for l in range(2):
            modulations(k, t, l, col, row_pick, mod_cols, mod_a, gates)
            stop_at(f"ada{l}")
            tiles = list(range(T_ALL))

            def shift_scale(which, n_ctx):
                def f(kt):
                    r = [(0, S, mod_a[:, which, 0, kt:kt + 1], mod_cols[:, 2 * which, kt, 0:1])]
                    if n_ctx:
                        r.append((S, S, mod_a[:, which, 1, kt:kt + 1], mod_cols[:, 2 * which, kt, 1:2]))
                    return r
                return f
            norm_to_columns(k, f"mix{l}", [x[:, i, :] for i in tiles], D, 1e-6, h_t, shift_scale(0, True))
            stop_at(f"norm{l}")
            if l == 0:
                swa_mla(k, t, x, h_t, gates, col, rope64, rope32)
            else:
                differential(k, t, x, h_t, gates, rope64)
            stop_at(f"mixer{l}")
            tiles = list(range(T_ALL if l == 0 else T_LAT))
            norm_to_columns(k, f"ffn{l}", [x[:, i, :] for i in tiles], D, 1e-6, h_t, shift_scale(1, l == 0))
            stop_at(f"normf{l}")
            experts(k, t, l, x, h_t, gates, len(tiles), descending)
            stop_at(f"moe{l}")
    row_norm(k, t, x)
    stop_at("block1")
    second_block(k, t, x, h_t, col, out)


def row_norm(k, t, x):
    nc = k.nc
    with ExitStack() as tmp:
        g = k.sb("final_g", [P, D], where=tmp)
        rs = k.sb("rs_final", [P, T_LAT], where=tmp)
        junk = k.sb("junk_final", [P, D], where=tmp)
        load_phase(k, [(g[:], t["final_norm"].partition_broadcast(P))])
        inv_rms(k, [x[:, i, :] for i in range(T_LAT)], D, 1e-6, rs, junk[:])

        def steps(v):
            for i in range(T_LAT):
                yield v.scalar_tensor_tensor(out=x[:, i, :], in0=x[:, i, :], scalar=rs[:, i:i + 1], in1=g[:],
                                             op0=ALU.mult, op1=ALU.mult)
        vector_phase(k, steps)


def modulations(k, t, l, col, row_pick, mod_cols, mod_a, gates):
    nc, sb = k.nc, k.sb
    with ExitStack() as tmp:
        sc = sb(f"silu_c{l}", [P, DK, 2], where=tmp)
        rows = sb(f"mod_rows{l}", [2, 6 * D], where=tmp)
        bias = sb(f"mod_bias{l}", [2, 6 * D], where=tmp)
        with nc.Block(no_gpsimd_drain=True) as block:
            @block.scalar
            def _(act):
                for r in range(2):
                    k.load_done.mark(act.dma_start(bias[r:r + 1, :], t["ada_b"][l:l + 1, :]), 16)
                for i, name in enumerate(("c", "c_ctx")):
                    chain(act, k.act_step, nc.scalar.activation(sc[:, :, i], col(name, 0, DK), ACT.Silu))
                act.wait_ge(k.load_done.sem, k.load_done.n)

            @block.sync
            def _(sp):
                k.pump(sp)

        def add_bias(who, r, n0, nn, bank):
            return nc.vector.tensor_tensor(rows[:, n0:n0 + nn], bank, bias[:, n0:n0 + nn], ALU.add)
        banks_phase(k, project_groups(k, lambda kt, r: sc[:, kt, :], DK, [2], 6 * D, add_bias, "dve"))

        def fill_columns(pe, banks):
            for i, kind in enumerate((0, 1, 3, 4)):
                for kt in range(DK):
                    c = 2 * (i * DK + kt)
                    mm = nc.tensor.transpose(banks[0][:, c:c + 2], rows[:, kind * D + kt * P:kind * D + (kt + 1) * P],
                                             k.ident[0:2, 0:2])
            yield mm

        groups = [(fill_columns, [("act", lambda bank: nc.scalar.copy(
            mod_cols[:].rearrange("p a b c -> p (a b c)"), bank[:, 0:8 * DK]))])]
        for s in range(2):
            for g, kind in enumerate((2, 5)):
                for half in range(2):
                    def spread(pe, banks, s=s, at=kind * D + half * BANK):
                        yield nc.tensor.matmul(banks[0], row_pick[:, s, :], rows[:, at:at + BANK], start=True, stop=True)
                    who = ("act", "dve")[half]
                    groups.append((spread, [(who, lambda bank, who=who, s=s, g=g, half=half: copy_by(
                        k, who, gates[:, s, g, half * BANK:(half + 1) * BANK], bank))]))
        banks_phase(k, groups)

        def gains(v):
            for which in range(2):
                for s in range(2):
                    yield v.scalar_tensor_tensor(out=mod_a[:, which, s, :], in0=mod_cols[:, 2 * which + 1, :, s],
                                                 scalar=1.0, in1=col(("mix", "ffn")[which] + str(l), 0, DK),
                                                 op0=ALU.add, op1=ALU.mult)
        vector_phase(k, gains)


def gated_residual(k, tag, o, x, gates, which, h_t, n_tiles):
    nc = k.nc
    jobs = [([o[:, i, kt * P:(kt + 1) * P] for i in range(n_tiles)],
             lambda who, bank, kt=kt: copy_by(k, who, h_t[:, kt, 0:n_tiles * P], bank)) for kt in range(DK)]
    banks_phase(k, transpose_groups(k, jobs))
    with ExitStack() as tmp:
        part = k.sb(f"gated_{tag}", [P, BANK], where=tmp)

        def add(who, r, n0, nn, bank):
            g = gates[:, 0 if r < T_LAT else 1, which, n0:n0 + nn]
            nc.vector.wait_ge(k.dve_evac.sem, k.dve_evac.n)
            chain(nc.vector, k.dve_step, nc.vector.tensor_tensor(part[:, 0:nn], bank, g, ALU.mult))
            return nc.vector.tensor_tensor(x[:, r, n0:n0 + nn], x[:, r, n0:n0 + nn], part[:, 0:nn], ALU.add)
        banks_phase(k, project_groups(k, lambda kt, r: h_t[:, kt, r * P:(r + 1) * P], DK, [P] * n_tiles, D, add,
                                      "dve"))


def swa_mla(k, t, x, h_t, gates, col, rope64, rope32):
    nc, sb = k.nc, k.sb
    with ExitStack() as mix:
        o = sb("ab_o", [P, T_ALL, D], where=mix)
        proj = sb("ab_proj", [P, T_ALL, 1184], where=mix)
        banks_phase(k, project_groups(
            k, lambda kt, r: h_t[:, kt, r * P:(r + 1) * P], DK, [P] * T_ALL, 1184,
            lambda who, r, n0, nn, bank: copy_by(k, who, proj[:, r, n0:n0 + nn], bank)))
        with ExitStack() as tmp:
            t1 = sb("rope_t1", [P, 640], where=tmp)
            qk_r = sb("rope_qk", [P, 640], where=tmp)
            kr_r = sb("rope_kr", [P, 32], where=tmp)

            def steps(v):
                for i in range(T_LAT):
                    xx = proj[:, i, 0:640].rearrange("p (h d) -> p h d", d=64)
                    oo = qk_r[:].rearrange("p (h d) -> p h d", d=64)
                    yield from rope_steps(v, xx, oo, t1[:].rearrange("p (h d) -> p h d", d=64),
                                          rope64[:, i, 0, :], rope64[:, i, 1, :], 10, 64)
                    yield v.tensor_copy(proj[:, i, 0:640], qk_r[:])
                    xx = proj[:, i, 1152:1184].rearrange("p (h d) -> p h d", d=32)
                    oo = kr_r[:].rearrange("p (h d) -> p h d", d=32)
                    yield from rope_steps(v, xx, oo, t1[:, 0:32].rearrange("p (h d) -> p h d", d=32),
                                          rope32[:, i, 0, :], rope32[:, i, 1, :], 1, 32)
                    yield v.tensor_copy(proj[:, i, 1152:1184], kr_r[:])
            vector_phase(k, steps)
        with ExitStack() as tmp:
            q_t = sb("swa_q_t", [P, 4, 2 * S], where=tmp)
            k_t = sb("swa_k_t", [P, 2 * S], where=tmp)
            mask = sb("swa_mask", [P, T_LAT, 2 * S], where=tmp)
            sink = sb("sink", [P, 8], where=tmp)
            pair = sb("swa_pair", [P, T_ALL, 4, 2, 64], where=tmp)
            load_phase(k, [(mask[:], t["swa_mask"].rearrange("(t p) k -> p t k", p=P)),
                           (sink[:], t["swa_sink"][0].partition_broadcast(P))])

            def steps(v):
                for i in range(T_ALL):
                    yield v.tensor_copy(pair[:, i], proj[:, i, 0:512].rearrange("p (a b d) -> p b a d", a=2, d=64))
            vector_phase(k, steps)
            jobs = [([pair[:, i, b].rearrange("p a d -> p (a d)") for i in range(T_ALL)],
                     lambda who, bank, b=b: copy_by(k, who, q_t[:, b, :], bank)) for b in range(4)]
            jobs.append(([proj[:, i, 512:640] for i in range(T_ALL)],
                         lambda who, bank: copy_by(k, who, k_t[:], bank)))
            banks_phase(k, transpose_groups(k, jobs))
            units = {0: [], 1: []}
            for i in range(T_ALL):
                lat = i < T_LAT
                k0 = 0 if lat else S
                for h in range(8):
                    a, b = divmod(h, 4)
                    rows = slice(64 * a, 64 * a + 64)
                    units[0 if lat else 1].append(dict(
                        qk=[(q_t[rows, b, i * P:(i + 1) * P], k_t[rows, k0:2 * S])],
                        v=[proj[:, j, 640 + 64 * a:704 + 64 * a] for j in range(k0 // P, T_ALL)],
                        mask=mask[:, i, :] if lat else None, sink=sink[:, h:h + 1], out=o[:, i, 64 * h:64 * h + 64]))
            attention(k, "swa", units[0], 64 ** -0.5, 2 * S, 64)
            attention(k, "swac", units[1], 64 ** -0.5, S, 64)
        stop_at("swa")
        with ExitStack() as tmp:
            q_t = h_t[0:96, :, :]
            k_t = sb("mla_k_t", [96, 8, 2 * S], where=tmp)
            kv = sb("mla_kv", [P, T_ALL, 1024], where=tmp)
            with ExitStack() as tq:
                cq_t = sb("cq_t", [P, 2, 2 * S], where=tq)
                q = sb("mla_q", [P, T_ALL, 768], where=tq)
                norm_to_columns(k, "cq", [proj[:, i, 768:1024] for i in range(T_ALL)], 256, 1e-6, cq_t,
                                lambda kt: [(0, 2 * S, col("q_norm", kt), None)])
                banks_phase(k, project_groups(
                    k, lambda kt, r: cq_t[:, kt, r * P:(r + 1) * P], 2, [P] * T_ALL, 768,
                    lambda who, r, n0, nn, bank: copy_by(k, who, q[:, r, n0:n0 + nn], bank)))
                with ExitStack() as tr:
                    t1 = sb("mla_t1", [P, 8, 32], where=tr)
                    qr = sb("mla_qr", [P, 8, 32], where=tr)

                    def steps(v):
                        for i in range(T_LAT):
                            xx = q[:, i, :].rearrange("p (h d) -> p h d", d=96)[:, :, 64:96]
                            yield from rope_steps(v, xx, qr[:], t1[:], rope32[:, i, 0, :], rope32[:, i, 1, :], 8, 32)
                            yield v.tensor_copy(xx, qr[:])
                    vector_phase(k, steps)
                jobs = [([q[:, i, 96 * h:96 * h + 96] for i in range(T_ALL)],
                         lambda who, bank, h=h: copy_by(k, who, q_t[:, h, :], bank)) for h in range(8)]
                banks_phase(k, transpose_groups(k, jobs))
            with ExitStack() as tk:
                ckv_t = sb("ckv_t", [P, 1, 2 * S], where=tk)
                kcat = sb("mla_kcat", [P, T_ALL, 8, 96], where=tk)
                norm_to_columns(k, "ckv", [proj[:, i, 1024:1152] for i in range(T_ALL)], 128, 1e-6, ckv_t,
                                lambda kt: [(0, 2 * S, col("kv_norm"), None)])
                banks_phase(k, project_groups(
                    k, lambda kt, r: ckv_t[:, kt, r * P:(r + 1) * P], 1, [P] * T_ALL, 1024,
                    lambda who, r, n0, nn, bank: copy_by(k, who, kv[:, r, n0:n0 + nn], bank)))

                def steps(v):
                    for i in range(T_ALL):
                        yield v.tensor_copy(kcat[:, i, :, 0:64],
                                            kv[:, i, :].rearrange("p (h d) -> p h d", d=128)[:, :, 0:64])
                        yield v.tensor_copy(kcat[:, i, :, 64:96],
                                            proj[:, i, 1152:1184].unsqueeze(1).to_broadcast([P, 8, 32]))
                vector_phase(k, steps)
                jobs = [([kcat[:, i, h, :] for i in range(T_ALL)],
                         lambda who, bank, h=h: copy_by(k, who, k_t[:, h, :], bank)) for h in range(8)]
                banks_phase(k, transpose_groups(k, jobs))
            units = {0: [], 1: []}
            for i in range(T_ALL):
                k0 = 0 if i < T_LAT else S
                for h in range(8):
                    units[min(1, k0)].append(dict(
                        qk=[(q_t[:, h, i * P:(i + 1) * P], k_t[:, h, k0:2 * S])],
                        v=[kv[:, j, 128 * h + 64:128 * h + 128] for j in range(k0 // P, T_ALL)],
                        mask=None, sink=None, out=o[:, i, 512 + 64 * h:576 + 64 * h]))
            attention(k, "mla", units[0], 96 ** -0.5, 2 * S, 64)
            attention(k, "mlac", units[1], 96 ** -0.5, S, 64)
        gated_residual(k, "ab", o, x, gates, 0, h_t, T_ALL)


def differential(k, t, x, h_t, gates, rope64):
    nc, sb = k.nc, k.sb
    lambda_init = 0.8 - 0.6 * math.exp(-0.3)
    with ExitStack() as mix:
        a1 = sb("diff_a1", [P, T_LAT, D], where=mix)
        a2 = sb("diff_a2", [P, T_LAT, D], where=mix)
        k_t = sb("diff_k_t", [P, 8, 2 * S], where=mix)
        q_t = sb("diff_q_t", [P, 8, S], where=mix)
        small = sb("diff_small", [P, 8], where=mix)
        vt = sb("diff_v", [P, T_ALL, D], where=mix)

        def roped_to_columns(tag, n_tiles, dst):
            with ExitStack() as tmp:
                z = sb(f"diff_{tag}", [P, n_tiles, D], where=tmp)
                t1 = sb(f"diff_t1{tag}", [P, D], where=tmp)
                zr = sb(f"diff_zr{tag}", [P, D], where=tmp)
                heads = lambda a: a.rearrange("p (h d) -> p h d", d=64)
                banks_phase(k, project_groups(
                    k, lambda kt, r: h_t[:, kt, r * P:(r + 1) * P], DK, [P] * n_tiles, D,
                    lambda who, r, n0, nn, bank: copy_by(k, who, z[:, r, n0:n0 + nn], bank)))

                def steps(v):
                    for i in range(T_LAT):
                        yield from rope_steps(v, heads(z[:, i, :]), heads(zr[:]), heads(t1[:]), rope64[:, i, 0, :],
                                              rope64[:, i, 1, :], 16, 64)
                        yield v.tensor_copy(z[:, i, :], zr[:])
                vector_phase(k, steps)
                jobs = [([z[:, i, j * P:(j + 1) * P] for i in range(n_tiles)],
                         lambda who, bank, j=j: copy_by(k, who, dst[:, j, :], bank)) for j in range(8)]
                banks_phase(k, transpose_groups(k, jobs))
        roped_to_columns("q", T_LAT, q_t)
        roped_to_columns("k", T_ALL, k_t)
        banks_phase(k, project_groups(
            k, lambda kt, r: h_t[:, kt, r * P:(r + 1) * P], DK, [P] * T_ALL, D,
            lambda who, r, n0, nn, bank: copy_by(k, who, vt[:, r, n0:n0 + nn], bank)))
        units = []
        for i in range(T_LAT):
            for j in range(8):
                for a, dst in enumerate((a1, a2)):
                    rows = slice(64 * a, 64 * a + 64)
                    units.append(dict(qk=[(q_t[rows, j, i * P:(i + 1) * P], k_t[rows, j, :])],
                                      v=[vt[:, m, j * P:(j + 1) * P] for m in range(T_ALL)],
                                      mask=None, sink=None, out=dst[:, i, j * P:(j + 1) * P]))
        attention(k, "diff", units, 64 ** -0.5, 2 * S, P)
        with ExitStack() as tmp:
            lqk = sb("lqk", [P, 4, 64], where=tmp)
            prod = sb("lqk_prod", [P, 64], where=tmp)
            subln = sb("subln", [P, P], where=tmp)
            ms = sb("diff_ms", [P, T_LAT * 8], where=tmp)
            load_phase(k, [(lqk[:, i, :], t["diff_lambda_" + n][0].partition_broadcast(P))
                           for i, n in enumerate(("q1", "k1", "q2", "k2"))]
                       + [(subln[:], t["diff_subln"][0].partition_broadcast(P))])

            def dots(v):
                for i in range(2):
                    yield v.tensor_tensor(prod[:], lqk[:, 2 * i, :], lqk[:, 2 * i + 1, :], ALU.mult)
                    yield v.reduce_sum(small[:, i:i + 1], prod[:], AX.X)
            vector_phase(k, dots)
            scalar_phase(k, lambda s: [s.activation(small[:, 2:4], small[:, 0:2], ACT.Exp)])
            whole = lambda a: a[:].rearrange("p t d -> p (t d)")
            per_head = lambda a: a[:].rearrange("p t (h d) -> p (t h) d", d=P)

            def combine(v):
                yield v.tensor_tensor(small[:, 4:5], small[:, 3:4], small[:, 2:3], ALU.subtract)
                yield v.tensor_scalar(small[:, 4:5], small[:, 4:5], -lambda_init, None, ALU.add)
                yield v.scalar_tensor_tensor(out=whole(a1), in0=whole(a2), scalar=small[:, 4:5], in1=whole(a1),
                                             op0=ALU.mult, op1=ALU.add)
                yield v.tensor_tensor(whole(a2), whole(a1), whole(a1), ALU.mult)
                yield v.tensor_reduce(ms[:], per_head(a2), AX.X, ALU.add)
                yield v.tensor_scalar(ms[:], ms[:], 1.0 / P, 1e-5, ALU.mult, ALU.add)
            vector_phase(k, combine)
            scalar_phase(k, lambda s: [s.activation(ms[:], ms[:], ACT.Sqrt)])

            def scaled(v):
                yield v.reciprocal(ms[:], ms[:])
                yield v.tensor_scalar(ms[:], ms[:], 1.0 - lambda_init, None, ALU.mult)
                yield v.tensor_tensor(per_head(a1), per_head(a1), ms[:].unsqueeze(2).to_broadcast([P, T_LAT * 8, P]),
                                      ALU.mult)
                yield v.tensor_tensor(per_head(a1), per_head(a1), subln[:].unsqueeze(1).to_broadcast([P, T_LAT * 8, P]),
                                      ALU.mult)
            vector_phase(k, scaled)
        gated_residual(k, "diff", a1, x, gates, 0, h_t, T_LAT)


def scalar_phase(k, steps):
    with k.nc.Block(no_gpsimd_drain=True) as block:
        @block.scalar
        def _(act):
            for ins in steps(k.nc.scalar):
                chain(act, k.act_step, ins)

        @block.sync
        def _(sp):
            k.pump(sp)


def route(k, t, l, h_t, n_tiles, descending, gate):
    nc, sb = k.nc, k.sb
    n = n_tiles
    with ExitStack() as tmp:
        wr = sb(f"router_w{l}", [P, DK, 36], where=tmp)
        br = sb(f"router_b{l}", [P, 36], where=tmp)
        lg = sb(f"logits{l}", [P, n, 36], where=tmp)
        one = sb(f"r_one{l}", [P, n, 4], where=tmp)
        w4 = sb(f"r_w4{l}", [P, n, 4], where=tmp)
        ex = sb(f"r_ex{l}", [P, n, 4], where=tmp)
        r1 = sb(f"r_r1{l}", [P, n, 8], where=tmp)
        em = sb(f"r_em{l}", [P, n, 32], where=tmp)
        pick = sb(f"r_pick{l}", [P, n, 2, 32], where=tmp)
        w32 = sb(f"r_w32{l}", [P, n, 32], where=tmp)
        load_phase(k, [(wr[:, :, 0:4], t["router_group_w"][l].rearrange("(j p) n -> p j n", p=P)),
                       (wr[:, :, 4:36], t["router_expert_w"][l].rearrange("(j p) n -> p j n", p=P)),
                       (br[:, 0:4], t["router_group_b"][l].partition_broadcast(P)),
                       (br[:, 4:36], t["router_expert_b"][l].partition_broadcast(P))])

        def fill(pe, banks):
            for i in range(n):
                for kt in range(DK):
                    mm = nc.tensor.matmul(banks[0][:, i * 36:(i + 1) * 36], h_t[:, kt, i * P:(i + 1) * P], wr[:, kt, :],
                                          start=(kt == 0), stop=(kt == DK - 1), skip_group_check=True)
            yield mm
        banks_phase(k, [(fill, [("dve", lambda bank: nc.vector.tensor_tensor(
            lg[:], bank[:, 0:n * 36].rearrange("p (i e) -> p i e", e=36), br[:].unsqueeze(1).to_broadcast([P, n, 36]),
            ALU.add))])])
        g, e = lg[:, :, 0:4], lg[:, :, 4:36]
        b4 = lambda a: a.to_broadcast([P, n, 4])
        b32 = lambda a: a.to_broadcast([P, n, 32])
        desc4, desc32 = descending[:, 28:32].unsqueeze(1), descending[:].unsqueeze(1)

        def first_max(v, out, vals, top, weight, desc, spread):
            yield v.tensor_reduce(top, vals, AX.X, ALU.max)
            yield v.tensor_tensor(weight, vals, spread(top), ALU.is_equal)
            yield v.tensor_tensor(weight, weight, spread(desc), ALU.mult)
            yield v.tensor_reduce(r1[:, :, 7:8], weight, AX.X, ALU.max)
            yield v.tensor_tensor(out, weight, spread(r1[:, :, 7:8]), ALU.is_equal)

        def choose(v):
            yield from first_max(v, one[:], g, r1[:, :, 0:1], w4[:], desc4, b4)
            yield v.tensor_tensor(ex[:], g, b4(r1[:, :, 0:1]), ALU.subtract)
            yield v.tensor_scalar(w4[:], one[:], -1.0, -NEG, ALU.add, ALU.mult)
            group = lambda a: a.unsqueeze(3).to_broadcast([P, n, 4, 8])
            em4 = em[:].rearrange("p i (g x) -> p i g x", g=4)
            for i in range(n):
                gi = lambda a: a[:, i, :].unsqueeze(2).to_broadcast([P, 4, 8])
                ei = em[:, i, :].rearrange("p (g x) -> p g x", g=4)
                yield v.tensor_tensor(ei, e[:, i, :].rearrange("p (g x) -> p g x", g=4), gi(one), ALU.mult)
                yield v.tensor_tensor(ei, ei, gi(w4), ALU.add)
            yield from first_max(v, pick[:, :, 0, :], em[:], r1[:, :, 1:2], w32[:], desc32, b32)
            yield v.scalar_tensor_tensor(out=em[:], in0=pick[:, :, 0, :], scalar=2 * NEG, in1=em[:], op0=ALU.mult,
                                         op1=ALU.add)
            yield from first_max(v, pick[:, :, 1, :], em[:], r1[:, :, 2:3], w32[:], desc32, b32)
            yield v.tensor_tensor(r1[:, :, 3:4], r1[:, :, 2:3], r1[:, :, 1:2], ALU.subtract)
        vector_phase(k, choose)
        scalar_phase(k, lambda s: [s.activation(ex[:], ex[:], ACT.Exp),
                                   s.activation(r1[:, :, 3:4], r1[:, :, 3:4], ACT.Exp)])

        def weigh(v):
            yield v.tensor_reduce(r1[:, :, 4:5], ex[:], AX.X, ALU.add)
            yield v.tensor_scalar(r1[:, :, 5:6], r1[:, :, 3:4], 1.0, None, ALU.add)
            yield v.tensor_tensor(r1[:, :, 4:5], r1[:, :, 4:5], r1[:, :, 5:6], ALU.mult)
            yield v.reciprocal(r1[:, :, 4:5], r1[:, :, 4:5])
            yield v.tensor_tensor(r1[:, :, 5:6], r1[:, :, 4:5], r1[:, :, 3:4], ALU.mult)
            yield v.tensor_tensor(pick[:, :, 0, :], pick[:, :, 0, :], b32(r1[:, :, 4:5]), ALU.mult)
            yield v.tensor_tensor(pick[:, :, 1, :], pick[:, :, 1, :], b32(r1[:, :, 5:6]), ALU.mult)
            yield v.tensor_tensor(gate[:], pick[:, :, 0, :], pick[:, :, 1, :], ALU.add)
        vector_phase(k, weigh)


def experts(k, t, l, x, h_t, gates, n_tiles, descending):
    nc, sb = k.nc, k.sb
    n_tok = n_tiles * P
    with ExitStack() as moe:
        gate = sb(f"gate{l}", [P, n_tiles, 32], where=moe)
        route(k, t, l, h_t, n_tiles, descending, gate)
        stop_at(f"route{l}")
        y = sb(f"moe_y{l}", [P, n_tiles, D], where=moe)
        silu = sb(f"moe_silu{l}", [P, 4, n_tok], where=moe)
        hid = sb(f"moe_hid{l}", [P, 4, n_tok], where=moe)
        silu_at = {}
        groups = []
        for e in range(32):
            def gate_out(who, b, h, bank, e=e):
                silu_at[e] = k.act_evac.n + 1
                return nc.scalar.activation(silu[:, b, :], bank, ACT.Silu)

            def up_out(who, b, h, bank, e=e):
                if b == 0:
                    nc.vector.wait_ge(k.act_evac.sem, silu_at[e])
                return nc.vector.tensor_tensor(hid[:, b, :], silu[:, b, :], bank, ALU.mult)

            def y_out(who, r, n0, nn, bank, e=e):
                g = gate[:, r, e:e + 1]
                if e == 0:
                    return nc.vector.tensor_scalar(y[:, r, n0:n0 + nn], bank, g, None, ALU.mult)
                return nc.vector.scalar_tensor_tensor(out=y[:, r, n0:n0 + nn], in0=bank, scalar=g,
                                                      in1=y[:, r, n0:n0 + nn], op0=ALU.mult, op1=ALU.add)
            tok = lambda kt: h_t[:, kt, 0:n_tok]
            groups += project_column_groups(k, tok, DK, n_tok, 512, gate_out, "act")
            groups += project_column_groups(k, tok, DK, n_tok, 512, up_out, "dve")
            down = project_groups(k, lambda kt, r: hid[:, kt, r * P:(r + 1) * P], 4, [P] * n_tiles, D, y_out, "dve")
            groups += [(down[0][0], down[0][1], True)] + down[1:]
        banks_phase(k, groups)

        def add(v):
            for r in range(n_tiles):
                yield v.tensor_tensor(y[:, r, :], y[:, r, :], gates[:, 0 if r < T_LAT else 1, 1, :], ALU.mult)
                yield v.tensor_tensor(x[:, r, :], x[:, r, :], y[:, r, :], ALU.add)
        vector_phase(k, add)


def second_block(k, t, x, h_t, col, out):
    nc, sb = k.nc, k.sb
    with ExitStack() as mix:
        br_t = sb("branches_t", [P, 3, 4, S], where=mix)
        norm_to_columns(k, "pre_mix", [x[:, i, :] for i in range(T_LAT)], D, 1e-6, h_t,
                        lambda kt: [(0, S, col("pre_mix", kt), None)])
        gla_branch(k, t, h_t, col, br_t)
        stop_at("gla")
        conv_branch(k, t, h_t, col, br_t)
        stop_at("sc")
        dilated_branch(k, t, h_t, br_t)
        stop_at("dil")
        with ExitStack() as tmp:
            open_ = sb("branch_gates", [P, 24, S], where=tmp)
            merged = sb("merged_t", [P, DK, S], where=tmp)
            part = sb("merge_part", [P, S], where=tmp)
            tok = lambda kt: h_t[:, kt, 0:S]
            banks_phase(k, project_column_groups(
                k, tok, DK, S, 3 * D,
                lambda who, b, h, bank: nc.scalar.activation(open_[:, b, :], bank, ACT.Sigmoid, bias=col("b_gate", b)),
                "act"))
            groups = []
            for g in range(3):
                def merge(who, b, h, bank, g=g):
                    if g == 0:
                        return nc.vector.tensor_tensor(merged[:, b, :], bank, open_[:, b, :], ALU.mult)
                    nc.vector.wait_ge(k.dve_evac.sem, k.dve_evac.n)
                    chain(nc.vector, k.dve_step, nc.vector.tensor_tensor(part[:], bank, open_[:, 8 * g + b, :],
                                                                         ALU.mult))
                    return nc.vector.tensor_tensor(merged[:, b, :], merged[:, b, :], part[:], ALU.add)
                groups += project_column_groups(k, lambda kt, g=g: br_t[:, g, kt, :], 4, S, D, merge, "dve")
            banks_phase(k, groups)
            normed_residual(k, t, "post_mix_g_2", x, lambda kt, r: merged[:, kt, r * P:(r + 1) * P], DK)
    stop_at("mix2")
    with ExitStack() as ffn:
        hid = sb("ff_hid", [P, 22, S], where=ffn)
        norm_to_columns(k, "pre_ffn", [x[:, i, :] for i in range(T_LAT)], D, 1e-6, h_t,
                        lambda kt: [(0, S, col("pre_ffn", kt), None)])
        tok = lambda kt: h_t[:, kt, 0:S]

        def conv(who, b, h, bank):
            v, o = nc.vector, hid[:, b, :]
            chain(v, k.dve_step, v.tensor_scalar(o, bank, col("ffw2", b), col("ff_b", b), ALU.mult, ALU.add))
            chain(v, k.dve_step, v.scalar_tensor_tensor(out=o[:, 1:S], in0=bank[:, 0:S - 1], scalar=col("ffw1", b),
                                                        in1=o[:, 1:S], op0=ALU.mult, op1=ALU.add))
            return v.scalar_tensor_tensor(out=o[:, 2:S], in0=bank[:, 0:S - 2], scalar=col("ffw0", b), in1=o[:, 2:S],
                                          op0=ALU.mult, op1=ALU.add)
        banks_phase(k, project_column_groups(k, tok, DK, S, 2816, conv, "dve"))
        scalar_phase(k, lambda s: [s.activation(hid[:, b:b + 2, :], hid[:, b:b + 2, :], ACT.Gelu_apprx_tanh)
                                   for b in range(0, 22, 2)])
        banks_phase(k, project_column_groups(
            k, tok, DK, S, 2816, lambda who, b, h, bank: nc.vector.tensor_tensor(hid[:, b, :], hid[:, b, :], bank,
                                                                                 ALU.mult), "dve"))
        normed_residual(k, t, "post_ffn_g_2", x, lambda kt, r: hid[:, kt, r * P:(r + 1) * P], 22)
    with nc.Block(no_gpsimd_drain=True) as block:
        @block.sync
        def _(sp):
            k.store_done.mark(sp.dma_start(out[0].rearrange("(t p) d -> p t d", p=P), x[:, 0:T_LAT, :]), 16)
            sp.wait_ge(k.store_done.sem, k.store_done.n)


def normed_residual(k, t, gain, x, lhs, k_tiles):
    nc, sb = k.nc, k.sb
    with ExitStack() as tmp:
        y = sb(f"y_{gain}", [P, T_LAT, D], where=tmp)
        g = sb(f"g_{gain}", [P, D], where=tmp)
        rs = sb(f"rs_{gain}", [P, T_LAT], where=tmp)
        junk = sb(f"junk_{gain}", [P, D], where=tmp)
        load_phase(k, [(g[:], t[gain][0].partition_broadcast(P))])
        banks_phase(k, project_groups(k, lhs, k_tiles, [P] * T_LAT, D,
                                      lambda who, r, n0, nn, bank: copy_by(k, who, y[:, r, n0:n0 + nn], bank)))
        inv_rms(k, [y[:, i, :] for i in range(T_LAT)], D, 1e-6, rs, junk[:])

        def steps(v):
            for i in range(T_LAT):
                yield v.scalar_tensor_tensor(out=y[:, i, :], in0=y[:, i, :], scalar=rs[:, i:i + 1], in1=g[:],
                                             op0=ALU.mult, op1=ALU.mult)
                yield v.tensor_tensor(x[:, i, :], x[:, i, :], y[:, i, :], ALU.add)
        vector_phase(k, steps)


def columns_of(k, h_t, n_cols, dst):
    return project_column_groups(k, lambda kt: h_t[:, kt, 0:S], DK, S, n_cols,
                                 lambda who, b, h, bank: copy_by(k, who, dst(b, h), bank))


def gla_branch(k, t, h_t, col, br_t):
    nc, sb = k.nc, k.sb
    C, N = 16, S // 16
    with ExitStack() as gla:
        keep = lambda name, shape: sb("gla_" + name, shape, where=gla)
        qk = keep("qk", [P, 4, S])
        v_row = keep("v", [P, T_LAT, 512])
        g_t = keep("g", [P, 4, S])
        a_t = keep("a", [16, S])
        lc = keep("lc", [P, 2, S])
        lag_is = keep("lag_is", [P, 16, 16])
        chunk_is = keep("chunk_is", [P, 8])
        head_is = keep("head_is", [P, 2])
        dec = keep("dec", [P, 2, N])
        states = keep("states", [P, 2, N, P])
        q_in = keep("q_in", [P, 2, S])
        ones = keep("ones", [P, P])
        s_t = keep("s_t", [P, T_LAT, 4, P])
        four = lambda a: a.rearrange("p b (n c) -> p b n c", c=C)
        with ExitStack() as tmp:
            keep2 = lambda name, shape: sb("gla_" + name, shape, where=tmp)
            w_a = keep2("w_a", [16, S])
            z, u, r = keep2("z", [P, 2, S]), keep2("u", [P, 2, S]), keep2("r", [P, S])
            k_in = keep2("k_in", [P, 2, S])
            load_phase(k, [(w_a[:], t["w_alpha_up_2"][0]), (lag_is[:], t["lag_is"]), (chunk_is[:], t["chunk_is"]),
                           (head_is[:], t["head_is"]), (r[:], t["within_chunk"])])
            groups = columns_of(k, h_t, 512, lambda b, h: qk[:, b, :])
            groups += project_groups(k, lambda kt, i: h_t[:, kt, i * P:(i + 1) * P], DK, [P] * T_LAT, 512,
                                     lambda who, i, n0, nn, bank: copy_by(k, who, v_row[:, i, :], bank))
            groups += columns_of(k, h_t, 528, lambda b, h: g_t[:, b, :] if b < 4 else a_t[:])
            banks_phase(k, groups)

            def alpha(pe, banks):
                for p in range(2):
                    mm = nc.tensor.matmul(banks[0][:, p * S:(p + 1) * S], w_a[:, p * P:(p + 1) * P], a_t[:],
                                          start=True, stop=True, skip_group_check=True)
                yield mm

            def add_b(bank):
                for p in range(2):
                    ins = nc.vector.tensor_scalar(z[:, p, :], bank[:, p * S:(p + 1) * S], col("b_alpha", p), None,
                                                  ALU.add)
                return ins
            banks_phase(k, [(alpha, [("dve", add_b)])])

            def soft(s):
                yield s.activation(u[:], z[:], ACT.Abs)
                yield s.activation(u[:], u[:], ACT.Exp, scale=-1.0)
                yield s.activation(u[:], u[:], ACT.Ln, bias=1.0)
            scalar_phase(k, soft)

            def sums(v):
                yield v.memset(ones[:], 1.0)
                yield v.tensor_scalar(z[:], z[:], 0.0, None, ALU.min)
                yield v.tensor_tensor(z[:], z[:], u[:], ALU.subtract)
                yield v.tensor_scalar(z[:], z[:], 1.0 / 16.0, None, ALU.mult)
                for p in range(2):
                    yield v.tensor_tensor_scan(lc[:, p, :], r[:], z[:, p, :], 0.0, ALU.mult, ALU.add)
                yield v.tensor_scalar(qk[:, 0:2, :], qk[:, 0:2, :], 64 ** -0.5, None, ALU.mult)
                yield v.tensor_tensor(four(z[:]), four(lc[:])[:, :, :, C - 1:C].to_broadcast([P, 2, N, C]),
                                      four(lc[:]), ALU.subtract)
            vector_phase(k, sums)

            def exps(s):
                yield s.activation(z[:], z[:], ACT.Exp)
                yield s.activation(u[:], lc[:], ACT.Exp)
                yield s.activation(dec[:].unsqueeze(3), four(lc[:])[:, :, :, C - 1:C], ACT.Exp)
            scalar_phase(k, exps)

            def ins_(v):
                yield v.tensor_tensor(k_in[:], qk[:, 2:4, :], z[:], ALU.mult)
                yield v.tensor_tensor(q_in[:], qk[:, 0:2, :], u[:], ALU.mult)
                yield v.memset(states[:, :, 0, :], 0.0)
            vector_phase(k, ins_)
            k_row = keep2("k_row", [P, T_LAT, 2, P])
            k_pick = keep2("k_pick", [P, T_LAT, 2, 8, P])
            banks_phase(k, transpose_groups(k, [
                ([k_in[:, p, i * P:(i + 1) * P] for p in range(2)],
                 lambda who, bank, i=i: copy_by(k, who, k_row[:, i].rearrange("p b d -> p (b d)"), bank))
                for i in range(T_LAT)]))

            def pick(v):
                for i in range(T_LAT):
                    for p in range(2):
                        yield v.tensor_tensor(k_pick[:, i, p], k_row[:, i, p, :].unsqueeze(1).to_broadcast([P, 8, P]),
                                              chunk_is[:].unsqueeze(2).to_broadcast([P, 8, P]), ALU.mult)
            vector_phase(k, pick)
            groups = []
            for p in range(2):
                for n in range(N - 1):
                    def fill(pe, banks, p=p, n=n):
                        i, c = divmod(n, 8)
                        yield nc.tensor.matmul(banks[0][:, 0:256], k_pick[:, i, p, c, :],
                                               v_row[:, i, 256 * p:256 * p + 256], start=True, stop=True)

                    def empty(bank, p=p, n=n, who=("act", "dve")[n % 2]):
                        copy_by(k, who, states[0:64, p, n + 1, :], bank[0:64, 0:P])
                        return copy_by(k, who, states[64:P, p, n + 1, :], bank[64:P, P:2 * P])
                    groups.append((fill, [(("act", "dve")[n % 2], empty)]))
            banks_phase(k, groups)

            def recur(v):
                for n in range(1, N - 1):
                    for p in range(2):
                        yield v.scalar_tensor_tensor(out=states[:, p, n + 1, :], in0=states[:, p, n, :],
                                                     scalar=dec[:, p, n:n + 1], in1=states[:, p, n + 1, :],
                                                     op0=ALU.mult, op1=ALU.add)
            vector_phase(k, recur)
        with ExitStack() as tmp:
            w = sb("gla_w", [P, C, 2, S], where=tmp)
            s_lag = sb("gla_s_lag", [P, T_LAT, C, 4], where=tmp)
            s_mul = sb("gla_s_mul", [P, 4, C, C], where=tmp)
            s_row = sb("gla_s_row", [P, 4, C], where=tmp)
            s_full = sb("gla_s_full", [P, 4, 8, C], where=tmp)
            pairs = [(p, lag) for lag in range(C) for p in range(2)]

            def differences(v):
                yield v.memset(w[:], 0.0)
                for p, lag in pairs:
                    f = four(lc[:])[:, p]
                    yield v.tensor_tensor(four(w[:, lag])[:, p, :, lag:C], f[:, :, lag:C], f[:, :, 0:C - lag],
                                          ALU.subtract)
            vector_phase(k, differences)

            def decays(s):
                for p, lag in pairs:
                    o = four(w[:, lag])[:, p, :, lag:C]
                    yield s.activation(o, o, ACT.Exp)
            scalar_phase(k, decays)

            def products(v):
                for p, lag in pairs:
                    o = four(w[:, lag])[:, p, :, lag:C]
                    yield v.tensor_tensor(o, o, four(qk[:, 0:2, :])[:, p, :, lag:C], ALU.mult)
                    yield v.tensor_tensor(o, o, four(qk[:, 2:4, :])[:, p, :, 0:C - lag], ALU.mult)
            vector_phase(k, products)

            def sum_heads(pe, banks):
                for i in range(T_LAT):
                    for lag in range(C):
                        for p in range(2):
                            c = (i * C + lag) * 4 + 2 * p
                            mm = nc.tensor.matmul(banks[0][:, c:c + 2], w[:, lag, p, i * P:(i + 1) * P], head_is[:],
                                                  start=True, stop=True, skip_group_check=True)
                yield mm
            banks_phase(k, [(sum_heads, [("dve", lambda bank: nc.vector.tensor_copy(
                s_lag[:].rearrange("p t c h -> p (t c h)"), bank[:, 0:T_LAT * C * 4]))])])
            for i in range(T_LAT):
                def spread(v, i=i):
                    for h in range(4):
                        yield v.tensor_tensor(
                            s_mul[:, h], s_lag[:, i, :, h].unsqueeze(1).to_broadcast([P, C, C]),
                            lag_is[:].rearrange("p l j -> p j l"), ALU.mult)
                    yield v.tensor_reduce(s_row[:], s_mul[:], AX.X, ALU.add)
                    for h in range(4):
                        yield v.tensor_tensor(s_full[:, h], s_row[:, h, :].unsqueeze(1).to_broadcast([P, 8, C]),
                                              chunk_is[:].unsqueeze(2).to_broadcast([P, 8, C]), ALU.mult)
                vector_phase(k, spread)
                banks_phase(k, transpose_groups(k, [(
                    [s_full[:, h].rearrange("p n c -> p (n c)") for h in range(4)],
                    lambda who, bank, i=i: copy_by(k, who, s_t[:, i].rearrange("p h j -> p (h j)"), bank))]))
        with ExitStack() as tmp:
            o_t = sb("gla_o", [P, 4, S], where=tmp)
            sq = sb("gla_sq", [P, 4, S], where=tmp)
            groups = []
            for half in range(2):
                rows = slice(64 * half, 64 * half + 64)

                def fill(pe, banks, half=half, rows=rows):
                    for p in range(2):
                        h = 2 * p + half
                        for i in range(T_LAT):
                            c0 = p * S + i * P
                            mm = nc.tensor.matmul(banks[0][:, c0:c0 + P], v_row[:, i, h * P:(h + 1) * P], s_t[:, i, h, :],
                                                  start=True, stop=False, skip_group_check=True)
                            for c in range(8):
                                n = 8 * i + c
                                mm = nc.tensor.matmul(banks[0][:, c0 + C * c:c0 + C * c + C], states[rows, p, n, :],
                                                      q_in[rows, p, n * C:(n + 1) * C], start=False, stop=(c == 7),
                                                      skip_group_check=True)
                    yield mm

                groups.append((fill, [("dve", lambda bank, half=half: nc.vector.tensor_copy(
                    o_t[:].rearrange("p (a b) s -> p b a s", b=2)[:, half],
                    bank.rearrange("p (a s) -> p a s", a=2)))]))
            banks_phase(k, groups)

            def squares(s):
                yield s.activation(sq[:], o_t[:], ACT.Square)
                yield s.activation(g_t[:], g_t[:], ACT.Silu)
            scalar_phase(k, squares)
            groups = []
            for hp in range(2):
                def fill(pe, banks, hp=hp):
                    yield nc.tensor.matmul(banks[0], ones[:], sq[:, 2 * hp:2 * hp + 2, :].rearrange("p h s -> p (h s)"),
                                           start=True, stop=True)
                groups.append((fill, [("dve", lambda bank, hp=hp: nc.vector.tensor_scalar(
                    q_in[:].rearrange("p h s -> p (h s)") if hp == 0 else lc[:].rearrange("p h s -> p (h s)"),
                    bank, 1.0 / P, 1e-6, ALU.mult, ALU.add))]))
            banks_phase(k, groups)
            scalar_phase(k, lambda s: [s.activation(a[:], a[:], ACT.Sqrt) for a in (q_in, lc)])

            def finish(v):
                for hp, a in enumerate((q_in, lc)):
                    o = o_t[:, 2 * hp:2 * hp + 2, :]
                    yield v.reciprocal(a[:], a[:])
                    yield v.tensor_tensor(o, o, a[:], ALU.mult)
                    yield v.scalar_tensor_tensor(out=br_t[:, 0, 2 * hp:2 * hp + 2, :], in0=o, scalar=col("gla_g"),
                                                 in1=g_t[:, 2 * hp:2 * hp + 2, :], op0=ALU.mult, op1=ALU.mult)
            vector_phase(k, finish)


def conv_branch(k, t, h_t, col, br_t):
    nc, sb = k.nc, k.sb
    with ExitStack() as tmp:
        z = sb("sc_z", [P, 12, S], where=tmp)
        banks_phase(k, columns_of(k, h_t, 1536, lambda b, h: z[:, b, :]))

        def steps(v):
            u = z[:, 4:8, :]
            yield v.tensor_tensor(u, u, z[:, 8:12, :], ALU.mult)
            for b in range(4):
                o, i = br_t[:, 1, b, :], z[:, 4 + b, :]
                yield v.tensor_scalar(o, i, col("scw2", b), None, ALU.mult)
                yield v.scalar_tensor_tensor(out=o[:, 1:S], in0=i[:, 0:S - 1], scalar=col("scw1", b), in1=o[:, 1:S],
                                             op0=ALU.mult, op1=ALU.add)
                yield v.scalar_tensor_tensor(out=o[:, 2:S], in0=i[:, 0:S - 2], scalar=col("scw0", b), in1=o[:, 2:S],
                                             op0=ALU.mult, op1=ALU.add)
            yield v.tensor_tensor(br_t[:, 1], br_t[:, 1], z[:, 0:4, :], ALU.mult)
        vector_phase(k, steps)


def dilated_branch(k, t, h_t, br_t):
    nc, sb = k.nc, k.sb
    with ExitStack() as dil:
        q_t = sb("dil_q_t", [P, 12, S], where=dil)
        k_t = sb("dil_k_t", [P, 12, S], where=dil)
        vv = sb("dil_v", [P, T_LAT, 1536], where=dil)
        y = sb("dil_y", [P, T_LAT, 512], where=dil)
        mask = sb("dil_mask", [P, T_LAT, 3 * S], where=dil)
        with ExitStack() as tmp:
            z = sb("dil_z", [P, T_LAT, 3072], where=tmp)
            tabs = sb("dil_tabs", [P, T_LAT, 2, P], where=tmp)
            pos_i = sb("pos_i", [P, T_LAT], I32, where=tmp)
            pos = sb("pos", [P, T_LAT], where=tmp)
            inv = sb("inv_freq", [P, 64], where=tmp)
            ang = sb("dil_ang", [P, T_LAT, 2, 64], where=tmp)
            rnd = sb("dil_rnd", [P, T_LAT, 2, 64], where=tmp)
            load_phase(k, [(mask[:], t["dil_mask"].rearrange("(t p) k -> p t k", p=P)), (inv[:], t["inv_freq"])]
                       + [(pos_i[:, i:i + 1], t["positions_2"][0, i * P:(i + 1) * P].unsqueeze(1))
                          for i in range(T_LAT)])

            def split(who, r, n0, nn, bank):
                dst = z[:, r, n0:n0 + nn] if n0 < 3072 else vv[:, r, n0 - 3072:n0 - 3072 + nn]
                return copy_by(k, who, dst, bank)
            banks_phase(k, project_groups(k, lambda kt, r: h_t[:, kt, r * P:(r + 1) * P], DK, [P] * T_LAT, 4608,
                                          split))
            two_pi = 2.0 * math.pi
            hi = 6.28125
            lo = float(np.float32(two_pi - hi))
            magic = 12582912.0

            def angles(v):
                yield v.tensor_copy(pos[:], pos_i[:])
                for i in range(T_LAT):
                    yield v.tensor_scalar(ang[:, i, 0, :], inv[:], pos[:, i:i + 1], None, ALU.mult)
                    yield v.tensor_scalar(rnd[:, i, 0, :], ang[:, i, 0, :], 1.0 / two_pi, None, ALU.mult)
                    yield v.tensor_scalar(rnd[:, i, 1, :], rnd[:, i, 0, :], 0.25, None, ALU.add)
                yield v.tensor_scalar(rnd[:], rnd[:], magic, None, ALU.add)
                yield v.tensor_scalar(rnd[:], rnd[:], -magic, None, ALU.add)
                for i in range(T_LAT):
                    yield v.tensor_copy(ang[:, i, 1, :], ang[:, i, 0, :])
                yield v.scalar_tensor_tensor(out=ang[:], in0=rnd[:], scalar=-hi, in1=ang[:], op0=ALU.mult, op1=ALU.add)
                yield v.scalar_tensor_tensor(out=ang[:], in0=rnd[:], scalar=-lo, in1=ang[:], op0=ALU.mult, op1=ALU.add)
                for i in range(T_LAT):
                    yield v.tensor_scalar(ang[:, i, 1, :], ang[:, i, 1, :], math.pi / 2, None, ALU.add)
                yield v.tensor_scalar(ang[:], ang[:], 3.1415925, -3.1415925, ALU.min, ALU.max)
            vector_phase(k, angles)

            def sines(s):
                for i in range(T_LAT):
                    yield s.activation(tabs[:, i, 1, 64:P], ang[:, i, 0, :], ACT.Sin)
                    yield s.activation(tabs[:, i, 1, 0:64], ang[:, i, 0, :], ACT.Sin, scale=-1.0)
                    yield s.activation(tabs[:, i, 0, 0:64], ang[:, i, 1, :], ACT.Sin)
                    yield s.activation(tabs[:, i, 0, 64:P], ang[:, i, 1, :], ACT.Sin)
            scalar_phase(k, sines)
            heads = lambda a: a.rearrange("p (h d) -> p h d", d=P)
            with ExitStack() as tr:
                t1 = sb("dil_t1", [P, 1536], where=tr)
                zr = sb("dil_zr", [P, 1536], where=tr)

                def rotate(v):
                    for i in range(T_LAT):
                        for half in range(2):
                            zz = z[:, i, 1536 * half:1536 * half + 1536]
                            yield from rope_steps(v, heads(zz), heads(zr[:]), heads(t1[:]), tabs[:, i, 0, :],
                                                  tabs[:, i, 1, :], 12, P)
                            yield v.tensor_copy(zz, zr[:])
                vector_phase(k, rotate)
            jobs = []
            for half, dst in enumerate((q_t, k_t)):
                for b in range(0, 12, 2):
                    jobs.append(([z[:, i, 1536 * half + (b + a) * P:1536 * half + (b + a + 1) * P]
                                  for a in range(2) for i in range(T_LAT)],
                                 lambda who, bank, b=b, dst=dst: copy_by(
                                     k, who, dst[:, b:b + 2, :].rearrange("p b s -> p (b s)"), bank)))
            banks_phase(k, transpose_groups(k, jobs))
        units = []
        for i in range(T_LAT):
            for h in range(4):
                units.append(dict(
                    qk=[(q_t[:, 4 * g + h, i * P:(i + 1) * P], k_t[:, 4 * g + h, :]) for g in range(3)],
                    v=[vv[:, j, (4 * g + h) * P:(4 * g + h + 1) * P] for g in range(3) for j in range(T_LAT)],
                    mask=mask[:, i, :], sink=None, out=y[:, i, h * P:(h + 1) * P]))
        attention(k, "dil", units, P ** -0.5, 3 * S, P)
        banks_phase(k, transpose_groups(k, [([y[:, i, b * P:(b + 1) * P] for i in range(T_LAT)],
                                             lambda who, bank, b=b: copy_by(k, who, br_t[:, 2, b, :], bank))
                                            for b in range(4)]))


def kernel(**inputs):
    import numpy as _np
    import concourse.bacc as _bacc
    from concourse import mybir as _mybir
    from concourse.bass_utils import run_bass_kernel_spmd as _run

    nc = _bacc.Bacc("TRN2", target_bir_lowering=False, num_devices=1)
    arrays, aps = {}, {}
    for name, a in list(inputs.items()) + list(shape_constants().items()):
        a = _np.ascontiguousarray(a)
        arrays[f"in_{name}_dram"] = a
        aps[name] = nc.dram_tensor(f"in_{name}_dram", a.shape, _mybir.dt.from_np(a.dtype), kind="ExternalInput").ap()
    out = nc.dram_tensor("out_0_dram", (1, S, D), F32, kind="ExternalOutput").ap()
    two_blocks(nc, aps, out)
    r = _run(nc, [arrays], core_ids=[0])
    return r.results[0]["out_0_dram"]
```

```python
import math
from contextlib import ExitStack

import numpy as np
import concourse.bass as bass
from concourse import mybir

F32 = mybir.dt.float32
I32 = mybir.dt.int32
U32 = mybir.dt.uint32
ACT = mybir.ActivationFunctionType
ALU = mybir.AluOpType
AX = mybir.AxisListType

P = 128
D = 1024
DK = D // P
S = 256
T_LAT = S // P
T_ALL = 2 * T_LAT
SLOTS = 8
SLOT = 64
BANK = 512
NEG = -1.0e30
STOP = None


class Tally:

    def __init__(self, sem):
        self.sem, self.n = sem, 0

    def mark(self, ins, by=1):
        ins.then_inc(self.sem, by)
        self.n += by
        return self.n


class Signal:

    def __init__(self, sem):
        self.sem, self.base = sem, 0

    def at(self, v):
        return self.sem, self.base + v


class Core:

    def __init__(self, nc, ctx):
        self.nc, self.ctx = nc, ctx
        sem = lambda n: ctx.enter_context(nc.semaphore(n))
        self.tensor_done = Tally(sem("tensor_done"))
        self.act_evac = Tally(sem("act_evac"))
        self.dve_evac = Tally(sem("dve_evac"))
        self.dve_step = Tally(sem("dve_step"))
        self.act_step = Tally(sem("act_step"))
        self.pool_step = Tally(sem("pool_step"))
        self.load_done = Tally(sem("load_done"))
        self.store_done = Tally(sem("store_done"))
        self.soft_done = Tally(sem("table_done"))
        self.gathered = [Tally(sem(f"gathered{i}")) for i in range(4)]
        self.stored = [Tally(sem(f"y_stored{i}")) for i in range(2)]
        self.scores_ready = Signal(sem("scores_ready"))
        self.max_ready = Signal(sem("max_ready"))
        self.probs_ready = Signal(sem("probs_ready"))
        self.turned = Signal(sem("probs_turned"))
        self.turned_copied = Signal(sem("turned_copied"))
        self.mixed = Signal(sem("values_mixed"))
        self.out_done = Signal(sem("out_done"))
        self.slot_full = [Tally(sem(f"slot_full{i}")) for i in range(SLOTS)]
        self.psum = ctx.enter_context(nc.psum_tensor("psum", [P, 8, BANK], F32))
        self.ring = [self.sb(f"ring{i}", [P, 4, BANK]) for i in range(SLOTS)]
        self.chunks, self.issued, self.taken, self.used_at = [], 0, 0, []

    def sb(self, name, shape, dt=F32, where=None):
        return (where or self.ctx).enter_context(self.nc.sbuf_tensor(name, shape, dt))

    def plan(self, w, k_rows, n_cols, n_first=0):
        for n0 in range(n_first, n_first + n_cols, BANK):
            nn = min(BANK, n_first + n_cols - n0)
            for k0 in range(0, k_rows, 4 * P):
                kt = min(4, (k_rows - k0) // P)
                self.chunks.append((w[k0:k0 + kt * P, n0:n0 + nn].rearrange("(j p) n -> p j n", p=P), kt, nn))

    def pump(self, sp):
        while self.issued < len(self.chunks):
            j = self.issued
            if j >= SLOTS:
                if j - SLOTS >= len(self.used_at):
                    break
                sp.wait_ge(self.tensor_done.sem, self.used_at[j - SLOTS])
            src, kt, nn = self.chunks[j]
            self.slot_full[j % SLOTS].mark(sp.dma_start(self.ring[j % SLOTS][:, 0:kt, 0:nn], src), 16)
            self.issued += 1

    def take(self, pe, kt, nn):
        j = self.taken
        self.taken += 1
        assert self.chunks[j][1:] == (kt, nn), (j, self.chunks[j][1:], kt, nn)
        pe.wait_ge(self.slot_full[j % SLOTS].sem, 16 * (j // SLOTS + 1))
        return self.ring[j % SLOTS][:, 0:kt, 0:nn]

    def used(self, at):
        self.used_at.append(at)


def chain(eng, tally, ins):
    eng.wait_ge(tally.sem, tally.mark(ins[-1] if isinstance(ins, list) else ins))


def banks_phase(k, groups, pool_program=None, act_last=None):
    nc = k.nc
    act0, dve0 = k.act_evac.n, k.dve_evac.n
    filled = []
    with nc.Block(no_gpsimd_drain=True) as block:
        @block.tensor
        def _(pe):
            holder = [None] * 8
            emptied = {"act": act0, "dve": dve0}
            at = 0
            for fill, empties, *after in groups:
                if after and emptied["act"] > act0:
                    pe.wait_ge(k.act_evac.sem, emptied["act"])
                if after and emptied["dve"] > dve0:
                    pe.wait_ge(k.dve_evac.sem, emptied["dve"])
                mine = [(at + i) % 8 for i in range(len(empties))]
                at += len(empties)
                for b in mine:
                    if holder[b] is not None:
                        pe.wait_ge(*holder[b])
                last = None
                for last in fill(pe, [k.psum[:, b, :] for b in mine]):
                    done = k.tensor_done.mark(last)
                filled.append(done)
                for b, (who, _) in zip(mine, empties):
                    emptied[who] += 1
                    holder[b] = (k.act_evac.sem if who == "act" else k.dve_evac.sem, emptied[who])

        def drain(eng, who, tally):
            at = 0
            for g, (_, empties, *_) in enumerate(groups):
                if any(w == who for w, _ in empties):
                    eng.wait_ge(k.tensor_done.sem, filled[g])
                for w, empty in empties:
                    if w == who:
                        tally.mark(empty(k.psum[:, at % 8, :]))
                    at += 1
            eng.wait_ge(tally.sem, tally.n)

        @block.scalar
        def _(act):
            drain(act, "act", k.act_evac)
            if act_last is not None:
                act_last(act)

        @block.vector
        def _(dve):
            drain(dve, "dve", k.dve_evac)

        if pool_program is not None:
            @block.gpsimd
            def _(pool):
                pool_program(pool)

        @block.sync
        def _(sp):
            k.pump(sp)


def copy_by(k, who, out, src):
    return k.nc.scalar.copy(out, src) if who == "act" else k.nc.vector.tensor_copy(out, src)


def turns():
    i = 0
    while True:
        yield ("act", "dve")[i % 2]
        i += 1


def project_groups(k, lhs, k_tiles, rows, n_cols, empty, who=None):
    groups = []
    turn = turns()
    for n0 in range(0, n_cols, BANK):
        nn = min(BANK, n_cols - n0)

        def fill(pe, banks, nn=nn):
            for k0 in range(0, k_tiles, 4):
                kt = min(4, k_tiles - k0)
                w = k.take(pe, kt, nn)
                for r, m in enumerate(rows):
                    for j in range(kt):
                        mm = k.nc.tensor.matmul(banks[r][0:m, 0:nn], lhs(k0 + j, r), w[:, j, :],
                                                start=(k0 + j == 0), stop=(k0 + j == k_tiles - 1))
                yield mm
                k.used(k.tensor_done.n)

        empties = []
        for r, m in enumerate(rows):
            w = who or next(turn)
            empties.append((w, lambda bank, w=w, r=r, n0=n0, nn=nn, m=m: empty(w, r, n0, nn, bank[0:m, 0:nn])))
        groups.append((fill, empties))
    return groups


def project_column_groups(k, rhs, k_tiles, n_rhs, n_cols, empty, who=None):
    groups = []
    turn = turns()
    for n0 in range(0, n_cols, BANK):
        nn = min(BANK, n_cols - n0)
        blocks = [(b, min(P, nn - b)) for b in range(0, nn, P)]

        def fill(pe, banks, nn=nn, blocks=blocks):
            for k0 in range(0, k_tiles, 4):
                kt = min(4, k_tiles - k0)
                w = k.take(pe, kt, nn)
                for i, (b, h) in enumerate(blocks):
                    for j in range(kt):
                        mm = k.nc.tensor.matmul(banks[i][0:h, 0:n_rhs], w[:, j, b:b + h], rhs(k0 + j),
                                                start=(k0 + j == 0), stop=(k0 + j == k_tiles - 1))
                yield mm
                k.used(k.tensor_done.n)

        empties = []
        for b, h in blocks:
            w = who or next(turn)
            empties.append((w, lambda bank, w=w, i=(n0 + b) // P, h=h: empty(w, i, h, bank[0:h, 0:n_rhs])))
        groups.append((fill, empties))
    return groups


def transpose_groups(k, jobs, who=None):
    groups = []
    turn = turns()
    for sources, empty in jobs:
        def fill(pe, banks, sources=sources):
            for i, src in enumerate(sources):
                r, w = src.shape
                mm = k.nc.tensor.transpose(banks[0][0:w, i * P:i * P + r], src, k.ident[0:r, 0:r])
            yield mm
        w = who or next(turn)
        wd = sources[0].shape[1]
        n = len(sources) * P
        groups.append((fill, [(w, lambda bank, w=w, wd=wd, n=n, empty=empty: empty(w, bank[0:wd, 0:n]))]))
    return groups


def vector_phase(k, steps):
    with k.nc.Block(no_gpsimd_drain=True) as block:
        @block.vector
        def _(dve):
            for ins in steps(k.nc.vector):
                chain(dve, k.dve_step, ins)

        @block.sync
        def _(sp):
            k.pump(sp)


def load_phase(k, loads):
    with k.nc.Block(no_gpsimd_drain=True) as block:
        @block.scalar
        def _(act):
            for out, src in loads:
                k.load_done.mark(act.dma_start(out, src), 16)
            act.wait_ge(k.load_done.sem, k.load_done.n)

        @block.sync
        def _(sp):
            k.pump(sp)


def inv_rms(k, xs, width, eps, rs, junk):
    nc, n = k.nc, len(xs)
    marks = {}
    with nc.Block(no_gpsimd_drain=True) as block:
        @block.scalar
        def _(act):
            for i in range(0, n, 2):
                chain(act, k.act_step, nc.scalar.activation(junk[0], xs[i], ACT.Square, accum_out=rs[:, i:i + 1]))
            marks["squares"] = k.act_step.n
            act.wait_ge(k.dve_step.sem, k.dve_step.n + n // 2 + 1)
            chain(act, k.act_step, nc.scalar.activation(rs[:, 0:n], rs[:, 0:n], ACT.Sqrt))
            marks["root"] = k.act_step.n

        @block.vector
        def _(dve):
            for i in range(1, n, 2):
                chain(dve, k.dve_step, nc.vector.tensor_tensor_reduce(
                    out=junk[1], in0=xs[i], in1=xs[i], scale=1.0, scalar=0.0, op0=ALU.mult, op1=ALU.add,
                    accum_out=rs[:, i:i + 1]))
            dve.wait_ge(k.act_step.sem, marks["squares"])
            k.dve_step.mark(nc.vector.tensor_scalar(rs[:, 0:n], rs[:, 0:n], 1.0 / width, eps, ALU.mult, ALU.add))
            dve.wait_ge(k.act_step.sem, marks["root"])
            chain(dve, k.dve_step, nc.vector.reciprocal(rs[:, 0:n], rs[:, 0:n]))

        @block.sync
        def _(sp):
            k.pump(sp)


def norm_to_columns(k, tag, xs, width, eps, out, scale_bias):
    nc = k.nc
    with ExitStack() as tmp:
        n = len(xs)
        rs = k.sb(f"rs_{tag}", [P, n], where=tmp)
        xn = k.sb(f"xn_{tag}", [P, n, width], where=tmp)
        inv_rms(k, xs, width, eps, rs, [xn[:, 0, :], xn[:, 1, :]])
        with nc.Block(no_gpsimd_drain=True) as block:
            @block.scalar
            def _(act):
                for i in range(0, n, 2):
                    k.act_step.mark(nc.scalar.mul(xn[:, i, :], xs[i], rs[:, i:i + 1]))
                act.wait_ge(k.act_step.sem, k.act_step.n)

            @block.vector
            def _(dve):
                for i in range(1, n, 2):
                    k.dve_step.mark(nc.vector.tensor_scalar(xn[:, i, :], xs[i], rs[:, i:i + 1], None, ALU.mult))
                if n > 1:
                    dve.wait_ge(k.dve_step.sem, k.dve_step.n)

            @block.sync
            def _(sp):
                k.pump(sp)

        jobs = []
        for kt in range(width // P):
            def empty(who, bank, kt=kt):
                for t0, tn, sc, bi in scale_bias(kt):
                    o, i = out[:, kt, t0:t0 + tn], bank[:, t0:t0 + tn]
                    if who == "act":
                        ins = nc.scalar.activation(o, i, ACT.Identity, scale=sc, bias=0.0 if bi is None else bi)
                    elif bi is None:
                        ins = nc.vector.tensor_scalar(o, i, sc, None, ALU.mult)
                    else:
                        ins = nc.vector.tensor_scalar(o, i, sc, bi, ALU.mult, ALU.add)
                return ins
            jobs.append(([xn[:, i, kt * P:(kt + 1) * P] for i in range(n)], empty))
        banks_phase(k, transpose_groups(k, jobs))


def attention(k, tag, units, scale, width, dv):
    nc = k.nc
    n = len(units)
    wide = 1 if width <= BANK else 2
    N_SCORES, N_TURNED, N_OUT = (3, 2, 3) if wide == 1 else (2, 1, 2)
    N_PROBS, N_PROBS_T, N_STAT = 3, 2, 4
    turned_bank = wide * N_SCORES
    out_bank = turned_bank + wide * N_TURNED
    with ExitStack() as tmp:
        masked = None
        if units[0]["mask"] is not None:
            masked = k.sb(f"sc_{tag}", [P, N_SCORES, width], where=tmp)
        probs = k.sb(f"pr_{tag}", [P, N_PROBS, width], where=tmp)
        probs_t = k.sb(f"pt_{tag}", [P, N_PROBS_T, width], where=tmp)
        stat = k.sb(f"st_{tag}", [P, N_STAT, 4], where=tmp)
        scores_ready, max_ready, probs_ready = k.scores_ready, k.max_ready, k.probs_ready
        turned, turned_copied, mixed, out_done = k.turned, k.turned_copied, k.mixed, k.out_done

        def widths(u):
            return sum(kk.shape[-1] for _, kk in u["qk"])

        def banks(first, i, depth, w):
            b = first + wide * (i % depth)
            return k.psum[:, b:b + wide, :].rearrange("p b n -> p (b n)")[:, 0:w]

        s_view = lambda i, w: banks(0, i, N_SCORES, w)
        t_view = lambda i, w: banks(turned_bank, i, N_TURNED, w)
        o_view = lambda i: k.psum[:, out_bank + i % N_OUT, 0:dv]
        column = lambda i, c: stat[:, i % N_STAT, c:c + 1]

        with nc.Block(no_gpsimd_drain=True) as block:
            @block.tensor
            def _(pe):
                def scores(i):
                    c = 0
                    for q, kk in units[i]["qk"]:
                        w = kk.shape[-1]
                        mm = nc.tensor.matmul(s_view(i, c + w)[:, c:c + w], q, kk, start=(c % BANK == 0), stop=True,
                                              skip_group_check=True)
                        c += w
                    mm.then_inc(scores_ready.sem, 1)

                def mix(i):
                    pe.wait_ge(*turned_copied.at(i + 1))
                    if i >= N_OUT:
                        pe.wait_ge(*out_done.at(i - N_OUT + 1))
                    w = widths(units[i])
                    for j in range(w // P):
                        mm = nc.tensor.matmul(o_view(i), probs_t[:, i % N_PROBS_T, j * P:(j + 1) * P],
                                              units[i]["v"][j], start=(j == 0), stop=(j == w // P - 1))
                    mm.then_inc(mixed.sem, 1)

                for i in range(min(N_SCORES, n)):
                    scores(i)
                for i in range(n):
                    w = widths(units[i])
                    pe.wait_ge(*probs_ready.at(i + 1))
                    if i >= N_TURNED:
                        pe.wait_ge(*turned_copied.at(i - N_TURNED + 1))
                    for j in range(w // P):
                        mm = nc.tensor.transpose(t_view(i, w)[:, j * P:(j + 1) * P],
                                                 probs[:, i % N_PROBS, j * P:(j + 1) * P], k.ident[:])
                    mm.then_inc(turned.sem, 1)
                    if i + N_SCORES < n:
                        scores(i + N_SCORES)
                    if i >= 1:
                        mix(i - 1)
                mix(n - 1)

            @block.vector
            def _(dve):
                v = nc.vector

                def maxima(i):
                    u, w = units[i], widths(units[i])
                    dve.wait_ge(*scores_ready.at(i + 1))
                    src, sc = s_view(i, w), scale
                    if u["mask"] is not None:
                        src, sc = masked[:, i % N_SCORES, 0:w], 1.0
                        chain(dve, k.dve_step, v.scalar_tensor_tensor(out=src, in0=s_view(i, w), scalar=scale,
                                                                      in1=u["mask"], op0=ALU.mult, op1=ALU.add))
                    chain(dve, k.dve_step, v.reduce_max(column(i, 0), src, AX.X))
                    if u["sink"] is not None:
                        last = v.tensor_scalar(column(i, 1), column(i, 0), -sc, u["minus_sink"], ALU.mult, ALU.min)
                    else:
                        last = v.tensor_scalar(column(i, 1), column(i, 0), -sc, None, ALU.mult)
                    last.then_inc(max_ready.sem, 1)

                def finish(i):
                    u = units[i]
                    dve.wait_ge(*mixed.at(i + 1))
                    dve.wait_ge(*probs_ready.at(i + 1))
                    if u["sink"] is not None:
                        chain(dve, k.dve_step, v.tensor_tensor(column(i, 2), column(i, 2), column(i, 3), ALU.add))
                    chain(dve, k.dve_step, v.reciprocal(column(i, 2), column(i, 2)))
                    v.tensor_scalar(u["out"], o_view(i), column(i, 2), None, ALU.mult).then_inc(out_done.sem, 1)

                for i in range(n):
                    maxima(i)
                    if i >= 2:
                        finish(i - 2)
                for i in range(max(0, n - 2), n):
                    finish(i)
                dve.wait_ge(*out_done.at(n))

            @block.scalar
            def _(act):
                def turn_copy(i):
                    w = widths(units[i])
                    act.wait_ge(*turned.at(i + 1))
                    if i >= N_PROBS_T:
                        act.wait_ge(*mixed.at(i - N_PROBS_T + 1))
                    nc.scalar.copy(probs_t[:, i % N_PROBS_T, 0:w], t_view(i, w)).then_inc(turned_copied.sem, 1)

                for i in range(n):
                    u, w = units[i], widths(units[i])
                    act.wait_ge(*max_ready.at(i + 1))
                    if i >= N_PROBS:
                        act.wait_ge(*turned.at(i - N_PROBS + 1))
                    if i >= N_STAT:
                        act.wait_ge(*out_done.at(i - N_STAT + 1))
                    if u["sink"] is not None:
                        nc.scalar.activation(column(i, 3), u["sink"], ACT.Exp, bias=column(i, 1))
                    src, sc = (s_view(i, w), scale) if u["mask"] is None else (masked[:, i % N_SCORES, 0:w], 1.0)
                    nc.scalar.activation(probs[:, i % N_PROBS, 0:w], src, ACT.Exp, scale=sc, bias=column(i, 1),
                                         accum_out=column(i, 2)).then_inc(probs_ready.sem, 1)
                    if i >= 1:
                        turn_copy(i - 1)
                turn_copy(n - 1)

            @block.sync
            def _(sp):
                k.pump(sp)
        for signal in (scores_ready, max_ready, probs_ready, turned, turned_copied, mixed, out_done):
            signal.base += n


def rope_steps(v, jobs):
    products, sums = [], []
    for x, out, t1, cos2, sin2, heads, hd in jobs:
        h2 = hd // 2
        c = cos2.unsqueeze(1).to_broadcast([P, heads, hd])
        s_lo = sin2[:, 0:h2].unsqueeze(1).to_broadcast([P, heads, h2])
        s_hi = sin2[:, h2:hd].unsqueeze(1).to_broadcast([P, heads, h2])
        products += [v.tensor_tensor(t1[:, :, 0:h2], x[:, :, h2:hd], s_lo, ALU.mult),
                     v.tensor_tensor(t1[:, :, h2:hd], x[:, :, 0:h2], s_hi, ALU.mult),
                     v.tensor_tensor(out, x, c, ALU.mult)]
    yield products
    yield [v.tensor_tensor(out, out, t1, ALU.add) for _, out, t1, *_ in jobs]


class Stop(Exception):
    pass


def shape_constants():
    f = np.float32
    tok = np.arange(S)
    row, col = (tok // 64).astype(f), (tok % 64).astype(f)

    def rope_table(dim):
        nf = dim // 4
        inv = (f(10000.0) ** (-np.arange(nf, dtype=f) / f(nf))).astype(f)
        ang = np.concatenate([row[:, None] * inv, col[:, None] * inv], axis=-1)
        c, s = np.cos(ang), np.sin(ang)
        return np.stack([np.concatenate([c, c], -1), np.concatenate([-s, s], -1)], 1).astype(f)

    q, kk = tok[:, None], tok[None, :]
    swa = np.where(np.abs(q - kk) <= 128, 0.0, NEG)
    swa = np.concatenate([swa, np.zeros((S, S))], 1).astype(f)
    dil = np.concatenate([np.where((q >= kk) & ((q - kk) % d == 0) & (q - kk <= 128 * d), 0.0, NEG)
                          for d in (1, 4, 16)], 1).astype(f)
    i16 = np.arange(P) % 16
    lag = (i16[:, None, None] - np.arange(16)[None, :, None] == np.arange(16)[None, None, :]).astype(f)
    sel = np.zeros((2, 2, P), f)
    sel[0, 0], sel[1, 1] = 1.0, 1.0
    inv = (f(10000.0) ** (-np.arange(0, P, 2, dtype=f) / f(P))).astype(f)
    head = np.zeros((P, 2), f)
    head[:64, 0], head[64:, 1] = 1.0, 1.0
    return {
        "ident": np.eye(P, dtype=f), "rope64": rope_table(64), "rope32": rope_table(32), "swa_mask": swa,
        "dil_mask": dil, "row_pick": sel, "inv_freq": np.tile(inv, (P, 1)),
        "lag_is": lag, "chunk_is": (np.arange(P)[:, None] // 16 == np.arange(8)[None, :]).astype(f),
        "head_is": head, "within_chunk": np.tile((tok % 16 != 0).astype(f), (P, 1)),
        "before": np.triu(np.ones((P, P), f), 1), "expert_number": np.tile(np.arange(32, dtype=f), (P, 1)),
        "descending": np.tile(np.arange(32, 0, -1, dtype=f), (P, 1)),
    }


def two_blocks(nc, t, out):
    try:
        with ExitStack() as ctx:
            program(Core(nc, ctx), t, out)
    except (Stop, AssertionError):
        if STOP is None:
            raise


def stop_at(name):
    if STOP == name:
        raise Stop()


def program(k, t, out):
    nc = k.nc
    sb = k.sb
    E = (range(32))

    for l in range(2):
        k.plan(t["ada_w"][l], D, 6 * D)
        if l == 0:
            k.plan(t["ab_w_in"][0], D, 1184)
            k.plan(t["mla_w_uq"][0], 256, 768)
            k.plan(t["mla_w_ukv"][0], 128, 1024)
            k.plan(t["ab_w_out"][0], D, D)
        else:
            k.plan(t["diff_w_in"][0], D, 3072)
            k.plan(t["diff_w_out"][0], D, D)
        for e in E:
            k.plan(t["expert_w1"][l, e], D, 512)
            k.plan(t["expert_w3"][l, e], D, 512)
            k.plan(t["expert_w2"][l, e], 512, D)
    w_in = t["w_in_2"][0]
    for first, cols in ((0, 512), (512, 512), (1024, 528), (1552, 1536), (3088, 4608)):
        k.plan(w_in, D, cols, first)
    k.plan(t["w_gate_2"][0], D, 3 * D)
    for g in range(3):
        k.plan(t["w_branch_2"][0, g], 512, D)
    k.plan(t["w_mix_out_2"][0], D, D)
    k.plan(t["w_ff_gate_2"][0], D, 2816)
    k.plan(t["w_ff_up_2"][0], D, 2816)
    k.plan(t["w_ff_down_2"][0], 2816, D)

    k.ident = sb("ident", [P, P])
    x = sb("x", [P, T_ALL, D])
    h_t = sb("h_t", [P, DK, 2 * S])
    cols = sb("cols", [P, 3 * P])
    rope64 = sb("rope64", [P, T_LAT, 2, 64])
    rope32 = sb("rope32", [P, T_LAT, 2, 32])
    row_pick = sb("row_pick", [2, 2, P])
    descending = sb("descending", [P, 32])
    x_dram = t["x"][0].rearrange("(t p) d -> p t d", p=P)
    ctx_dram = t["ctx"][0].rearrange("(t p) d -> p t d", p=P)
    vec = lambda a: a.rearrange("(r c) -> r c", c=P)
    packs = [[("c", t["c"][0]), ("c_ctx", t["c_ctx"]), ("mix0", t["norm_mix"][0]), ("mix1", t["norm_mix"][1]),
              ("ffn0", t["norm_ffn"][0]), ("ffn1", t["norm_ffn"][1]), ("pre_mix", t["pre_mix_g_2"][0]),
              ("pre_ffn", t["pre_ffn_g_2"][0]), ("b_gate", t["b_gate_2"][0])],
             [("ffw0", t["ff_conv_w_2"][0, 0]), ("ffw1", t["ff_conv_w_2"][0, 1]), ("ffw2", t["ff_conv_w_2"][0, 2]),
              ("ff_b", t["ff_conv_b_2"][0]), ("scw0", t["sc_conv_w_2"][0, 0]), ("scw1", t["sc_conv_w_2"][0, 1]),
              ("scw2", t["sc_conv_w_2"][0, 2]), ("b_alpha", t["b_alpha_2"][0]), ("q_norm", t["mla_q_norm"][0]),
              ("kv_norm", t["mla_kv_norm"][0]), ("gla_g", t["gla_norm_g_2"][0])]]
    where = {}
    with ExitStack() as tmp:
        pk = [sb(f"pack{i}", [P, P], where=tmp) for i in range(2)]
        with nc.Block(no_gpsimd_drain=True) as block:
            @block.gpsimd
            def _(pool):
                for p in pk:
                    chain(pool, k.pool_step, nc.gpsimd.memset(p[:], 0.0))
        loads = [(k.ident[:], t["ident"]), (x[:, 0:T_LAT, :], x_dram), (x[:, T_LAT:T_ALL, :], ctx_dram),
                 (rope64[:], t["rope64"].rearrange("(t p) a b -> p t a b", p=P)),
                 (rope32[:], t["rope32"].rearrange("(t p) a b -> p t a b", p=P)),
                 (row_pick[:], t["row_pick"]), (descending[:], t["descending"])]
        for i, pack in enumerate(packs):
            r = 0
            for name, a in pack:
                n = a.shape[0] // P
                loads.append((pk[i][r:r + n, :], vec(a)))
                where[name] = i * P + r
                r += n
        load_phase(k, loads)
        banks_phase(k, transpose_groups(k, [([p[:] for p in pk],
                                             lambda who, bank: copy_by(k, who, cols[:, 0:2 * P], bank))]))
    col = lambda name, i=0, n=1: cols[:, where[name] + i:where[name] + i + n]
    stop_at("setup")

    mod_cols = sb("mod_cols", [P, 4, DK, 2])
    mod_a = sb("mod_a", [P, 2, 2, DK])
    first = ctx_first = ExitStack()
    with first:
        gates = sb("gates", [P, 2, 2, D], where=first)
        for l in range(2):
            modulations(k, t, l, col, row_pick, mod_cols, mod_a, gates)
            stop_at(f"ada{l}")
            tiles = list(range(T_ALL))

            def shift_scale(which, n_ctx):
                def f(kt):
                    r = [(0, S, mod_a[:, which, 0, kt:kt + 1], mod_cols[:, 2 * which, kt, 0:1])]
                    if n_ctx:
                        r.append((S, S, mod_a[:, which, 1, kt:kt + 1], mod_cols[:, 2 * which, kt, 1:2]))
                    return r
                return f
            norm_to_columns(k, f"mix{l}", [x[:, i, :] for i in tiles], D, 1e-6, h_t, shift_scale(0, True))
            stop_at(f"norm{l}")
            if l == 0:
                swa_mla(k, t, x, h_t, gates, col, rope64, rope32)
            else:
                differential(k, t, x, h_t, gates, rope64)
            stop_at(f"mixer{l}")
            tiles = list(range(T_ALL if l == 0 else T_LAT))
            norm_to_columns(k, f"ffn{l}", [x[:, i, :] for i in tiles], D, 1e-6, h_t, shift_scale(1, l == 0))
            stop_at(f"normf{l}")
            experts(k, t, l, x, h_t, gates, len(tiles), descending)
            stop_at(f"moe{l}")
    row_norm(k, t, x)
    stop_at("block1")
    second_block(k, t, x, h_t, col, out)


def row_norm(k, t, x):
    nc = k.nc
    with ExitStack() as tmp:
        g = k.sb("final_g", [P, D], where=tmp)
        rs = k.sb("rs_final", [P, T_LAT], where=tmp)
        junk = k.sb("junk_final", [P, 2, D], where=tmp)
        load_phase(k, [(g[:], t["final_norm"].partition_broadcast(P))])
        inv_rms(k, [x[:, i, :] for i in range(T_LAT)], D, 1e-6, rs, [junk[:, 0, :], junk[:, 1, :]])

        def steps(v):
            for i in range(T_LAT):
                yield v.scalar_tensor_tensor(out=x[:, i, :], in0=x[:, i, :], scalar=rs[:, i:i + 1], in1=g[:],
                                             op0=ALU.mult, op1=ALU.mult)
        vector_phase(k, steps)


def modulations(k, t, l, col, row_pick, mod_cols, mod_a, gates):
    nc, sb = k.nc, k.sb
    with ExitStack() as tmp:
        sc = sb(f"silu_c{l}", [P, DK, 2], where=tmp)
        rows = sb(f"mod_rows{l}", [2, 6 * D], where=tmp)
        bias = sb(f"mod_bias{l}", [2, 6 * D], where=tmp)
        with nc.Block(no_gpsimd_drain=True) as block:
            @block.scalar
            def _(act):
                for r in range(2):
                    k.load_done.mark(act.dma_start(bias[r:r + 1, :], t["ada_b"][l:l + 1, :]), 16)
                for i, name in enumerate(("c", "c_ctx")):
                    chain(act, k.act_step, nc.scalar.activation(sc[:, :, i], col(name, 0, DK), ACT.Silu))
                act.wait_ge(k.load_done.sem, k.load_done.n)

            @block.sync
            def _(sp):
                k.pump(sp)

        def add_bias(who, r, n0, nn, bank):
            return nc.vector.tensor_tensor(rows[:, n0:n0 + nn], bank, bias[:, n0:n0 + nn], ALU.add)
        banks_phase(k, project_groups(k, lambda kt, r: sc[:, kt, :], DK, [2], 6 * D, add_bias, "dve"))

        def fill_columns(pe, banks):
            for i, kind in enumerate((0, 1, 3, 4)):
                for kt in range(DK):
                    c = 2 * (i * DK + kt)
                    mm = nc.tensor.transpose(banks[0][:, c:c + 2], rows[:, kind * D + kt * P:kind * D + (kt + 1) * P],
                                             k.ident[0:2, 0:2])
            yield mm

        groups = [(fill_columns, [("act", lambda bank: nc.scalar.copy(
            mod_cols[:].rearrange("p a b c -> p (a b c)"), bank[:, 0:8 * DK]))])]
        for s in range(2):
            for g, kind in enumerate((2, 5)):
                for half in range(2):
                    def spread(pe, banks, s=s, at=kind * D + half * BANK):
                        yield nc.tensor.matmul(banks[0], row_pick[:, s, :], rows[:, at:at + BANK], start=True, stop=True)
                    who = ("act", "dve")[half]
                    groups.append((spread, [(who, lambda bank, who=who, s=s, g=g, half=half: copy_by(
                        k, who, gates[:, s, g, half * BANK:(half + 1) * BANK], bank))]))
        banks_phase(k, groups)

        def gains(v):
            for which in range(2):
                for s in range(2):
                    yield v.scalar_tensor_tensor(out=mod_a[:, which, s, :], in0=mod_cols[:, 2 * which + 1, :, s],
                                                 scalar=1.0, in1=col(("mix", "ffn")[which] + str(l), 0, DK),
                                                 op0=ALU.add, op1=ALU.mult)
        vector_phase(k, gains)


def gated_residual(k, tag, o, x, gates, which, h_t, n_tiles):
    nc = k.nc
    jobs = [([o[:, i, kt * P:(kt + 1) * P] for i in range(n_tiles)],
             lambda who, bank, kt=kt: copy_by(k, who, h_t[:, kt, 0:n_tiles * P], bank)) for kt in range(DK)]
    banks_phase(k, transpose_groups(k, jobs))
    with ExitStack() as tmp:
        part = k.sb(f"gated_{tag}", [P, BANK], where=tmp)

        def add(who, r, n0, nn, bank):
            g = gates[:, 0 if r < T_LAT else 1, which, n0:n0 + nn]
            nc.vector.wait_ge(k.dve_evac.sem, k.dve_evac.n)
            chain(nc.vector, k.dve_step, nc.vector.tensor_tensor(part[:, 0:nn], bank, g, ALU.mult))
            return nc.vector.tensor_tensor(x[:, r, n0:n0 + nn], x[:, r, n0:n0 + nn], part[:, 0:nn], ALU.add)
        banks_phase(k, project_groups(k, lambda kt, r: h_t[:, kt, r * P:(r + 1) * P], DK, [P] * n_tiles, D, add,
                                      "dve"))


def swa_mla(k, t, x, h_t, gates, col, rope64, rope32):
    nc, sb = k.nc, k.sb
    with ExitStack() as mix:
        o = sb("ab_o", [P, T_ALL, D], where=mix)
        proj = sb("ab_proj", [P, T_ALL, 1184], where=mix)
        banks_phase(k, project_groups(
            k, lambda kt, r: h_t[:, kt, r * P:(r + 1) * P], DK, [P] * T_ALL, 1184,
            lambda who, r, n0, nn, bank: copy_by(k, who, proj[:, r, n0:n0 + nn], bank)))
        with ExitStack() as tmp:
            t1 = sb("rope_t1", [P, T_LAT, 672], where=tmp)
            roped = sb("rope_out", [P, T_LAT, 672], where=tmp)

            def steps(v):
                jobs = []
                for i in range(T_LAT):
                    heads = lambda a, d: a.rearrange("p (h d) -> p h d", d=d)
                    jobs.append((heads(proj[:, i, 0:640], 64), heads(roped[:, i, 0:640], 64),
                                 heads(t1[:, i, 0:640], 64), rope64[:, i, 0, :], rope64[:, i, 1, :], 10, 64))
                    jobs.append((heads(proj[:, i, 1152:1184], 32), heads(roped[:, i, 640:672], 32),
                                 heads(t1[:, i, 640:672], 32), rope32[:, i, 0, :], rope32[:, i, 1, :], 1, 32))
                yield from rope_steps(v, jobs)
                yield [v.tensor_copy(proj[:, 0:T_LAT, 0:640], roped[:, :, 0:640]),
                       v.tensor_copy(proj[:, 0:T_LAT, 1152:1184], roped[:, :, 640:672])]
            vector_phase(k, steps)
        with ExitStack() as tmp:
            q_t = sb("swa_q_t", [P, 4, 2 * S], where=tmp)
            k_t = sb("swa_k_t", [P, 2 * S], where=tmp)
            mask = sb("swa_mask", [P, T_LAT, 2 * S], where=tmp)
            sink = sb("sink", [P, 8], where=tmp)
            minus_sink = sb("minus_sink", [P, 8], where=tmp)
            pair = sb("swa_pair", [P, T_ALL, 4, 2, 64], where=tmp)
            load_phase(k, [(mask[:], t["swa_mask"].rearrange("(t p) k -> p t k", p=P)),
                           (sink[:], t["swa_sink"][0].partition_broadcast(P))])

            def steps(v):
                yield v.tensor_scalar(minus_sink[:], sink[:], -1.0, None, ALU.mult)
                for i in range(T_ALL):
                    yield v.tensor_copy(pair[:, i], proj[:, i, 0:512].rearrange("p (a b d) -> p b a d", a=2, d=64))
            vector_phase(k, steps)
            jobs = [([pair[:, i, b].rearrange("p a d -> p (a d)") for i in range(T_ALL)],
                     lambda who, bank, b=b: copy_by(k, who, q_t[:, b, :], bank)) for b in range(4)]
            jobs.append(([proj[:, i, 512:640] for i in range(T_ALL)],
                         lambda who, bank: copy_by(k, who, k_t[:], bank)))
            banks_phase(k, transpose_groups(k, jobs))
            units = {0: [], 1: []}
            for i in range(T_ALL):
                lat = i < T_LAT
                k0 = 0 if lat else S
                for h in range(8):
                    a, b = divmod(h, 4)
                    rows = slice(64 * a, 64 * a + 64)
                    units[0 if lat else 1].append(dict(
                        qk=[(q_t[rows, b, i * P:(i + 1) * P], k_t[rows, k0:2 * S])],
                        v=[proj[:, j, 640 + 64 * a:704 + 64 * a] for j in range(k0 // P, T_ALL)],
                        mask=mask[:, i, :] if lat else None, sink=sink[:, h:h + 1],
                        minus_sink=minus_sink[:, h:h + 1], out=o[:, i, 64 * h:64 * h + 64]))
            attention(k, "swa", units[0], 64 ** -0.5, 2 * S, 64)
            attention(k, "swac", units[1], 64 ** -0.5, S, 64)
        stop_at("swa")
        with ExitStack() as tmp:
            q_t = h_t[0:96, :, :]
            k_t = sb("mla_k_t", [96, 8, 2 * S], where=tmp)
            kv = sb("mla_kv", [P, T_ALL, 1024], where=tmp)
            with ExitStack() as tq:
                cq_t = sb("cq_t", [P, 2, 2 * S], where=tq)
                q = sb("mla_q", [P, T_ALL, 768], where=tq)
                norm_to_columns(k, "cq", [proj[:, i, 768:1024] for i in range(T_ALL)], 256, 1e-6, cq_t,
                                lambda kt: [(0, 2 * S, col("q_norm", kt), None)])
                banks_phase(k, project_groups(
                    k, lambda kt, r: cq_t[:, kt, r * P:(r + 1) * P], 2, [P] * T_ALL, 768,
                    lambda who, r, n0, nn, bank: copy_by(k, who, q[:, r, n0:n0 + nn], bank)))
                with ExitStack() as tr:
                    t1 = sb("mla_t1", [P, T_LAT, 8, 32], where=tr)
                    qr = sb("mla_qr", [P, T_LAT, 8, 32], where=tr)
                    rope_part = lambda i: q[:, i, :].rearrange("p (h d) -> p h d", d=96)[:, :, 64:96]

                    def steps(v):
                        yield from rope_steps(v, [(rope_part(i), qr[:, i], t1[:, i], rope32[:, i, 0, :],
                                                   rope32[:, i, 1, :], 8, 32) for i in range(T_LAT)])
                        yield [v.tensor_copy(rope_part(i), qr[:, i]) for i in range(T_LAT)]
                    vector_phase(k, steps)
                jobs = [([q[:, i, 96 * h:96 * h + 96] for i in range(T_ALL)],
                         lambda who, bank, h=h: copy_by(k, who, q_t[:, h, :], bank)) for h in range(8)]
                banks_phase(k, transpose_groups(k, jobs))
            with ExitStack() as tk:
                ckv_t = sb("ckv_t", [P, 1, 2 * S], where=tk)
                kcat = sb("mla_kcat", [P, T_ALL, 8, 96], where=tk)
                norm_to_columns(k, "ckv", [proj[:, i, 1024:1152] for i in range(T_ALL)], 128, 1e-6, ckv_t,
                                lambda kt: [(0, 2 * S, col("kv_norm"), None)])
                banks_phase(k, project_groups(
                    k, lambda kt, r: ckv_t[:, kt, r * P:(r + 1) * P], 1, [P] * T_ALL, 1024,
                    lambda who, r, n0, nn, bank: copy_by(k, who, kv[:, r, n0:n0 + nn], bank)))

                def steps(v):
                    yield [v.tensor_copy(kcat[:, i, :, 0:64],
                                         kv[:, i, :].rearrange("p (h d) -> p h d", d=128)[:, :, 0:64])
                           for i in range(T_ALL)] + [
                        v.tensor_copy(kcat[:, i, :, 64:96], proj[:, i, 1152:1184].unsqueeze(1).to_broadcast([P, 8, 32]))
                        for i in range(T_ALL)]
                vector_phase(k, steps)
                jobs = [([kcat[:, i, h, :] for i in range(T_ALL)],
                         lambda who, bank, h=h: copy_by(k, who, k_t[:, h, :], bank)) for h in range(8)]
                banks_phase(k, transpose_groups(k, jobs))
            units = {0: [], 1: []}
            for i in range(T_ALL):
                k0 = 0 if i < T_LAT else S
                for h in range(8):
                    units[min(1, k0)].append(dict(
                        qk=[(q_t[:, h, i * P:(i + 1) * P], k_t[:, h, k0:2 * S])],
                        v=[kv[:, j, 128 * h + 64:128 * h + 128] for j in range(k0 // P, T_ALL)],
                        mask=None, sink=None, out=o[:, i, 512 + 64 * h:576 + 64 * h]))
            attention(k, "mla", units[0], 96 ** -0.5, 2 * S, 64)
            attention(k, "mlac", units[1], 96 ** -0.5, S, 64)
        gated_residual(k, "ab", o, x, gates, 0, h_t, T_ALL)


def differential(k, t, x, h_t, gates, rope64):
    nc, sb = k.nc, k.sb
    lambda_init = 0.8 - 0.6 * math.exp(-0.3)
    with ExitStack() as mix:
        a1 = sb("diff_a1", [P, T_LAT, D], where=mix)
        a2 = sb("diff_a2", [P, T_LAT, D], where=mix)
        k_t = sb("diff_k_t", [P, 8, 2 * S], where=mix)
        q_t = sb("diff_q_t", [P, 8, S], where=mix)
        small = sb("diff_small", [P, 8], where=mix)
        vt = sb("diff_v", [P, T_ALL, D], where=mix)

        def roped_to_columns(tag, n_tiles, dst):
            with ExitStack() as tmp:
                z = sb(f"diff_{tag}", [P, n_tiles, D], where=tmp)
                t1 = sb(f"diff_t1{tag}", [P, T_LAT, D], where=tmp)
                heads = lambda a: a.rearrange("p (h d) -> p h d", d=64)
                banks_phase(k, project_groups(
                    k, lambda kt, r: h_t[:, kt, r * P:(r + 1) * P], DK, [P] * n_tiles, D,
                    lambda who, r, n0, nn, bank: copy_by(k, who, z[:, r, n0:n0 + nn], bank)))

                def steps(v):
                    products = []
                    for i in range(T_LAT):
                        x, o = heads(z[:, i, :]), heads(t1[:, i, :])
                        lo = rope64[:, i, 1, 0:32].unsqueeze(1).to_broadcast([P, 16, 32])
                        hi = rope64[:, i, 1, 32:64].unsqueeze(1).to_broadcast([P, 16, 32])
                        products += [v.tensor_tensor(o[:, :, 0:32], x[:, :, 32:64], lo, ALU.mult),
                                     v.tensor_tensor(o[:, :, 32:64], x[:, :, 0:32], hi, ALU.mult)]
                    yield products
                    yield [v.tensor_tensor(heads(z[:, i, :]), heads(z[:, i, :]),
                                           rope64[:, i, 0, :].unsqueeze(1).to_broadcast([P, 16, 64]), ALU.mult)
                           for i in range(T_LAT)]
                    yield v.tensor_tensor(z[:, 0:T_LAT, :], z[:, 0:T_LAT, :], t1[:], ALU.add)
                vector_phase(k, steps)
                jobs = [([z[:, i, j * P:(j + 1) * P] for i in range(n_tiles)],
                         lambda who, bank, j=j: copy_by(k, who, dst[:, j, :], bank)) for j in range(8)]
                banks_phase(k, transpose_groups(k, jobs))
        roped_to_columns("q", T_LAT, q_t)
        roped_to_columns("k", T_ALL, k_t)
        banks_phase(k, project_groups(
            k, lambda kt, r: h_t[:, kt, r * P:(r + 1) * P], DK, [P] * T_ALL, D,
            lambda who, r, n0, nn, bank: copy_by(k, who, vt[:, r, n0:n0 + nn], bank)))
        units = []
        for i in range(T_LAT):
            for j in range(8):
                for a, dst in enumerate((a1, a2)):
                    rows = slice(64 * a, 64 * a + 64)
                    units.append(dict(qk=[(q_t[rows, j, i * P:(i + 1) * P], k_t[rows, j, :])],
                                      v=[vt[:, m, j * P:(j + 1) * P] for m in range(T_ALL)],
                                      mask=None, sink=None, out=dst[:, i, j * P:(j + 1) * P]))
        attention(k, "diff", units, 64 ** -0.5, 2 * S, P)
        with ExitStack() as tmp:
            lqk = sb("lqk", [P, 4, 64], where=tmp)
            prod = sb("lqk_prod", [P, 64], where=tmp)
            subln = sb("subln", [P, P], where=tmp)
            ms = sb("diff_ms", [P, T_LAT * 8], where=tmp)
            load_phase(k, [(lqk[:, i, :], t["diff_lambda_" + n][0].partition_broadcast(P))
                           for i, n in enumerate(("q1", "k1", "q2", "k2"))]
                       + [(subln[:], t["diff_subln"][0].partition_broadcast(P))])

            def dots(v):
                for i in range(2):
                    yield v.tensor_tensor(prod[:], lqk[:, 2 * i, :], lqk[:, 2 * i + 1, :], ALU.mult)
                    yield v.reduce_sum(small[:, i:i + 1], prod[:], AX.X)
            vector_phase(k, dots)
            scalar_phase(k, lambda s: [s.activation(small[:, 2:4], small[:, 0:2], ACT.Exp)])
            whole = lambda a: a[:].rearrange("p t d -> p (t d)")
            per_head = lambda a: a[:].rearrange("p t (h d) -> p (t h) d", d=P)

            def combine(v):
                yield v.tensor_tensor(small[:, 4:5], small[:, 3:4], small[:, 2:3], ALU.subtract)
                yield v.tensor_scalar(small[:, 4:5], small[:, 4:5], -lambda_init, None, ALU.add)
                yield v.scalar_tensor_tensor(out=whole(a1), in0=whole(a2), scalar=small[:, 4:5], in1=whole(a1),
                                             op0=ALU.mult, op1=ALU.add)
                yield v.tensor_tensor(whole(a2), whole(a1), whole(a1), ALU.mult)
                yield v.tensor_reduce(ms[:], per_head(a2), AX.X, ALU.add)
                yield v.tensor_scalar(ms[:], ms[:], 1.0 / P, 1e-5, ALU.mult, ALU.add)
            vector_phase(k, combine)
            scalar_phase(k, lambda s: [s.activation(ms[:], ms[:], ACT.Sqrt)])

            def scaled(v):
                yield v.reciprocal(ms[:], ms[:])
                yield v.tensor_scalar(ms[:], ms[:], 1.0 - lambda_init, None, ALU.mult)
                yield v.tensor_tensor(per_head(a1), per_head(a1), ms[:].unsqueeze(2).to_broadcast([P, T_LAT * 8, P]),
                                      ALU.mult)
                yield v.tensor_tensor(per_head(a1), per_head(a1), subln[:].unsqueeze(1).to_broadcast([P, T_LAT * 8, P]),
                                      ALU.mult)
            vector_phase(k, scaled)
        gated_residual(k, "diff", a1, x, gates, 0, h_t, T_LAT)


def scalar_phase(k, steps):
    with k.nc.Block(no_gpsimd_drain=True) as block:
        @block.scalar
        def _(act):
            for ins in steps(k.nc.scalar):
                chain(act, k.act_step, ins)

        @block.sync
        def _(sp):
            k.pump(sp)


def route(k, t, l, h_t, n_tiles, descending, pick, weight):
    nc, sb = k.nc, k.sb
    n = n_tiles
    with ExitStack() as tmp:
        wr = sb(f"router_w{l}", [P, DK, 36], where=tmp)
        br = sb(f"router_b{l}", [P, 36], where=tmp)
        lg = sb(f"logits{l}", [P, n, 36], where=tmp)
        one = sb(f"r_one{l}", [P, n, 4], where=tmp)
        w4 = sb(f"r_w4{l}", [P, n, 4], where=tmp)
        ex = sb(f"r_ex{l}", [P, n, 4], where=tmp)
        r1 = sb(f"r_r1{l}", [P, n, 8], where=tmp)
        em = sb(f"r_em{l}", [P, n, 32], where=tmp)
        w32 = sb(f"r_w32{l}", [P, n, 32], where=tmp)
        load_phase(k, [(wr[:, :, 0:4], t["router_group_w"][l].rearrange("(j p) n -> p j n", p=P)),
                       (wr[:, :, 4:36], t["router_expert_w"][l].rearrange("(j p) n -> p j n", p=P)),
                       (br[:, 0:4], t["router_group_b"][l].partition_broadcast(P)),
                       (br[:, 4:36], t["router_expert_b"][l].partition_broadcast(P))])

        def fill(pe, banks):
            for i in range(n):
                for kt in range(DK):
                    mm = nc.tensor.matmul(banks[0][:, i * 36:(i + 1) * 36], h_t[:, kt, i * P:(i + 1) * P], wr[:, kt, :],
                                          start=(kt == 0), stop=(kt == DK - 1), skip_group_check=True)
            yield mm
        banks_phase(k, [(fill, [("dve", lambda bank: nc.vector.tensor_tensor(
            lg[:], bank[:, 0:n * 36].rearrange("p (i e) -> p i e", e=36), br[:].unsqueeze(1).to_broadcast([P, n, 36]),
            ALU.add))])])
        g, e = lg[:, :, 0:4], lg[:, :, 4:36]
        b4 = lambda a: a.to_broadcast([P, n, 4])
        b32 = lambda a: a.to_broadcast([P, n, 32])
        desc4, desc32 = descending[:, 28:32].unsqueeze(1), descending[:].unsqueeze(1)

        def first_max(v, out, vals, top, weight, desc, spread):
            yield v.tensor_reduce(top, vals, AX.X, ALU.max)
            yield v.tensor_tensor(weight, vals, spread(top), ALU.is_equal)
            yield v.tensor_tensor(weight, weight, spread(desc), ALU.mult)
            yield v.tensor_reduce(r1[:, :, 7:8], weight, AX.X, ALU.max)
            yield v.tensor_tensor(out, weight, spread(r1[:, :, 7:8]), ALU.is_equal)

        def choose(v):
            yield from first_max(v, one[:], g, r1[:, :, 0:1], w4[:], desc4, b4)
            yield v.tensor_tensor(ex[:], g, b4(r1[:, :, 0:1]), ALU.subtract)
            yield v.tensor_scalar(w4[:], one[:], -1.0, -NEG, ALU.add, ALU.mult)
            group = lambda a: a.unsqueeze(3).to_broadcast([P, n, 4, 8])
            em4 = em[:].rearrange("p i (g x) -> p i g x", g=4)
            for i in range(n):
                gi = lambda a: a[:, i, :].unsqueeze(2).to_broadcast([P, 4, 8])
                ei = em[:, i, :].rearrange("p (g x) -> p g x", g=4)
                yield v.tensor_tensor(ei, e[:, i, :].rearrange("p (g x) -> p g x", g=4), gi(one), ALU.mult)
                yield v.tensor_tensor(ei, ei, gi(w4), ALU.add)
            yield from first_max(v, pick[:, :, 0, :], em[:], r1[:, :, 1:2], w32[:], desc32, b32)
            yield v.scalar_tensor_tensor(out=em[:], in0=pick[:, :, 0, :], scalar=2 * NEG, in1=em[:], op0=ALU.mult,
                                         op1=ALU.add)
            yield from first_max(v, pick[:, :, 1, :], em[:], r1[:, :, 2:3], w32[:], desc32, b32)
            yield v.tensor_tensor(r1[:, :, 3:4], r1[:, :, 2:3], r1[:, :, 1:2], ALU.subtract)
        vector_phase(k, choose)
        scalar_phase(k, lambda s: [s.activation(ex[:], ex[:], ACT.Exp),
                                   s.activation(r1[:, :, 3:4], r1[:, :, 3:4], ACT.Exp)])

        def weigh(v):
            yield v.tensor_reduce(r1[:, :, 4:5], ex[:], AX.X, ALU.add)
            yield v.tensor_scalar(r1[:, :, 5:6], r1[:, :, 3:4], 1.0, None, ALU.add)
            yield v.tensor_tensor(r1[:, :, 4:5], r1[:, :, 4:5], r1[:, :, 5:6], ALU.mult)
            yield v.reciprocal(r1[:, :, 4:5], r1[:, :, 4:5])
            yield v.tensor_copy(weight[:, :, 0:1], r1[:, :, 4:5])
            yield v.tensor_tensor(weight[:, :, 1:2], r1[:, :, 4:5], r1[:, :, 3:4], ALU.mult)
        vector_phase(k, weigh)


def place_tokens(k, t, l, n_tiles, pick, table_at, row_at, control, n_blocks):
    nc, sb = k.nc, k.sb
    n, more = n_tiles, n_blocks - 32
    with ExitStack() as tmp:
        before = sb(f"before{l}", [P, P], where=tmp)
        ones = sb(f"p_ones{l}", [P, P], where=tmp)
        number = sb(f"number{l}", [P, 32], where=tmp)
        chosen = sb(f"chosen{l}", [P, n, 32], where=tmp)
        rank = sb(f"rank{l}", [P, n, 32], where=tmp)
        blk = sb(f"blk{l}", [P, n, 32], where=tmp)
        away = sb(f"away{l}", [P, n, 32], where=tmp)
        extra = sb(f"extra{l}", [P, 32], where=tmp)
        extra_end = sb(f"extra_end{l}", [P, 32], where=tmp)
        ends = sb(f"ends{l}", [P, more, 32], where=tmp)
        ctl = sb(f"ctl{l}", [P, 16], where=tmp)
        at_f = sb(f"at_f{l}", [P, 2, n, 2], where=tmp)
        load_phase(k, [(before[:], t["before"]), (number[:], t["expert_number"])])

        def choose(v):
            yield v.memset(ones[:], 1.0)
            yield v.tensor_tensor(chosen[:], pick[:, :, 0, :], pick[:, :, 1, :], ALU.add)
        vector_phase(k, choose)

        def count(pe, banks):
            for i in range(n):
                for j in range(i + 1):
                    nc.tensor.matmul(banks[0][:, i * 32:i * 32 + 32], (before if j == i else ones)[:], chosen[:, j, :],
                                     start=(j == 0), stop=(j == i), skip_group_check=True)
            for j in range(n):
                mm = nc.tensor.matmul(banks[1][:, 0:32], ones[:], chosen[:, j, :], start=(j == 0), stop=(j == n - 1))
            yield mm

        banks_phase(k, [(count, [
            ("dve", lambda bank: nc.vector.tensor_copy(rank[:].rearrange("p i e -> p (i e)"), bank[:, 0:n * 32])),
            ("dve", lambda bank: nc.vector.tensor_scalar(extra[:], bank[:, 0:32], -(SLOT + 1) / 2, 1.0 / SLOT,
                                                         ALU.add, ALU.mult))])])
        magic = 12582912.0

        def place(v):
            yield v.tensor_scalar(extra[:], extra[:], magic, None, ALU.add)
            yield v.tensor_scalar(extra[:], extra[:], -magic, 0.0, ALU.add, ALU.max)
            yield v.tensor_tensor_scan(extra_end[:], ones[:, 0:32], extra[:], 0.0, ALU.mult, ALU.add)
            yield v.tensor_scalar(blk[:], rank[:], -(SLOT - 1) / 2, 1.0 / SLOT, ALU.add, ALU.mult)
            yield v.tensor_scalar(blk[:], blk[:], magic, None, ALU.add)
            yield v.tensor_scalar(blk[:], blk[:], -magic, None, ALU.add)
            yield v.scalar_tensor_tensor(out=rank[:], in0=blk[:], scalar=-float(SLOT), in1=rank[:], op0=ALU.mult,
                                         op1=ALU.add)
            yield v.tensor_tensor(extra[:], extra_end[:], extra[:], ALU.subtract)
            yield v.tensor_scalar(extra[:], extra[:], 31.0, None, ALU.add)
            yield v.tensor_tensor(extra[:], extra[:], number[:], ALU.subtract)
            yield v.tensor_tensor(away[:], blk[:], extra[:].unsqueeze(1).to_broadcast([P, n, 32]), ALU.add)
            yield v.tensor_scalar(blk[:], blk[:], 0.5, None, ALU.is_ge)
            yield v.tensor_tensor(blk[:], blk[:], away[:], ALU.mult)
            yield v.tensor_tensor(blk[:], blk[:], number[:].unsqueeze(1).to_broadcast([P, n, 32]), ALU.add)
            yield v.scalar_tensor_tensor(out=away[:], in0=blk[:], scalar=float(SLOT), in1=rank[:], op0=ALU.mult,
                                         op1=ALU.add)
            yield v.scalar_tensor_tensor(out=rank[:], in0=rank[:], scalar=float(n_blocks), in1=blk[:], op0=ALU.mult,
                                         op1=ALU.add)
            for c in range(2):
                for which, value in enumerate((rank, away)):
                    yield v.tensor_tensor(chosen[:], pick[:, :, c, :], value[:], ALU.mult)
                    yield v.tensor_reduce(at_f[:, which, :, c], chosen[:], AX.X, ALU.add)
            yield v.tensor_copy(table_at[:], at_f[:, 0])
            yield v.tensor_copy(row_at[:], at_f[:, 1])
            yield v.memset(ctl[:], 0.0)
            yield v.tensor_tensor(ends[:], extra_end[:].unsqueeze(1).to_broadcast([P, more, 32]),
                                  number[:, 0:more].unsqueeze(2).to_broadcast([P, more, 32]), ALU.is_le)
            yield v.tensor_reduce(ctl[:, 1:1 + more], ends[:], AX.X, ALU.add)
            yield v.tensor_scalar(ctl[:, 1:1 + more], ctl[:, 1:1 + more], 31.0, None, ALU.min)
            yield v.tensor_copy(ctl[:, 0:1], extra_end[:, 31:32])
            yield v.tensor_copy(control[:], ctl[0:1, :])
        vector_phase(k, place)


def experts(k, t, l, x, h_t, gates, n_tiles, descending):
    nc, sb = k.nc, k.sb
    n_tok = n_tiles * P
    more = 2 * n_tok // (SLOT + 1)
    n_blocks = 32 + more
    h_rows = nc.dram_tensor(f"h_rows{l}", (n_tok, D), F32).ap()
    table = nc.dram_tensor(f"slot_table{l}", (SLOT * n_blocks, 1), U32).ap()
    y_rows = nc.dram_tensor(f"y_rows{l}", (SLOT * n_blocks, D), F32).ap()
    row_of = lambda ap: bass.IndirectOffsetOnAxis(ap=ap, axis=0)
    with ExitStack() as moe:
        pick = sb(f"pick{l}", [P, n_tiles, 2, 32], where=moe)
        weight = sb(f"weight{l}", [P, n_tiles, 2], where=moe)
        table_at = sb(f"table_at{l}", [P, n_tiles, 2], U32, where=moe)
        row_at = sb(f"row_at{l}", [P, n_tiles, 2], U32, where=moe)
        control = sb(f"control{l}", [1, 16], I32, where=moe)
        slots = sb(f"slots{l}", [SLOT, n_blocks], U32, where=moe)
        with ExitStack() as tmp:
            rows = sb(f"h_row_tiles{l}", [P, n_tiles, D], where=tmp)
            groups = transpose_groups(k, [
                ([h_t[:, kt, i * P:(i + 1) * P] for kt in range(4 * half, 4 * half + 4)],
                 lambda who, bank, i=i, half=half: copy_by(k, who, rows[:, i, half * BANK:(half + 1) * BANK], bank))
                for i in range(n_tiles) for half in range(2)])
            banks_phase(k, groups)
            with nc.Block(no_gpsimd_drain=True) as block:
                @block.scalar
                def _(act):
                    k.store_done.mark(act.dma_start(h_rows.rearrange("(t p) d -> p t d", p=P), rows[:]), 16)

                @block.sync
                def _(sp):
                    k.pump(sp)
            route(k, t, l, h_t, n_tiles, descending, pick, weight)
            place_tokens(k, t, l, n_tiles, pick, table_at, row_at, control, n_blocks)
            token = sb(f"token{l}", [P, n_tiles], U32, where=tmp)
            zeros = sb(f"slot_zeros{l}", [SLOT, n_blocks], U32, where=tmp)
            zero_row = sb(f"zero_row{l}", [SLOT, D], where=tmp)
            with nc.Block(no_gpsimd_drain=True) as block:
                @block.vector
                def _(dve):
                    chain(dve, k.dve_step, nc.vector.memset(zero_row[:], 0.0))

                @block.scalar
                def _(act):
                    act.wait_ge(k.dve_step.sem, k.dve_step.n)
                    k.store_done.mark(act.dma_start(y_rows[32 * SLOT:, :].rearrange("(b r) d -> r b d", r=SLOT),
                                                    zero_row[:].unsqueeze(1).to_broadcast([SLOT, more, D])), 16)

                @block.gpsimd
                def _(pool):
                    chain(pool, k.pool_step, nc.gpsimd.iota(token[:], [[P, n_tiles]], base=0, channel_multiplier=1))
                    chain(pool, k.pool_step, nc.gpsimd.memset(zeros[:], 0))
                    k.soft_done.mark(pool.dma_start(table.rearrange("(r b) o -> r (b o)", r=SLOT), zeros[:]), 16)
                    pool.wait_ge(k.soft_done.sem, k.soft_done.n)
                    for i in range(n_tiles):
                        for c in range(2):
                            k.soft_done.mark(nc.gpsimd.indirect_dma_start(table, row_of(table_at[:, i, c:c + 1]),
                                                                          token[:, i:i + 1], None), 16)
                    pool.wait_ge(k.soft_done.sem, k.soft_done.n)
                    k.soft_done.mark(pool.dma_start(slots[:], table.rearrange("(r b) o -> r (b o)", r=SLOT)), 16)
                    pool.wait_ge(k.soft_done.sem, k.soft_done.n)
                    pool.wait_ge(k.store_done.sem, k.store_done.n)

                @block.sync
                def _(sp):
                    k.pump(sp)
        stop_at(f"route{l}")
        with ExitStack() as tmp:
            first_blocks(k, l, tmp, h_rows, y_rows, slots, row_of)
        stop_at(f"first{l}")
        with ExitStack() as tmp:
            further_blocks(k, t, l, tmp, more, h_rows, y_rows, slots, control, row_of)
        with ExitStack() as tmp:
            got = sb(f"y_got{l}", [P, 4, D], where=tmp)
            turns_ = [(i, c) for i in range(n_tiles) for c in range(2)]
            used_at = []
            with nc.Block(no_gpsimd_drain=True) as block:
                @block.vector
                def _(dve):
                    v = nc.vector
                    for m, (i, c) in enumerate(turns_):
                        g = got[:, m % 4, :]
                        dve.wait_ge(k.gathered[m % 4].sem, k.gathered[m % 4].n + 16 * (m // 4 + 1))
                        if c == 0:
                            chain(dve, k.dve_step, v.tensor_scalar(g, g, weight[:, i, 0:1], None, ALU.mult))
                            used_at.append(None)
                            continue
                        f = got[:, (m - 1) % 4, :]
                        chain(dve, k.dve_step, v.scalar_tensor_tensor(out=g, in0=g, scalar=weight[:, i, 1:2], in1=f,
                                                                      op0=ALU.mult, op1=ALU.add))
                        used_at[m - 1] = k.dve_step.n
                        chain(dve, k.dve_step, v.tensor_tensor(g, g, gates[:, 0 if i < T_LAT else 1, 1, :], ALU.mult))
                        chain(dve, k.dve_step, v.tensor_tensor(x[:, i, :], x[:, i, :], g, ALU.add))
                        used_at.append(k.dve_step.n)

                @block.gpsimd
                def _(pool):
                    for m, (i, c) in enumerate(turns_):
                        if m >= 4:
                            pool.wait_ge(k.dve_step.sem, used_at[m - 4])
                        k.gathered[m % 4].mark(nc.gpsimd.indirect_dma_start(got[:, m % 4, :], None, y_rows,
                                                                            row_of(row_at[:, i, c:c + 1])), 16)

                @block.sync
                def _(sp):
                    k.pump(sp)


def first_blocks(k, l, tmp, h_rows, y_rows, slots, row_of):
    nc, sb = k.nc, k.sb
    xg = sb(f"x_gathered{l}", [SLOT, 3, D], where=tmp)
    xt = sb(f"x_slots_t{l}", [P, 2, DK, SLOT], where=tmp)
    silu = sb(f"silu{l}", [P, 256], where=tmp)
    hid = sb(f"hid{l}", [P, 256], where=tmp)
    hid_t = sb(f"hid_t{l}", [P, 2, P], where=tmp)
    y_sb = sb(f"y_sb{l}", [P, 2, BANK], where=tmp)
    gathered0 = [g.n for g in k.gathered]
    stored0 = [s.n for s in k.stored]
    turned_at, silu_at, y_at = {}, {}, {}
    groups = []

    def store(act, e):
        act.wait_ge(k.act_evac.sem, y_at[e])
        for half in range(2):
            k.stored[e % 2].mark(act.dma_start(y_rows[e * SLOT:(e + 1) * SLOT, half * BANK:(half + 1) * BANK],
                                               y_sb[64 * half:64 * half + SLOT, e % 2, :]), 16)

    def turn_x(e):
        def fill(pe, banks):
            pe.wait_ge(k.gathered[e % 3].sem, gathered0[e % 3] + 16 * (e // 3 + 1))
            for kt in range(DK):
                mm = nc.tensor.transpose(banks[0][:, kt * SLOT:(kt + 1) * SLOT], xg[:, e % 3, kt * P:(kt + 1) * P],
                                         k.ident[0:SLOT, 0:SLOT])
            turned_at[e] = k.tensor_done.n + 1
            yield mm
        return (fill, [("dve", lambda bank: nc.vector.tensor_copy(
            xt[:, e % 2].rearrange("p k s -> p (k s)"), bank))])

    def up(e, empty, who):
        def fill(pe, banks):
            for k0 in range(0, DK, 4):
                w = k.take(pe, 4, BANK)
                mm = hidden(nc, banks[0], xt[:, e % 2], w, k0)
                yield mm
                k.used(k.tensor_done.n)
        return (fill, [(who, empty)], True)

    def silu_out(e):
        def empty(bank):
            if e >= 1:
                store(nc.scalar, e - 1)
            silu_at[e] = k.act_evac.n + 1
            return nc.scalar.activation(silu[:], bank[:, 0:256], ACT.Silu)
        return empty

    def hid_out(e):
        def empty(bank):
            nc.vector.wait_ge(k.act_evac.sem, silu_at[e])
            return nc.vector.tensor_tensor(hid[:], silu[:], bank[:, 0:256], ALU.mult)
        return empty

    def turn_hid(e):
        def fill(pe, banks):
            for b in range(2):
                mm = nc.tensor.transpose(banks[0][:, b * P:(b + 1) * P], hid[:, b * P:(b + 1) * P], k.ident[:])
            yield mm
        return (fill, [("dve", lambda bank: nc.vector.tensor_copy(hid_t[:].rearrange("p b s -> p (b s)"),
                                                                  bank[:, 0:256]))], True)

    def down(e):
        def fill(pe, banks):
            w = [k.take(pe, 4, BANK), k.take(pe, 4, BANK)]
            yield outward(nc, banks[0], hid_t, w)
            k.used(k.tensor_done.n)
            k.used(k.tensor_done.n)

        def empty(bank):
            if e >= 2:
                nc.scalar.wait_ge(k.stored[e % 2].sem, stored0[e % 2] + 32 * (e // 2))
            y_at[e] = k.act_evac.n + 1
            return nc.scalar.copy(y_sb[:, e % 2, :], bank)
        return (fill, [("act", empty)], True)

    groups.append(turn_x(0))
    for e in range(32):
        if e + 1 < 32:
            groups.append(turn_x(e + 1))
        groups += [up(e, silu_out(e), "act"), up(e, hid_out(e), "dve"), turn_hid(e), down(e)]

    def gathers(pool):
        for e in range(32):
            if e >= 3:
                pool.wait_ge(k.tensor_done.sem, turned_at[e - 3])
            k.gathered[e % 3].mark(nc.gpsimd.indirect_dma_start(xg[:, e % 3, :], None, h_rows,
                                                                row_of(slots[:, e:e + 1])), 16)

    def last(act):
        store(act, 31)
        for s in k.stored:
            act.wait_ge(s.sem, s.n)
    banks_phase(k, groups, gathers, last)


def hidden(nc, bank, xt, w, k0):
    for j in range(4):
        for half in range(2):
            mm = nc.tensor.matmul(bank[64 * half:64 * half + SLOT, 0:256], xt[:, k0 + j, :],
                                  w[:, j, 256 * half:256 * half + 256], start=(k0 + j == 0), stop=(k0 + j == DK - 1))
    return mm


def outward(nc, bank, hid_t, w):
    for j in range(4):
        for half in range(2):
            mm = nc.tensor.matmul(bank[64 * half:64 * half + SLOT, :], hid_t[:, j % 2, 64 * (j // 2):64 * (j // 2) + SLOT],
                                  w[half][:, j, :], start=(j == 0), stop=(j == 3))
    return mm


def further_blocks(k, t, l, tmp, more, h_rows, y_rows, slots, control, row_of):
    nc, sb = k.nc, k.sb
    sem = lambda name: k.ctx.enter_context(nc.semaphore(f"further_{name}{l}"))
    weights_in, x_in, pe_done, dve_done, act_done, y_out = (sem(s) for s in ("weights", "x", "pe", "dve", "act", "y"))
    w = [sb(f"fw{l}_{i}", [P, 4, BANK], where=tmp) for i in range(6)]
    xg = sb(f"fx{l}", [SLOT, D], where=tmp)
    xt = sb(f"fxt{l}", [P, DK, SLOT], where=tmp)
    silu = sb(f"fsilu{l}", [P, 256], where=tmp)
    hid = sb(f"fhid{l}", [P, 256], where=tmp)
    hid_t = sb(f"fhid_t{l}", [P, 2, P], where=tmp)
    y_sb = sb(f"fy{l}", [P, BANK], where=tmp)
    w1, w3, w2 = (t[n][l] for n in ("expert_w1", "expert_w3", "expert_w2"))
    half_rows = lambda a, k0: a[:, k0 * P:(k0 + 4) * P, :].rearrange("e (j p) n -> p (e j) n", p=P)
    bank = lambda b: k.psum[:, b, :]
    with nc.Block(no_gpsimd_drain=True) as block:
        @block.sync
        def _(sp):
            n = sp.value_load(control[0:1, 0:1], min_val=0, max_val=more)
            for j in range(more):
                with sp.If(n > j):
                    e = bass.ds(sp.value_load(control[0:1, 1 + j:2 + j], min_val=0, max_val=31), 1)
                    if j >= 1:
                        sp.wait_ge(pe_done, 5 * j)
                    for slot, src in zip(w, (half_rows(w1[e], 0), half_rows(w1[e], 4), half_rows(w3[e], 0),
                                             half_rows(w3[e], 4), half_rows(w2[e], 0)[:, :, 0:BANK],
                                             half_rows(w2[e], 0)[:, :, BANK:D])):
                        sp.dma_start(slot[:], src).then_inc(weights_in, 16)

        @block.gpsimd
        def _(pool):
            n = pool.value_load(control[0:1, 0:1], min_val=0, max_val=more)
            for j in range(more):
                with pool.If(n > j):
                    if j >= 1:
                        pool.wait_ge(pe_done, 5 * (j - 1) + 1)
                    nc.gpsimd.indirect_dma_start(xg[:], None, h_rows, row_of(slots[:, 32 + j:33 + j])).then_inc(x_in, 16)

        @block.tensor
        def _(pe):
            n = pe.value_load(control[0:1, 0:1], min_val=0, max_val=more)
            for j in range(more):
                with pe.If(n > j):
                    pe.wait_ge(x_in, 16 * (j + 1))
                    for kt in range(DK):
                        mm = nc.tensor.transpose(bank(0)[:, kt * SLOT:(kt + 1) * SLOT], xg[:, kt * P:(kt + 1) * P],
                                                 k.ident[0:SLOT, 0:SLOT])
                    mm.then_inc(pe_done, 1)
                    pe.wait_ge(weights_in, 96 * (j + 1))
                    pe.wait_ge(dve_done, 3 * j + 1)
                    for b in range(2):
                        for half in range(2):
                            mm = hidden(nc, bank(1 + b), xt, w[2 * b + half], 4 * half)
                        mm.then_inc(pe_done, 1)
                    pe.wait_ge(dve_done, 3 * j + 2)
                    for b in range(2):
                        mm = nc.tensor.transpose(bank(3)[:, b * P:(b + 1) * P], hid[:, b * P:(b + 1) * P], k.ident[:])
                    mm.then_inc(pe_done, 1)
                    pe.wait_ge(dve_done, 3 * j + 3)
                    outward(nc, bank(4), hid_t, w[4:6]).then_inc(pe_done, 1)

        @block.vector
        def _(dve):
            n = dve.value_load(control[0:1, 0:1], min_val=0, max_val=more)
            for j in range(more):
                with dve.If(n > j):
                    dve.wait_ge(pe_done, 5 * j + 1)
                    nc.vector.tensor_copy(xt[:].rearrange("p k s -> p (k s)"), bank(0)).then_inc(dve_done, 1)
                    dve.wait_ge(pe_done, 5 * j + 3)
                    dve.wait_ge(act_done, 2 * j + 1)
                    nc.vector.tensor_tensor(hid[:], silu[:], bank(2)[:, 0:256], ALU.mult).then_inc(dve_done, 1)
                    dve.wait_ge(pe_done, 5 * j + 4)
                    nc.vector.tensor_copy(hid_t[:].rearrange("p b s -> p (b s)"), bank(3)[:, 0:256]).then_inc(dve_done, 1)

        @block.scalar
        def _(act):
            n = act.value_load(control[0:1, 0:1], min_val=0, max_val=more)
            for j in range(more):
                with act.If(n > j):
                    act.wait_ge(pe_done, 5 * j + 2)
                    nc.scalar.activation(silu[:], bank(1)[:, 0:256], ACT.Silu).then_inc(act_done, 1)
                    act.wait_ge(pe_done, 5 * j + 5)
                    nc.scalar.copy(y_sb[:], bank(4)).then_inc(act_done, 1)
                    act.wait_ge(act_done, 2 * j + 2)
                    for half in range(2):
                        act.dma_start(y_rows[(32 + j) * SLOT:(33 + j) * SLOT, half * BANK:(half + 1) * BANK],
                                      y_sb[64 * half:64 * half + SLOT, :]).then_inc(y_out, 16)
                    act.wait_ge(y_out, 32 * (j + 1))


def second_block(k, t, x, h_t, col, out):
    nc, sb = k.nc, k.sb
    with ExitStack() as mix:
        br_t = sb("branches_t", [P, 3, 4, S], where=mix)
        norm_to_columns(k, "pre_mix", [x[:, i, :] for i in range(T_LAT)], D, 1e-6, h_t,
                        lambda kt: [(0, S, col("pre_mix", kt), None)])
        gla_branch(k, t, h_t, col, br_t)
        stop_at("gla")
        conv_branch(k, t, h_t, col, br_t)
        stop_at("sc")
        dilated_branch(k, t, h_t, br_t)
        stop_at("dil")
        with ExitStack() as tmp:
            open_ = sb("branch_gates", [P, 24, S], where=tmp)
            merged = sb("merged_t", [P, DK, S], where=tmp)
            part = sb("merge_part", [P, S], where=tmp)
            tok = lambda kt: h_t[:, kt, 0:S]
            banks_phase(k, project_column_groups(
                k, tok, DK, S, 3 * D,
                lambda who, b, h, bank: nc.scalar.activation(open_[:, b, :], bank, ACT.Sigmoid, bias=col("b_gate", b)),
                "act"))
            groups = []
            for g in range(3):
                def merge(who, b, h, bank, g=g):
                    if g == 0:
                        return nc.vector.tensor_tensor(merged[:, b, :], bank, open_[:, b, :], ALU.mult)
                    nc.vector.wait_ge(k.dve_evac.sem, k.dve_evac.n)
                    chain(nc.vector, k.dve_step, nc.vector.tensor_tensor(part[:], bank, open_[:, 8 * g + b, :],
                                                                         ALU.mult))
                    return nc.vector.tensor_tensor(merged[:, b, :], merged[:, b, :], part[:], ALU.add)
                groups += project_column_groups(k, lambda kt, g=g: br_t[:, g, kt, :], 4, S, D, merge, "dve")
            banks_phase(k, groups)
            normed_residual(k, t, "post_mix_g_2", x, lambda kt, r: merged[:, kt, r * P:(r + 1) * P], DK)
    stop_at("mix2")
    with ExitStack() as ffn:
        hid = sb("ff_hid", [P, 22, S], where=ffn)
        norm_to_columns(k, "pre_ffn", [x[:, i, :] for i in range(T_LAT)], D, 1e-6, h_t,
                        lambda kt: [(0, S, col("pre_ffn", kt), None)])
        tok = lambda kt: h_t[:, kt, 0:S]

        def conv(who, b, h, bank):
            v, o = nc.vector, hid[:, b, :]
            chain(v, k.dve_step, v.tensor_scalar(o, bank, col("ffw2", b), col("ff_b", b), ALU.mult, ALU.add))
            chain(v, k.dve_step, v.scalar_tensor_tensor(out=o[:, 1:S], in0=bank[:, 0:S - 1], scalar=col("ffw1", b),
                                                        in1=o[:, 1:S], op0=ALU.mult, op1=ALU.add))
            return v.scalar_tensor_tensor(out=o[:, 2:S], in0=bank[:, 0:S - 2], scalar=col("ffw0", b), in1=o[:, 2:S],
                                          op0=ALU.mult, op1=ALU.add)
        banks_phase(k, project_column_groups(k, tok, DK, S, 2816, conv, "dve"))
        scalar_phase(k, lambda s: [s.activation(hid[:, b:b + 2, :], hid[:, b:b + 2, :], ACT.Gelu_apprx_tanh)
                                   for b in range(0, 22, 2)])
        banks_phase(k, project_column_groups(
            k, tok, DK, S, 2816, lambda who, b, h, bank: nc.vector.tensor_tensor(hid[:, b, :], hid[:, b, :], bank,
                                                                                 ALU.mult), "dve"))
        normed_residual(k, t, "post_ffn_g_2", x, lambda kt, r: hid[:, kt, r * P:(r + 1) * P], 22)
    with nc.Block(no_gpsimd_drain=True) as block:
        @block.sync
        def _(sp):
            k.store_done.mark(sp.dma_start(out[0].rearrange("(t p) d -> p t d", p=P), x[:, 0:T_LAT, :]), 16)
            sp.wait_ge(k.store_done.sem, k.store_done.n)


def normed_residual(k, t, gain, x, lhs, k_tiles):
    nc, sb = k.nc, k.sb
    with ExitStack() as tmp:
        y = sb(f"y_{gain}", [P, T_LAT, D], where=tmp)
        g = sb(f"g_{gain}", [P, D], where=tmp)
        rs = sb(f"rs_{gain}", [P, T_LAT], where=tmp)
        junk = sb(f"junk_{gain}", [P, 2, D], where=tmp)
        load_phase(k, [(g[:], t[gain][0].partition_broadcast(P))])
        banks_phase(k, project_groups(k, lhs, k_tiles, [P] * T_LAT, D,
                                      lambda who, r, n0, nn, bank: copy_by(k, who, y[:, r, n0:n0 + nn], bank)))
        inv_rms(k, [y[:, i, :] for i in range(T_LAT)], D, 1e-6, rs, [junk[:, 0, :], junk[:, 1, :]])

        def steps(v):
            for i in range(T_LAT):
                yield v.scalar_tensor_tensor(out=y[:, i, :], in0=y[:, i, :], scalar=rs[:, i:i + 1], in1=g[:],
                                             op0=ALU.mult, op1=ALU.mult)
                yield v.tensor_tensor(x[:, i, :], x[:, i, :], y[:, i, :], ALU.add)
        vector_phase(k, steps)


def columns_of(k, h_t, n_cols, dst):
    return project_column_groups(k, lambda kt: h_t[:, kt, 0:S], DK, S, n_cols,
                                 lambda who, b, h, bank: copy_by(k, who, dst(b, h), bank))


def gla_branch(k, t, h_t, col, br_t):
    nc, sb = k.nc, k.sb
    C, N = 16, S // 16
    with ExitStack() as gla:
        keep = lambda name, shape: sb("gla_" + name, shape, where=gla)
        qk = keep("qk", [P, 4, S])
        v_row = keep("v", [P, T_LAT, 512])
        g_t = keep("g", [P, 4, S])
        a_t = keep("a", [16, S])
        lc = keep("lc", [P, 2, S])
        lag_is = keep("lag_is", [P, 16, 16])
        chunk_is = keep("chunk_is", [P, 8])
        head_is = keep("head_is", [P, 2])
        dec = keep("dec", [P, 2, N])
        states = keep("states", [P, 2, N, P])
        q_in = keep("q_in", [P, 2, S])
        ones = keep("ones", [P, P])
        s_t = keep("s_t", [P, T_LAT, 4, P])
        four = lambda a: a.rearrange("p b (n c) -> p b n c", c=C)
        with ExitStack() as tmp:
            keep2 = lambda name, shape: sb("gla_" + name, shape, where=tmp)
            w_a = keep2("w_a", [16, S])
            z, u, r = keep2("z", [P, 2, S]), keep2("u", [P, 2, S]), keep2("r", [P, S])
            k_in = keep2("k_in", [P, 2, S])
            load_phase(k, [(w_a[:], t["w_alpha_up_2"][0]), (lag_is[:], t["lag_is"]), (chunk_is[:], t["chunk_is"]),
                           (head_is[:], t["head_is"]), (r[:], t["within_chunk"])])
            groups = columns_of(k, h_t, 512, lambda b, h: qk[:, b, :])
            groups += project_groups(k, lambda kt, i: h_t[:, kt, i * P:(i + 1) * P], DK, [P] * T_LAT, 512,
                                     lambda who, i, n0, nn, bank: copy_by(k, who, v_row[:, i, :], bank))
            groups += columns_of(k, h_t, 528, lambda b, h: g_t[:, b, :] if b < 4 else a_t[:])
            banks_phase(k, groups)

            def alpha(pe, banks):
                for p in range(2):
                    mm = nc.tensor.matmul(banks[0][:, p * S:(p + 1) * S], w_a[:, p * P:(p + 1) * P], a_t[:],
                                          start=True, stop=True, skip_group_check=True)
                yield mm

            def add_b(bank):
                for p in range(2):
                    ins = nc.vector.tensor_scalar(z[:, p, :], bank[:, p * S:(p + 1) * S], col("b_alpha", p), None,
                                                  ALU.add)
                return ins
            banks_phase(k, [(alpha, [("dve", add_b)])])

            def soft(s):
                yield s.activation(u[:], z[:], ACT.Abs)
                yield s.activation(u[:], u[:], ACT.Exp, scale=-1.0)
                yield s.activation(u[:], u[:], ACT.Ln, bias=1.0)
            scalar_phase(k, soft)

            def sums(v):
                yield [v.memset(ones[:], 1.0), v.tensor_scalar(z[:], z[:], 0.0, None, ALU.min)]
                yield v.tensor_tensor(z[:], z[:], u[:], ALU.subtract)
                yield v.tensor_scalar(z[:], z[:], 1.0 / 16.0, None, ALU.mult)
                yield [v.tensor_tensor_scan(lc[:, p, :], r[:], z[:, p, :], 0.0, ALU.mult, ALU.add)
                       for p in range(2)] + [
                    v.tensor_scalar(qk[:, 0:2, :], qk[:, 0:2, :], 64 ** -0.5, None, ALU.mult)]
                yield v.tensor_tensor(four(z[:]), four(lc[:])[:, :, :, C - 1:C].to_broadcast([P, 2, N, C]),
                                      four(lc[:]), ALU.subtract)
            vector_phase(k, sums)

            def exps(s):
                yield [s.activation(z[:], z[:], ACT.Exp), s.activation(u[:], lc[:], ACT.Exp),
                       s.activation(dec[:].unsqueeze(3), four(lc[:])[:, :, :, C - 1:C], ACT.Exp)]
            scalar_phase(k, exps)

            def ins_(v):
                yield [v.tensor_tensor(k_in[:], qk[:, 2:4, :], z[:], ALU.mult),
                       v.tensor_tensor(q_in[:], qk[:, 0:2, :], u[:], ALU.mult),
                       v.memset(states[:, :, 0, :], 0.0)]
            vector_phase(k, ins_)
            k_row = keep2("k_row", [P, T_LAT, 2, P])
            k_pick = keep2("k_pick", [P, T_LAT, 2, 8, P])
            banks_phase(k, transpose_groups(k, [
                ([k_in[:, p, i * P:(i + 1) * P] for p in range(2)],
                 lambda who, bank, i=i: copy_by(k, who, k_row[:, i].rearrange("p b d -> p (b d)"), bank))
                for i in range(T_LAT)]))

            def pick(v):
                yield [v.tensor_tensor(k_pick[:, i, p], k_row[:, i, p, :].unsqueeze(1).to_broadcast([P, 8, P]),
                                       chunk_is[:].unsqueeze(2).to_broadcast([P, 8, P]), ALU.mult)
                       for i in range(T_LAT) for p in range(2)]
            vector_phase(k, pick)
            groups = []
            for p in range(2):
                for n in range(N - 1):
                    def fill(pe, banks, p=p, n=n):
                        i, c = divmod(n, 8)
                        yield nc.tensor.matmul(banks[0][:, 0:256], k_pick[:, i, p, c, :],
                                               v_row[:, i, 256 * p:256 * p + 256], start=True, stop=True)

                    def empty(bank, p=p, n=n, who=("act", "dve")[n % 2]):
                        copy_by(k, who, states[0:64, p, n + 1, :], bank[0:64, 0:P])
                        return copy_by(k, who, states[64:P, p, n + 1, :], bank[64:P, P:2 * P])
                    groups.append((fill, [(("act", "dve")[n % 2], empty)]))
            banks_phase(k, groups)

            def recur(v):
                for n in range(1, N - 1):
                    yield [v.scalar_tensor_tensor(out=states[:, p, n + 1, :], in0=states[:, p, n, :],
                                                  scalar=dec[:, p, n:n + 1], in1=states[:, p, n + 1, :],
                                                  op0=ALU.mult, op1=ALU.add) for p in range(2)]
            vector_phase(k, recur)
        with ExitStack() as tmp:
            w = sb("gla_w", [P, C, 2, S], where=tmp)
            s_lag = sb("gla_s_lag", [P, T_LAT, C, 4], where=tmp)
            s_mul = sb("gla_s_mul", [P, 4, C, C], where=tmp)
            s_row = sb("gla_s_row", [P, 4, C], where=tmp)
            s_full = sb("gla_s_full", [P, 4, 8, C], where=tmp)
            def differences(v):
                yield v.memset(w[:], 0.0)
                f = four(lc[:])
                yield [v.tensor_tensor(four(w[:, lag])[:, :, :, lag:C], f[:, :, :, lag:C], f[:, :, :, 0:C - lag],
                                       ALU.subtract) for lag in range(C)]
            vector_phase(k, differences)

            def decays(s):
                yield [s.activation(four(w[:, lag])[:, :, :, lag:C], four(w[:, lag])[:, :, :, lag:C], ACT.Exp)
                       for lag in range(C)]
            scalar_phase(k, decays)

            def products(v):
                q, kk = four(qk[:, 0:2, :]), four(qk[:, 2:4, :])
                for factor, at in ((q, lambda lag: slice(lag, C)), (kk, lambda lag: slice(0, C - lag))):
                    yield [v.tensor_tensor(four(w[:, lag])[:, :, :, lag:C], four(w[:, lag])[:, :, :, lag:C],
                                           factor[:, :, :, at(lag)], ALU.mult) for lag in range(C)]
            vector_phase(k, products)

            def sum_heads(pe, banks):
                for i in range(T_LAT):
                    for lag in range(C):
                        for p in range(2):
                            c = (i * C + lag) * 4 + 2 * p
                            mm = nc.tensor.matmul(banks[0][:, c:c + 2], w[:, lag, p, i * P:(i + 1) * P], head_is[:],
                                                  start=True, stop=True, skip_group_check=True)
                yield mm
            banks_phase(k, [(sum_heads, [("dve", lambda bank: nc.vector.tensor_copy(
                s_lag[:].rearrange("p t c h -> p (t c h)"), bank[:, 0:T_LAT * C * 4]))])])
            for i in range(T_LAT):
                def spread(v, i=i):
                    yield [v.tensor_tensor(s_mul[:, h], s_lag[:, i, :, h].unsqueeze(1).to_broadcast([P, C, C]),
                                           lag_is[:].rearrange("p l j -> p j l"), ALU.mult) for h in range(4)]
                    yield v.tensor_reduce(s_row[:], s_mul[:], AX.X, ALU.add)
                    yield [v.tensor_tensor(s_full[:, h], s_row[:, h, :].unsqueeze(1).to_broadcast([P, 8, C]),
                                           chunk_is[:].unsqueeze(2).to_broadcast([P, 8, C]), ALU.mult)
                           for h in range(4)]
                vector_phase(k, spread)
                banks_phase(k, transpose_groups(k, [(
                    [s_full[:, h].rearrange("p n c -> p (n c)") for h in range(4)],
                    lambda who, bank, i=i: copy_by(k, who, s_t[:, i].rearrange("p h j -> p (h j)"), bank))]))
        with ExitStack() as tmp:
            o_t = sb("gla_o", [P, 4, S], where=tmp)
            sq = sb("gla_sq", [P, 4, S], where=tmp)
            groups = []
            for half in range(2):
                rows = slice(64 * half, 64 * half + 64)

                def fill(pe, banks, half=half, rows=rows):
                    for p in range(2):
                        h = 2 * p + half
                        for i in range(T_LAT):
                            c0 = p * S + i * P
                            mm = nc.tensor.matmul(banks[0][:, c0:c0 + P], v_row[:, i, h * P:(h + 1) * P], s_t[:, i, h, :],
                                                  start=True, stop=False, skip_group_check=True)
                            for c in range(8):
                                n = 8 * i + c
                                mm = nc.tensor.matmul(banks[0][:, c0 + C * c:c0 + C * c + C], states[rows, p, n, :],
                                                      q_in[rows, p, n * C:(n + 1) * C], start=False, stop=(c == 7),
                                                      skip_group_check=True)
                    yield mm

                groups.append((fill, [("dve", lambda bank, half=half: nc.vector.tensor_copy(
                    o_t[:].rearrange("p (a b) s -> p b a s", b=2)[:, half],
                    bank.rearrange("p (a s) -> p a s", a=2)))]))
            banks_phase(k, groups)

            def squares(s):
                yield s.activation(sq[:], o_t[:], ACT.Square)
                yield s.activation(g_t[:], g_t[:], ACT.Silu)
            scalar_phase(k, squares)
            groups = []
            for hp in range(2):
                def fill(pe, banks, hp=hp):
                    yield nc.tensor.matmul(banks[0], ones[:], sq[:, 2 * hp:2 * hp + 2, :].rearrange("p h s -> p (h s)"),
                                           start=True, stop=True)
                groups.append((fill, [("dve", lambda bank, hp=hp: nc.vector.tensor_scalar(
                    q_in[:].rearrange("p h s -> p (h s)") if hp == 0 else lc[:].rearrange("p h s -> p (h s)"),
                    bank, 1.0 / P, 1e-6, ALU.mult, ALU.add))]))
            banks_phase(k, groups)
            scalar_phase(k, lambda s: [s.activation(a[:], a[:], ACT.Sqrt) for a in (q_in, lc)])

            def finish(v):
                for hp, a in enumerate((q_in, lc)):
                    o = o_t[:, 2 * hp:2 * hp + 2, :]
                    yield v.reciprocal(a[:], a[:])
                    yield v.tensor_tensor(o, o, a[:], ALU.mult)
                    yield v.scalar_tensor_tensor(out=br_t[:, 0, 2 * hp:2 * hp + 2, :], in0=o, scalar=col("gla_g"),
                                                 in1=g_t[:, 2 * hp:2 * hp + 2, :], op0=ALU.mult, op1=ALU.mult)
            vector_phase(k, finish)


def conv_branch(k, t, h_t, col, br_t):
    nc, sb = k.nc, k.sb
    with ExitStack() as tmp:
        z = sb("sc_z", [P, 12, S], where=tmp)
        banks_phase(k, columns_of(k, h_t, 1536, lambda b, h: z[:, b, :]))

        def steps(v):
            u = z[:, 4:8, :]
            yield v.tensor_tensor(u, u, z[:, 8:12, :], ALU.mult)
            o, i = br_t[:, 1], z[:, 4:8, :]
            yield [v.tensor_scalar(o[:, b, :], i[:, b, :], col("scw2", b), None, ALU.mult) for b in range(4)]
            for back, name in ((1, "scw1"), (2, "scw0")):
                yield [v.scalar_tensor_tensor(out=o[:, b, back:S], in0=i[:, b, 0:S - back], scalar=col(name, b),
                                              in1=o[:, b, back:S], op0=ALU.mult, op1=ALU.add) for b in range(4)]
            yield v.tensor_tensor(br_t[:, 1], br_t[:, 1], z[:, 0:4, :], ALU.mult)
        vector_phase(k, steps)


def dilated_branch(k, t, h_t, br_t):
    nc, sb = k.nc, k.sb
    with ExitStack() as dil:
        q_t = sb("dil_q_t", [P, 12, S], where=dil)
        k_t = sb("dil_k_t", [P, 12, S], where=dil)
        vv = sb("dil_v", [P, T_LAT, 1536], where=dil)
        y = sb("dil_y", [P, T_LAT, 512], where=dil)
        mask = sb("dil_mask", [P, T_LAT, 3 * S], where=dil)
        with ExitStack() as tmp:
            z = sb("dil_z", [P, T_LAT, 3072], where=tmp)
            tabs = sb("dil_tabs", [P, T_LAT, 2, P], where=tmp)
            pos_i = sb("pos_i", [P, T_LAT], I32, where=tmp)
            pos = sb("pos", [P, T_LAT], where=tmp)
            inv = sb("inv_freq", [P, 64], where=tmp)
            ang = sb("dil_ang", [P, T_LAT, 2, 64], where=tmp)
            rnd = sb("dil_rnd", [P, T_LAT, 2, 64], where=tmp)
            load_phase(k, [(mask[:], t["dil_mask"].rearrange("(t p) k -> p t k", p=P)), (inv[:], t["inv_freq"])]
                       + [(pos_i[:, i:i + 1], t["positions_2"][0, i * P:(i + 1) * P].unsqueeze(1))
                          for i in range(T_LAT)])

            def split(who, r, n0, nn, bank):
                dst = z[:, r, n0:n0 + nn] if n0 < 3072 else vv[:, r, n0 - 3072:n0 - 3072 + nn]
                return copy_by(k, who, dst, bank)
            banks_phase(k, project_groups(k, lambda kt, r: h_t[:, kt, r * P:(r + 1) * P], DK, [P] * T_LAT, 4608,
                                          split))
            two_pi = 2.0 * math.pi
            hi = 6.28125
            lo = float(np.float32(two_pi - hi))
            magic = 12582912.0

            def angles(v):
                yield v.tensor_copy(pos[:], pos_i[:])
                for i in range(T_LAT):
                    yield v.tensor_scalar(ang[:, i, 0, :], inv[:], pos[:, i:i + 1], None, ALU.mult)
                    yield v.tensor_scalar(rnd[:, i, 0, :], ang[:, i, 0, :], 1.0 / two_pi, None, ALU.mult)
                    yield v.tensor_scalar(rnd[:, i, 1, :], rnd[:, i, 0, :], 0.25, None, ALU.add)
                yield v.tensor_scalar(rnd[:], rnd[:], magic, None, ALU.add)
                yield v.tensor_scalar(rnd[:], rnd[:], -magic, None, ALU.add)
                for i in range(T_LAT):
                    yield v.tensor_copy(ang[:, i, 1, :], ang[:, i, 0, :])
                yield v.scalar_tensor_tensor(out=ang[:], in0=rnd[:], scalar=-hi, in1=ang[:], op0=ALU.mult, op1=ALU.add)
                yield v.scalar_tensor_tensor(out=ang[:], in0=rnd[:], scalar=-lo, in1=ang[:], op0=ALU.mult, op1=ALU.add)
                for i in range(T_LAT):
                    yield v.tensor_scalar(ang[:, i, 1, :], ang[:, i, 1, :], math.pi / 2, None, ALU.add)
                yield v.tensor_scalar(ang[:], ang[:], 3.1415925, -3.1415925, ALU.min, ALU.max)
            vector_phase(k, angles)

            def sines(s):
                yield [s.activation(tabs[:, :, 1, 64:P], ang[:, :, 0, :], ACT.Sin),
                       s.activation(tabs[:, :, 1, 0:64], ang[:, :, 0, :], ACT.Sin, scale=-1.0),
                       s.activation(tabs[:, :, 0, 0:64], ang[:, :, 1, :], ACT.Sin),
                       s.activation(tabs[:, :, 0, 64:P], ang[:, :, 1, :], ACT.Sin)]
            scalar_phase(k, sines)
            heads = lambda a: a.rearrange("p (h d) -> p h d", d=P)
            with ExitStack() as tr:
                t1 = sb("dil_t1", [P, 3072], where=tr)

                def rotate(v):
                    for i in range(T_LAT):
                        zz, tt_ = heads(z[:, i, :]), heads(t1[:])
                        lo = tabs[:, i, 1, 0:64].unsqueeze(1).to_broadcast([P, 24, 64])
                        hi = tabs[:, i, 1, 64:P].unsqueeze(1).to_broadcast([P, 24, 64])
                        yield [v.tensor_tensor(tt_[:, :, 0:64], zz[:, :, 64:P], lo, ALU.mult),
                               v.tensor_tensor(tt_[:, :, 64:P], zz[:, :, 0:64], hi, ALU.mult)]
                        yield v.tensor_tensor(zz, zz, tabs[:, i, 0, :].unsqueeze(1).to_broadcast([P, 24, P]), ALU.mult)
                        yield v.tensor_tensor(zz, zz, tt_, ALU.add)
                vector_phase(k, rotate)
            jobs = []
            for half, dst in enumerate((q_t, k_t)):
                for b in range(0, 12, 2):
                    jobs.append(([z[:, i, 1536 * half + (b + a) * P:1536 * half + (b + a + 1) * P]
                                  for a in range(2) for i in range(T_LAT)],
                                 lambda who, bank, b=b, dst=dst: copy_by(
                                     k, who, dst[:, b:b + 2, :].rearrange("p b s -> p (b s)"), bank)))
            banks_phase(k, transpose_groups(k, jobs))
        units = []
        for i in range(T_LAT):
            for h in range(4):
                units.append(dict(
                    qk=[(q_t[:, 4 * g + h, i * P:(i + 1) * P], k_t[:, 4 * g + h, :]) for g in range(3)],
                    v=[vv[:, j, (4 * g + h) * P:(4 * g + h + 1) * P] for g in range(3) for j in range(T_LAT)],
                    mask=mask[:, i, :], sink=None, out=y[:, i, h * P:(h + 1) * P]))
        attention(k, "dil", units, P ** -0.5, 3 * S, P)
        banks_phase(k, transpose_groups(k, [([y[:, i, b * P:(b + 1) * P] for i in range(T_LAT)],
                                             lambda who, bank, b=b: copy_by(k, who, br_t[:, 2, b, :], bank))
                                            for b in range(4)]))


def kernel(**inputs):
    import numpy as _np
    import concourse.bacc as _bacc
    from concourse import mybir as _mybir
    from concourse.bass_utils import run_bass_kernel_spmd as _run

    nc = _bacc.Bacc("TRN2", target_bir_lowering=False, num_devices=1)
    arrays, aps = {}, {}
    for name, a in list(inputs.items()) + list(shape_constants().items()):
        a = _np.ascontiguousarray(a)
        arrays[f"in_{name}_dram"] = a
        aps[name] = nc.dram_tensor(f"in_{name}_dram", a.shape, _mybir.dt.from_np(a.dtype), kind="ExternalInput").ap()
    out = nc.dram_tensor("out_0_dram", (1, S, D), F32, kind="ExternalOutput").ap()
    two_blocks(nc, aps, out)
    r = _run(nc, [arrays], core_ids=[0])
    return r.results[0]["out_0_dram"]
```

```python
import math
from contextlib import ExitStack

import numpy as np
import concourse.bass as bass
from concourse import mybir

F32 = mybir.dt.float32
I32 = mybir.dt.int32
U32 = mybir.dt.uint32
ACT = mybir.ActivationFunctionType
ALU = mybir.AluOpType
AX = mybir.AxisListType

P = 128
D = 1024
DK = D // P
S = 256
T_LAT = S // P
T_ALL = 2 * T_LAT
SLOTS = 8
WIDE_SLOTS = 14
SLOT = 64
BANK = 512
NEG = -1.0e30
STOP = None


class Tally:

    def __init__(self, sem):
        self.sem, self.n = sem, 0

    def mark(self, ins, by=1):
        ins.then_inc(self.sem, by)
        self.n += by
        return self.n


class Signal:

    def __init__(self, sem):
        self.sem, self.base = sem, 0

    def at(self, v):
        return self.sem, self.base + v


class Core:

    def __init__(self, nc, ctx):
        self.nc, self.ctx = nc, ctx
        sem = lambda n: ctx.enter_context(nc.semaphore(n))
        self.tensor_done = Tally(sem("tensor_done"))
        self.act_evac = Tally(sem("act_evac"))
        self.dve_evac = Tally(sem("dve_evac"))
        self.dve_step = Tally(sem("dve_step"))
        self.dve_own = Tally(sem("dve_own"))
        self.act_step = Tally(sem("act_step"))
        self.pool_step = Tally(sem("pool_step"))
        self.load_done = Tally(sem("load_done"))
        self.store_done = Tally(sem("store_done"))
        self.soft_done = Tally(sem("table_done"))
        self.gathered = [Tally(sem(f"gathered{i}")) for i in range(4)]
        self.stored = [Tally(sem(f"y_stored{i}")) for i in range(2)]
        self.scores_ready = Signal(sem("scores_ready"))
        self.max_ready = Signal(sem("max_ready"))
        self.probs_ready = Signal(sem("probs_ready"))
        self.turned = Signal(sem("probs_turned"))
        self.turned_copied = Signal(sem("turned_copied"))
        self.mixed = Signal(sem("values_mixed"))
        self.out_done = Signal(sem("out_done"))
        self.slot_full = [Tally(sem(f"slot_full{i}")) for i in range(WIDE_SLOTS)]
        self.psum = ctx.enter_context(nc.psum_tensor("psum", [P, 8, BANK], F32))
        self.ring = [self.sb(f"ring{i}", [P, 4, BANK]) for i in range(SLOTS)]
        self.next_slot, self.in_slot = 0, {}
        self.chunks, self.issued, self.taken, self.used_at = [], 0, 0, []
        self.wanted, self.awaited, self.pump_to = [], 0, None

    def sb(self, name, shape, dt=F32, where=None):
        return (where or self.ctx).enter_context(self.nc.sbuf_tensor(name, shape, dt))

    def plan(self, w, k_rows, n_cols, n_first=0, slots=None):
        for n0 in range(n_first, n_first + n_cols, BANK):
            nn = min(BANK, n_first + n_cols - n0)
            for k0 in range(0, k_rows, 4 * P):
                kt = min(4, (k_rows - k0) // P)
                if slots is None:
                    slot = self.next_slot
                    self.next_slot = (slot + 1) % SLOTS
                else:
                    slot = next(slots)
                before = self.in_slot.setdefault(slot, [])
                self.chunks.append((w[k0:k0 + kt * P, n0:n0 + nn].rearrange("(j p) n -> p j n", p=P), kt, nn, slot,
                                    before[-1] if before else None, len(before) + 1))
                before.append(len(self.chunks) - 1)

    def wide_slots(self):
        order = [(self.next_slot + i) % SLOTS for i in range(SLOTS)] + list(range(SLOTS, WIDE_SLOTS))
        while True:
            yield from order

    def widen(self, where, tag):
        self.ring += [self.sb(f"wide{tag}_{i}", [P, 4, BANK], where=where) for i in range(SLOTS, WIDE_SLOTS)]
        where.callback(lambda: self.ring.__delitem__(slice(SLOTS, None)))

    def pump(self, sp):
        for dst, src in self.wanted:
            self.load_done.mark(sp.dma_start(dst, src), 16)
        self.wanted = []
        while self.issued < (len(self.chunks) if self.pump_to is None else self.pump_to):
            src, kt, nn, slot, before, _ = self.chunks[self.issued]
            if slot >= len(self.ring) or (before is not None and before >= len(self.used_at)):
                break
            if before is not None:
                sp.wait_ge(self.tensor_done.sem, self.used_at[before])
            self.slot_full[slot].mark(sp.dma_start(self.ring[slot][:, 0:kt, 0:nn], src), 16)
            self.issued += 1

    def take(self, pe, kt, nn):
        _, rows, cols, slot, _, times = self.chunks[self.taken]
        assert (rows, cols) == (kt, nn), (self.taken, rows, cols, kt, nn)
        self.taken += 1
        pe.wait_ge(self.slot_full[slot].sem, 16 * times)
        return self.ring[slot][:, 0:kt, 0:nn]

    def ahead(self, loads):
        self.wanted += loads

    def await_loads(self, act):
        if self.load_done.n > self.awaited:
            self.awaited = self.load_done.n
            act.wait_ge(self.load_done.sem, self.awaited)

    def used(self, at):
        self.used_at.append(at)


def chain(eng, tally, ins):
    eng.wait_ge(tally.sem, tally.mark(ins[-1] if isinstance(ins, list) else ins))


def banks_phase(k, groups, pool_program=None, act_last=None, wait_loads=True, pool_first=None, act_first=None,
                dve_first=None):
    nc = k.nc
    act0, dve0 = k.act_evac.n, k.dve_evac.n
    filled = []
    with nc.Block(no_gpsimd_drain=True) as block:
        if pool_first is not None:
            @block.gpsimd
            def _(pool):
                pool_first(pool)

        @block.tensor
        def _(pe):
            holder = [None] * 8
            emptied = {"act": act0, "dve": dve0}
            at = 0
            for fill, empties, *after in groups:
                if after and emptied["act"] > act0:
                    pe.wait_ge(k.act_evac.sem, emptied["act"])
                if after and emptied["dve"] > dve0:
                    pe.wait_ge(k.dve_evac.sem, emptied["dve"])
                mine = [(at + i) % 8 for i in range(len(empties))]
                at += len(empties)
                for b in mine:
                    if holder[b] is not None:
                        pe.wait_ge(*holder[b])
                last = None
                for last in fill(pe, [k.psum[:, b, :] for b in mine]):
                    done = k.tensor_done.mark(last)
                filled.append(done)
                for b, (who, _) in zip(mine, empties):
                    emptied[who] += 1
                    holder[b] = (k.act_evac.sem if who == "act" else k.dve_evac.sem, emptied[who])

        def drain(eng, who, tally):
            at = 0
            for g, (_, empties, *_) in enumerate(groups):
                if any(w == who for w, _ in empties):
                    eng.wait_ge(k.tensor_done.sem, filled[g])
                for w, empty in empties:
                    if w == who:
                        tally.mark(empty(k.psum[:, at % 8, :]))
                    at += 1
            eng.wait_ge(tally.sem, tally.n)

        @block.scalar
        def _(act):
            if act_first is not None:
                act_first(act)
            drain(act, "act", k.act_evac)
            if wait_loads:
                k.await_loads(act)
            if act_last is not None:
                act_last(act)

        @block.vector
        def _(dve):
            if dve_first is not None:
                dve_first(dve)
            drain(dve, "dve", k.dve_evac)

        if pool_program is not None:
            @block.gpsimd
            def _(pool):
                pool_program(pool)

        @block.sync
        def _(sp):
            k.pump(sp)


def copy_by(k, who, out, src):
    return k.nc.scalar.copy(out, src) if who == "act" else k.nc.vector.tensor_copy(out, src)


def turns():
    i = 0
    while True:
        yield ("act", "dve")[i % 2]
        i += 1


def project_groups(k, lhs, k_tiles, rows, n_cols, empty, who=None):
    groups = []
    turn = turns()
    for n0 in range(0, n_cols, BANK):
        nn = min(BANK, n_cols - n0)

        def fill(pe, banks, nn=nn):
            for k0 in range(0, k_tiles, 4):
                kt = min(4, k_tiles - k0)
                w = k.take(pe, kt, nn)
                for r, m in enumerate(rows):
                    for j in range(kt):
                        mm = k.nc.tensor.matmul(banks[r][0:m, 0:nn], lhs(k0 + j, r), w[:, j, :],
                                                start=(k0 + j == 0), stop=(k0 + j == k_tiles - 1))
                yield mm
                k.used(k.tensor_done.n)

        empties = []
        for r, m in enumerate(rows):
            w = who(r, n0) if callable(who) else who or next(turn)
            empties.append((w, lambda bank, w=w, r=r, n0=n0, nn=nn, m=m: empty(w, r, n0, nn, bank[0:m, 0:nn])))
        groups.append((fill, empties))
    return groups


def project_column_groups(k, rhs, k_tiles, n_rhs, n_cols, empty, who=None):
    groups = []
    turn = turns()
    for n0 in range(0, n_cols, BANK):
        nn = min(BANK, n_cols - n0)
        blocks = [(b, min(P, nn - b)) for b in range(0, nn, P)]

        def fill(pe, banks, nn=nn, blocks=blocks):
            for k0 in range(0, k_tiles, 4):
                kt = min(4, k_tiles - k0)
                w = k.take(pe, kt, nn)
                for i, (b, h) in enumerate(blocks):
                    for j in range(kt):
                        mm = k.nc.tensor.matmul(banks[i][0:h, 0:n_rhs], w[:, j, b:b + h], rhs(k0 + j),
                                                start=(k0 + j == 0), stop=(k0 + j == k_tiles - 1))
                yield mm
                k.used(k.tensor_done.n)

        empties = []
        for b, h in blocks:
            w = who or next(turn)
            empties.append((w, lambda bank, w=w, i=(n0 + b) // P, h=h: empty(w, i, h, bank[0:h, 0:n_rhs])))
        groups.append((fill, empties))
    return groups


def transpose_groups(k, jobs, who=None, diagonal=None):
    groups = []
    turn = turns()
    for sources, empty in jobs:
        def fill(pe, banks, sources=sources):
            for i, src in enumerate(sources):
                r, w = src.shape
                if diagonal is None:
                    mm = k.nc.tensor.transpose(banks[0][0:w, i * P:i * P + r], src, k.ident[0:r, 0:r])
                else:
                    mm = k.nc.tensor.matmul(banks[0][0:w, i * P:i * P + r], src, diagonal[:, i, :], start=True,
                                            stop=True, skip_group_check=True)
            yield mm
        w = who or next(turn)
        wd = sources[0].shape[1]
        n = len(sources) * P
        groups.append((fill, [(w, lambda bank, w=w, wd=wd, n=n, empty=empty: empty(w, bank[0:wd, 0:n]))]))
    return groups


def vector_phase(k, steps):
    with k.nc.Block(no_gpsimd_drain=True) as block:
        @block.vector
        def _(dve):
            for ins in steps(k.nc.vector):
                chain(dve, k.dve_step, ins)

        @block.sync
        def _(sp):
            k.pump(sp)


def load_phase(k, loads):
    with k.nc.Block(no_gpsimd_drain=True) as block:
        @block.scalar
        def _(act):
            for out, src in loads:
                k.load_done.mark(act.dma_start(out, src), 16)
            k.await_loads(act)

        @block.sync
        def _(sp):
            k.pump(sp)


def inv_rms(k, xs, width, eps, rs, junk, diagonal=None):
    nc, n = k.nc, len(xs)
    marks = {}
    with nc.Block(no_gpsimd_drain=True) as block:
        @block.scalar
        def _(act):
            for i in range(0, n, 2):
                chain(act, k.act_step, nc.scalar.activation(junk[0], xs[i], ACT.Square, accum_out=rs[:, i:i + 1]))
            marks["squares"] = k.act_step.n
            act.wait_ge(k.dve_step.sem, k.dve_step.n + n // 2 + 1)
            chain(act, k.act_step, nc.scalar.activation(rs[:, 0:n], rs[:, 0:n], ACT.Sqrt))
            marks["root"] = k.act_step.n

        @block.vector
        def _(dve):
            for i in range(1, n, 2):
                chain(dve, k.dve_step, nc.vector.tensor_tensor_reduce(
                    out=junk[1], in0=xs[i], in1=xs[i], scale=1.0, scalar=0.0, op0=ALU.mult, op1=ALU.add,
                    accum_out=rs[:, i:i + 1]))
            dve.wait_ge(k.act_step.sem, marks["squares"])
            k.dve_step.mark(nc.vector.tensor_scalar(rs[:, 0:n], rs[:, 0:n], 1.0 / width, eps, ALU.mult, ALU.add))
            dve.wait_ge(k.act_step.sem, marks["root"])
            chain(dve, k.dve_step, nc.vector.reciprocal(rs[:, 0:n], rs[:, 0:n]))
            if diagonal is not None:
                chain(dve, k.dve_step, [nc.vector.tensor_scalar(diagonal[:, i, :], k.ident[:], rs[:, i:i + 1], None,
                                                                ALU.mult) for i in range(n)])

        @block.sync
        def _(sp):
            k.pump(sp)


def norm_to_columns(k, tag, xs, width, eps, out, scale_bias):
    nc = k.nc
    with ExitStack() as tmp:
        n = len(xs)
        rs = k.sb(f"rs_{tag}", [P, n], where=tmp)
        junk = k.sb(f"junk_{tag}", [P, 2, width], where=tmp)
        diagonal = k.sb(f"diag_{tag}", [P, n, P], where=tmp)
        inv_rms(k, xs, width, eps, rs, [junk[:, 0, :], junk[:, 1, :]], diagonal)
        jobs = []
        for kt in range(width // P):
            def empty(who, bank, kt=kt):
                for t0, tn, sc, bi in scale_bias(kt):
                    o, i = out[:, kt, t0:t0 + tn], bank[:, t0:t0 + tn]
                    if who == "act":
                        ins = nc.scalar.activation(o, i, ACT.Identity, scale=sc, bias=0.0 if bi is None else bi)
                    elif bi is None:
                        ins = nc.vector.tensor_scalar(o, i, sc, None, ALU.mult)
                    else:
                        ins = nc.vector.tensor_scalar(o, i, sc, bi, ALU.mult, ALU.add)
                return ins
            jobs.append(([xs[i][:, kt * P:(kt + 1) * P] for i in range(n)], empty))
        banks_phase(k, transpose_groups(k, jobs, diagonal=diagonal))


def attention(k, tag, units, scale, width, dv):
    nc = k.nc
    n = len(units)
    wide = 1 if width <= BANK else 2
    N_SCORES, N_TURNED, N_OUT = (3, 2, 3) if wide == 1 else (2, 1, 2)
    N_PROBS, N_PROBS_T, N_STAT = 3, 2, 4
    turned_bank = wide * N_SCORES
    out_bank = turned_bank + wide * N_TURNED
    with ExitStack() as tmp:
        masked = None
        if units[0]["mask"] is not None:
            masked = k.sb(f"sc_{tag}", [P, N_SCORES, width], where=tmp)
        probs = k.sb(f"pr_{tag}", [P, N_PROBS, width], where=tmp)
        probs_t = k.sb(f"pt_{tag}", [P, N_PROBS_T, width], where=tmp)
        stat = k.sb(f"st_{tag}", [P, N_STAT, 4], where=tmp)
        scores_ready, max_ready, probs_ready = k.scores_ready, k.max_ready, k.probs_ready
        turned, turned_copied, mixed, out_done = k.turned, k.turned_copied, k.mixed, k.out_done

        def widths(u):
            return sum(kk.shape[-1] for _, kk in u["qk"])

        def banks(first, i, depth, w):
            b = first + wide * (i % depth)
            return k.psum[:, b:b + wide, :].rearrange("p b n -> p (b n)")[:, 0:w]

        s_view = lambda i, w: banks(0, i, N_SCORES, w)
        t_view = lambda i, w: banks(turned_bank, i, N_TURNED, w)
        o_view = lambda i: k.psum[:, out_bank + i % N_OUT, 0:dv]
        column = lambda i, c: stat[:, i % N_STAT, c:c + 1]

        with nc.Block(no_gpsimd_drain=True) as block:
            @block.tensor
            def _(pe):
                def scores(i):
                    c = 0
                    for q, kk in units[i]["qk"]:
                        w = kk.shape[-1]
                        mm = nc.tensor.matmul(s_view(i, c + w)[:, c:c + w], q, kk, start=(c % BANK == 0), stop=True,
                                              skip_group_check=True)
                        c += w
                    mm.then_inc(scores_ready.sem, 1)

                def mix(i):
                    pe.wait_ge(*turned_copied.at(i + 1))
                    if i >= N_OUT:
                        pe.wait_ge(*out_done.at(i - N_OUT + 1))
                    w = widths(units[i])
                    for j in range(w // P):
                        mm = nc.tensor.matmul(o_view(i), probs_t[:, i % N_PROBS_T, j * P:(j + 1) * P],
                                              units[i]["v"][j], start=(j == 0), stop=(j == w // P - 1))
                    mm.then_inc(mixed.sem, 1)

                for i in range(min(N_SCORES, n)):
                    scores(i)
                for i in range(n):
                    w = widths(units[i])
                    pe.wait_ge(*probs_ready.at(i + 1))
                    if i >= N_TURNED:
                        pe.wait_ge(*turned_copied.at(i - N_TURNED + 1))
                    for j in range(w // P):
                        mm = nc.tensor.transpose(t_view(i, w)[:, j * P:(j + 1) * P],
                                                 probs[:, i % N_PROBS, j * P:(j + 1) * P], k.ident[:])
                    mm.then_inc(turned.sem, 1)
                    if i + N_SCORES < n:
                        scores(i + N_SCORES)
                    if i >= 1:
                        mix(i - 1)
                mix(n - 1)

            @block.vector
            def _(dve):
                v = nc.vector

                def maxima(i):
                    u, w = units[i], widths(units[i])
                    dve.wait_ge(*scores_ready.at(i + 1))
                    src, sc = s_view(i, w), scale
                    if u["mask"] is not None:
                        src, sc = masked[:, i % N_SCORES, 0:w], 1.0
                        chain(dve, k.dve_step, v.scalar_tensor_tensor(out=src, in0=s_view(i, w), scalar=scale,
                                                                      in1=u["mask"], op0=ALU.mult, op1=ALU.add))
                    chain(dve, k.dve_step, v.reduce_max(column(i, 0), src, AX.X))
                    if u["sink"] is not None:
                        last = v.tensor_scalar(column(i, 1), column(i, 0), -sc, u["minus_sink"], ALU.mult, ALU.min)
                    else:
                        last = v.tensor_scalar(column(i, 1), column(i, 0), -sc, None, ALU.mult)
                    last.then_inc(max_ready.sem, 1)

                def finish(i):
                    u = units[i]
                    dve.wait_ge(*mixed.at(i + 1))
                    dve.wait_ge(*probs_ready.at(i + 1))
                    if u["sink"] is not None:
                        chain(dve, k.dve_step, v.tensor_tensor(column(i, 2), column(i, 2), column(i, 3), ALU.add))
                    chain(dve, k.dve_step, v.reciprocal(column(i, 2), column(i, 2)))
                    v.tensor_scalar(u["out"], o_view(i), column(i, 2), None, ALU.mult).then_inc(out_done.sem, 1)

                for i in range(n):
                    maxima(i)
                    if i >= 2:
                        finish(i - 2)
                for i in range(max(0, n - 2), n):
                    finish(i)
                dve.wait_ge(*out_done.at(n))

            @block.scalar
            def _(act):
                def turn_copy(i):
                    w = widths(units[i])
                    act.wait_ge(*turned.at(i + 1))
                    if i >= N_PROBS_T:
                        act.wait_ge(*mixed.at(i - N_PROBS_T + 1))
                    nc.scalar.copy(probs_t[:, i % N_PROBS_T, 0:w], t_view(i, w)).then_inc(turned_copied.sem, 1)

                for i in range(n):
                    u, w = units[i], widths(units[i])
                    act.wait_ge(*max_ready.at(i + 1))
                    if i >= N_PROBS:
                        act.wait_ge(*turned.at(i - N_PROBS + 1))
                    if i >= N_STAT:
                        act.wait_ge(*out_done.at(i - N_STAT + 1))
                    if u["sink"] is not None:
                        nc.scalar.activation(column(i, 3), u["sink"], ACT.Exp, bias=column(i, 1))
                    src, sc = (s_view(i, w), scale) if u["mask"] is None else (masked[:, i % N_SCORES, 0:w], 1.0)
                    nc.scalar.activation(probs[:, i % N_PROBS, 0:w], src, ACT.Exp, scale=sc, bias=column(i, 1),
                                         accum_out=column(i, 2)).then_inc(probs_ready.sem, 1)
                    if i >= 1:
                        turn_copy(i - 1)
                turn_copy(n - 1)

            @block.sync
            def _(sp):
                k.pump(sp)
        for signal in (scores_ready, max_ready, probs_ready, turned, turned_copied, mixed, out_done):
            signal.base += n


def rope_steps(v, jobs):
    products, sums = [], []
    for x, out, t1, cos2, sin2, heads, hd in jobs:
        h2 = hd // 2
        c = cos2.unsqueeze(1).to_broadcast([P, heads, hd])
        s_lo = sin2[:, 0:h2].unsqueeze(1).to_broadcast([P, heads, h2])
        s_hi = sin2[:, h2:hd].unsqueeze(1).to_broadcast([P, heads, h2])
        products += [v.tensor_tensor(t1[:, :, 0:h2], x[:, :, h2:hd], s_lo, ALU.mult),
                     v.tensor_tensor(t1[:, :, h2:hd], x[:, :, 0:h2], s_hi, ALU.mult),
                     v.tensor_tensor(out, x, c, ALU.mult)]
    yield products
    yield [v.tensor_tensor(out, out, t1, ALU.add) for _, out, t1, *_ in jobs]


def clear_other_halves(k, q_t):
    def program(pool):
        chain(pool, k.pool_step, [k.nc.gpsimd.memset(q_t[64:P, 0], 0.0), k.nc.gpsimd.memset(q_t[0:64, 1], 0.0)])
    return program


def copy_halves(k, who, q_t, block, bank):
    copy_by(k, who, q_t[0:64, 0, block, :], bank[0:64])
    return copy_by(k, who, q_t[64:P, 1, block, :], bank[64:P])


def rope_out(k, src, out, t1, cos2, sin2, hd):
    v = k.nc.vector
    heads, h2 = src.shape[-1] // hd, hd // 2
    split = lambda a: a.rearrange("p (h d) -> p h d", d=hd)
    x, o, t = split(src), split(out), split(t1[:, 0:heads * hd])
    v.wait_ge(k.dve_evac.sem, k.dve_evac.n)
    v.tensor_tensor(t[:, :, 0:h2], x[:, :, h2:hd], sin2[:, 0:h2].unsqueeze(1).to_broadcast([P, heads, h2]), ALU.mult)
    v.tensor_tensor(t[:, :, h2:hd], x[:, :, 0:h2], sin2[:, h2:hd].unsqueeze(1).to_broadcast([P, heads, h2]), ALU.mult)
    chain(v, k.dve_step, v.tensor_tensor(o, x, cos2.unsqueeze(1).to_broadcast([P, heads, hd]), ALU.mult))
    return v.tensor_tensor(o, o, t, ALU.add)


class Stop(Exception):
    pass


def shape_constants():
    f = np.float32
    tok = np.arange(S)
    row, col = (tok // 64).astype(f), (tok % 64).astype(f)

    def rope_table(dim):
        nf = dim // 4
        inv = (f(10000.0) ** (-np.arange(nf, dtype=f) / f(nf))).astype(f)
        ang = np.concatenate([row[:, None] * inv, col[:, None] * inv], axis=-1)
        c, s = np.cos(ang), np.sin(ang)
        return np.stack([np.concatenate([c, c], -1), np.concatenate([-s, s], -1)], 1).astype(f)

    q, kk = tok[:, None], tok[None, :]
    swa = np.where(np.abs(q - kk) <= 128, 0.0, NEG)
    swa = np.concatenate([swa, np.zeros((S, S))], 1).astype(f)
    dil = np.concatenate([np.where((q >= kk) & ((q - kk) % d == 0) & (q - kk <= 128 * d), 0.0, NEG)
                          for d in (1, 4, 16)], 1).astype(f)
    i16 = np.arange(P) % 16
    lag = (i16[:, None, None] - np.arange(16)[None, :, None] == np.arange(16)[None, None, :]).astype(f)
    fold = (np.arange(P)[:, None] % 32 == np.arange(32)[None, :]).astype(f)
    inv = (f(10000.0) ** (-np.arange(0, P, 2, dtype=f) / f(P))).astype(f)
    head = np.zeros((P, 62), f)
    head[:64, 30], head[64:, 31] = 1.0, 1.0
    return {
        "ident": np.eye(P, dtype=f), "rope64": rope_table(64), "rope32": rope_table(32), "swa_mask": swa,
        "dil_mask": dil, "fold_pick": fold, "inv_freq": np.tile(inv, (P, 1)),
        "lag_is": lag, "chunk_is": (np.arange(P)[:, None] // 16 == np.arange(8)[None, :]).astype(f),
        "head_is": head, "within_chunk": np.tile((tok % 16 != 0).astype(f), (P, 1)),
        "before": np.triu(np.ones((P, P), f), 1), "expert_number": np.tile(np.arange(32, dtype=f), (P, 1)),
        "descending": np.tile(np.arange(32, 0, -1, dtype=f), (P, 1)),
    }


def two_blocks(nc, t, out):
    try:
        with ExitStack() as ctx:
            program(Core(nc, ctx), t, out)
    except (Stop, AssertionError):
        if STOP is None:
            raise


def stop_at(name):
    if STOP == name:
        raise Stop()


def program(k, t, out):
    nc = k.nc
    sb = k.sb

    ada_part = lambda l, part: k.plan(t["ada_w"][l], D, 2 * D, 2 * D * part)
    ada_part(0, 0)
    for l in range(2):
        if l == 0:
            k.plan(t["ab_w_in"][0], D, 1184)
            ada_part(0, 1)
            ada_part(0, 2)
            ada_part(1, 0)
            k.plan(t["mla_w_uq"][0], 256, 768)
            k.plan(t["mla_w_ukv"][0], 128, 1024)
            ada_part(1, 1)
            ada_part(1, 2)
            k.plan(t["ab_w_out"][0], D, D)
        else:
            k.plan(t["diff_w_in"][0], D, 3072)
            k.plan(t["diff_w_out"][0], D, D)
        slots = k.wide_slots()
        for e in range(32):
            k.plan(t["expert_w1"][l, e], D, 512, slots=slots)
            k.plan(t["expert_w3"][l, e], D, 512, slots=slots)
            k.plan(t["expert_w2"][l, e], 512, D, slots=slots)
    w_in = t["w_in_2"][0]
    for first, cols in ((0, 512), (512, 512), (1024, 528), (1552, 1536), (3088, 4608)):
        k.plan(w_in, D, cols, first)
    k.plan(t["w_gate_2"][0], D, 3 * D)
    for g in range(3):
        k.plan(t["w_branch_2"][0, g], 512, D)
    k.plan(t["w_mix_out_2"][0], D, D)
    k.plan(t["w_ff_gate_2"][0], D, 2816)
    k.plan(t["w_ff_up_2"][0], D, 2816)
    k.plan(t["w_ff_down_2"][0], 2816, D)

    k.ident = sb("ident", [P, P])
    x = sb("x", [P, T_ALL, D])
    h_t = sb("h_t", [P, DK, 2 * S])
    cols = sb("cols", [P, 3 * P])
    silu_c = sb("silu_c", [P, DK, 32])
    mods = sb("mods", [P, 2, 6 * DK, 2])
    fold_pick = sb("fold_pick", [P, 32])
    rope64 = sb("rope64", [P, T_LAT, 2, 64])
    rope32 = sb("rope32", [P, T_LAT, 2, 32])
    descending = sb("descending", [P, 32])
    router_w = sb("router_w", [P, 2, DK, 36])
    router_b = sb("router_b", [P, 2, 36])
    before = sb("before", [P, P])
    number = sb("expert_number", [P, 32])
    late = {name: sb("late_" + name, shape) for name, shape in (
        ("inv_freq", [P, 64]), ("w_alpha_up", [16, S]), ("lag_is", [P, 16, 16]), ("chunk_is", [P, 8]),
        ("head_is", [P, 62]), ("within_chunk", [P, S]))}
    late["positions"] = sb("late_positions", [P, T_LAT], I32)
    late_from = {"inv_freq": t["inv_freq"],
                 "w_alpha_up": t["w_alpha_up_2"][0], "lag_is": t["lag_is"], "chunk_is": t["chunk_is"],
                 "head_is": t["head_is"], "within_chunk": t["within_chunk"]}
    late["fold_pick"] = fold_pick
    late_loads = [(late[name][:], src) for name, src in late_from.items()]
    late_loads += [(late["positions"][:, i:i + 1], t["positions_2"][0, i * P:(i + 1) * P].unsqueeze(1))
                   for i in range(T_LAT)]
    x_dram = t["x"][0].rearrange("(t p) d -> p t d", p=P)
    ctx_dram = t["ctx"][0].rearrange("(t p) d -> p t d", p=P)
    vec = lambda a: a.rearrange("(r c) -> r c", c=P)
    packs = [[("c", t["c"][0]), ("c_ctx", t["c_ctx"]), ("mix0", t["norm_mix"][0]), ("mix1", t["norm_mix"][1]),
              ("ffn0", t["norm_ffn"][0]), ("ffn1", t["norm_ffn"][1]), ("pre_mix", t["pre_mix_g_2"][0]),
              ("pre_ffn", t["pre_ffn_g_2"][0]), ("b_gate", t["b_gate_2"][0])],
             [("ffw0", t["ff_conv_w_2"][0, 0]), ("ffw1", t["ff_conv_w_2"][0, 1]), ("ffw2", t["ff_conv_w_2"][0, 2]),
              ("ff_b", t["ff_conv_b_2"][0]), ("scw0", t["sc_conv_w_2"][0, 0]), ("scw1", t["sc_conv_w_2"][0, 1]),
              ("scw2", t["sc_conv_w_2"][0, 2]), ("b_alpha", t["b_alpha_2"][0]), ("q_norm", t["mla_q_norm"][0]),
              ("kv_norm", t["mla_kv_norm"][0]), ("gla_g", t["gla_norm_g_2"][0])],
             [("ada_b0", t["ada_b"][0]), ("ada_b1", t["ada_b"][1])]]
    where = {}
    with ExitStack() as tmp:
        pk = [sb(f"pack{i}", [P, P], where=tmp) for i in range(3)]
        with nc.Block(no_gpsimd_drain=True) as block:
            @block.gpsimd
            def _(pool):
                for p in pk:
                    last = nc.gpsimd.memset(p[:], 0.0)
                chain(pool, k.pool_step, last)

            @block.vector
            def _(dve):
                chain(dve, k.dve_step, nc.vector.memset(silu_c[:], 0.0))
        loads = [(k.ident[:], t["ident"]), (fold_pick[:], t["fold_pick"])]
        k.pump_to = 2
        for i, pack in enumerate(packs):
            r = 0
            for name, a in pack:
                n = a.shape[0] // P
                loads.append((pk[i][r:r + n, :], vec(a)))
                where[name] = i * P + r
                r += n
        load_phase(k, loads)
        k.pump_to = None
        banks_phase(k, transpose_groups(k, [([p[:] for p in pk],
                                             lambda who, bank: copy_by(k, who, cols[:], bank))]))
    k.ahead([(x[:, 0:T_LAT, :], x_dram), (x[:, T_LAT:T_ALL, :], ctx_dram),
             (rope64[:], t["rope64"].rearrange("(t p) a b -> p t a b", p=P)),
             (rope32[:], t["rope32"].rearrange("(t p) a b -> p t a b", p=P))])
    router_loads = ([(descending[:], t["descending"]), (before[:], t["before"]), (number[:], t["expert_number"])]
            + [load for l in range(2) for load in (
                (router_w[:, l, :, 0:4], t["router_group_w"][l].rearrange("(j p) n -> p j n", p=P)),
                (router_w[:, l, :, 4:36], t["router_expert_w"][l].rearrange("(j p) n -> p j n", p=P)),
                (router_b[:, l, 0:4], t["router_group_b"][l].partition_broadcast(P)),
                (router_b[:, l, 4:36], t["router_expert_b"][l].partition_broadcast(P)))])
    col = lambda name, i=0, n=1: cols[:, where[name] + i:where[name] + i + n]
    stop_at("setup")

    mod_a = sb("mod_a", [P, 2, 2, DK])
    with k.nc.Block(no_gpsimd_drain=True) as block:
        @block.scalar
        def _(act):
            chain(act, k.act_step, [nc.scalar.activation(silu_c[:, :, i], col(name, 0, DK), ACT.Silu)
                                    for i, name in enumerate(("c", "c_ctx"))])

        @block.sync
        def _(sp):
            k.pump(sp)
    modulate = lambda l, parts: modulations(k, l, parts, col, silu_c, fold_pick, mods)
    modulate(0, (0,))
    with ExitStack() as first:
        gates = sb("gates", [P, 2, 2, D], where=first)
        for l in range(2):
            norm_gains(k, l, (0,) if l == 0 else (0, 1), col, mods, mod_a)
            if l == 0:
                load_phase(k, [])
                k.ahead(router_loads)
            else:
                spread_gates(k, l, mods, gates)
            stop_at(f"ada{l}")
            tiles = list(range(T_ALL))

            def shift_scale(which, n_ctx):
                def f(kt):
                    r = [(0, S, mod_a[:, which, 0, kt:kt + 1], mods[:, l, 3 * which * DK + kt, 0:1])]
                    if n_ctx:
                        r.append((S, S, mod_a[:, which, 1, kt:kt + 1], mods[:, l, 3 * which * DK + kt, 1:2]))
                    return r
                return f
            norm_to_columns(k, f"mix{l}", [x[:, i, :] for i in tiles], D, 1e-6, h_t, shift_scale(0, True))
            stop_at(f"norm{l}")
            if l == 0:
                swa_mla(k, t, x, h_t, gates, col, rope64, rope32, modulate, mods)
                norm_gains(k, l, (1,), col, mods, mod_a)
            else:
                final_g = sb("final_g", [P, D], where=first)
                k.ahead(late_loads + [(final_g[:], t["final_norm"].partition_broadcast(P))])
                differential(k, t, x, h_t, gates, rope64)
            stop_at(f"mixer{l}")
            tiles = list(range(T_ALL if l == 0 else T_LAT))
            norm_to_columns(k, f"ffn{l}", [x[:, i, :] for i in tiles], D, 1e-6, h_t, shift_scale(1, l == 0))
            stop_at(f"normf{l}")
            tables = dict(descending=descending, router_w=router_w[:, l], router_b=router_b[:, l], before=before,
                          number=number)
            experts(k, t, l, x, h_t, gates, len(tiles), tables)
            stop_at(f"moe{l}")
        row_norm(k, final_g, x)
    stop_at("block1")
    second_block(k, t, x, h_t, col, out, late)


def row_norm(k, g, x):
    nc = k.nc
    with ExitStack() as tmp:
        rs = k.sb("rs_final", [P, T_LAT], where=tmp)
        junk = k.sb("junk_final", [P, 2, D], where=tmp)
        inv_rms(k, [x[:, i, :] for i in range(T_LAT)], D, 1e-6, rs, [junk[:, 0, :], junk[:, 1, :]])

        def steps(v):
            for i in range(T_LAT):
                yield v.scalar_tensor_tensor(out=x[:, i, :], in0=x[:, i, :], scalar=rs[:, i:i + 1], in1=g[:],
                                             op0=ALU.mult, op1=ALU.mult)
        vector_phase(k, steps)


def modulations(k, l, parts, col, silu_c, fold_pick, mods):
    nc = k.nc
    per_part = 6 * D // 3
    with ExitStack() as tmp:
        rows = k.sb(f"mod_rows{l}_{parts[0]}", [P, per_part], where=tmp)
        groups = []
        turn = turns()
        for part in parts:
            for n0 in range(0, per_part, BANK):
                def fill(pe, banks):
                    for k0 in range(0, DK, 4):
                        w = k.take(pe, 4, BANK)
                        for j in range(4):
                            mm = nc.tensor.matmul(banks[0][32 * j:32 * j + 32, :], silu_c[:, k0 + j, :], w[:, j, :],
                                                  start=(k0 == 0), stop=(k0 + 4 == DK))
                        yield mm
                        k.used(k.tensor_done.n)
                who = next(turn)
                groups.append((fill, [(who, lambda bank, who=who, n0=n0: copy_by(k, who, rows[:, n0:n0 + BANK],
                                                                                  bank))]))

            def turn_rows(pe, banks):
                for b in range(per_part // P):
                    mm = nc.tensor.matmul(banks[0][:, 2 * b:2 * b + 2], rows[:, b * P:(b + 1) * P], fold_pick[:, 0:2],
                                          start=True, stop=True, skip_group_check=True)
                yield mm

            def add_bias(bank, part=part, n=per_part // P):
                b0 = part * n
                return nc.vector.tensor_tensor(
                    mods[:, l, b0:b0 + n, :], bank[:, 0:2 * n].rearrange("p (b s) -> p b s", s=2),
                    col(f"ada_b{l}", b0, n).unsqueeze(2).to_broadcast([P, n, 2]), ALU.add)
            groups.append((turn_rows, [("dve", add_bias)], True))
        banks_phase(k, groups, wait_loads=False)


def spread_gates(k, l, mods, gates):
    nc = k.nc
    groups = []
    for s in range(2):
        for g, kind in enumerate((2, 5)):
            for half in range(2):
                def spread(pe, banks, s=s, at=kind * DK + 4 * half):
                    for j in range(4):
                        mm = nc.tensor.matmul(banks[0][:, j * P:(j + 1) * P],
                                              mods[:, l, at + j, s:s + 1].to_broadcast([P, P]), k.ident[:],
                                              start=True, stop=True, skip_group_check=True)
                    yield mm
                who = ("act", "dve")[half]
                groups.append((spread, [(who, lambda bank, who=who, s=s, g=g, half=half: copy_by(
                    k, who, gates[:, s, g, half * BANK:(half + 1) * BANK], bank))]))
    banks_phase(k, groups)


def norm_gains(k, l, which_norms, col, mods, mod_a):
    vector_phase(k, lambda v: [[v.scalar_tensor_tensor(
        out=mod_a[:, which, s, :], in0=mods[:, l, (3 * which + 1) * DK:(3 * which + 2) * DK, s], scalar=1.0,
        in1=col(("mix", "ffn")[which] + str(l), 0, DK), op0=ALU.add, op1=ALU.mult)
        for which in which_norms for s in range(2)]])


def gated_residual(k, tag, o, x, gates, which, h_t, n_tiles):
    nc = k.nc
    jobs = [([o[:, i, kt * P:(kt + 1) * P] for i in range(n_tiles)],
             lambda who, bank, kt=kt: copy_by(k, who, h_t[:, kt, 0:n_tiles * P], bank)) for kt in range(DK)]
    banks_phase(k, transpose_groups(k, jobs))
    with ExitStack() as tmp:
        part = k.sb(f"gated_{tag}", [P, BANK], where=tmp)

        def add(who, r, n0, nn, bank):
            g = gates[:, 0 if r < T_LAT else 1, which, n0:n0 + nn]
            nc.vector.wait_ge(k.dve_evac.sem, k.dve_evac.n)
            chain(nc.vector, k.dve_step, nc.vector.tensor_tensor(part[:, 0:nn], bank, g, ALU.mult))
            return nc.vector.tensor_tensor(x[:, r, n0:n0 + nn], x[:, r, n0:n0 + nn], part[:, 0:nn], ALU.add)
        banks_phase(k, project_groups(k, lambda kt, r: h_t[:, kt, r * P:(r + 1) * P], DK, [P] * n_tiles, D, add,
                                      "dve"))


def swa_mla(k, t, x, h_t, gates, col, rope64, rope32, modulate, mods):
    nc, sb = k.nc, k.sb
    with ExitStack() as mix:
        o = sb("ab_o", [P, T_ALL, D], where=mix)
        mask = sb("swa_mask", [P, T_LAT, 2 * S], where=mix)
        sink = sb("sink", [P, 8], where=mix)
        k.ahead([(mask[:], t["swa_mask"].rearrange("(t p) k -> p t k", p=P)),
                 (sink[:], t["swa_sink"][0].partition_broadcast(P))])
        proj = sb("ab_proj", [P, T_ALL, 1184], where=mix)
        with ExitStack() as tmp:
            t1 = sb("rope_t1", [P, BANK], where=tmp)

            def out_of_psum(who, r, n0, nn, bank):
                dst = proj[:, r, n0:n0 + nn]
                if who == "act":
                    return nc.scalar.copy(dst, bank)
                roped, table, hd = {0: ((0, 512), rope64, 64), 512: ((0, 128), rope64, 64),
                                    1024: ((128, 160), rope32, 32)}[n0]
                plain = slice(roped[1], nn) if n0 == 512 else slice(0, roped[0])
                if n0:
                    nc.vector.tensor_copy(dst[:, plain], bank[:, plain])
                roped = slice(*roped)
                return rope_out(k, bank[:, roped], dst[:, roped], t1, table[:, r, 0, :], table[:, r, 1, :], hd)
            banks_phase(k, project_groups(
                k, lambda kt, r: h_t[:, kt, r * P:(r + 1) * P], DK, [P] * T_ALL, 1184, out_of_psum,
                lambda r, n0: "dve" if r < T_LAT else "act"))
        with ExitStack() as tmp:
            q_t = sb("swa_q_t", [P, 2, 4, 2 * S], where=tmp)
            k_t = sb("swa_k_t", [P, 2 * S], where=tmp)
            minus_sink = sb("minus_sink", [P, 8], where=tmp)
            load_phase(k, [])
            with ExitStack() as tq:
                pair = sb("swa_pair", [P, T_ALL, 4, 2, 64], where=tq)

                def steps(v):
                    yield [v.tensor_scalar(minus_sink[:], sink[:], -1.0, None, ALU.mult)] + [
                        v.tensor_copy(pair[:, i], proj[:, i, 0:512].rearrange("p (a b d) -> p b a d", a=2, d=64))
                        for i in range(T_ALL)]
                vector_phase(k, steps)
                jobs = [([pair[:, i, b].rearrange("p a d -> p (a d)") for i in range(T_ALL)],
                         lambda who, bank, b=b: copy_halves(k, who, q_t, b, bank)) for b in range(4)]
                jobs.append(([proj[:, i, 512:640] for i in range(T_ALL)],
                             lambda who, bank: copy_by(k, who, k_t[:], bank)))
                banks_phase(k, transpose_groups(k, jobs), clear_other_halves(k, q_t))
            units = {0: [], 1: []}
            for i in range(T_ALL):
                lat = i < T_LAT
                k0 = 0 if lat else S
                for h in range(8):
                    a, b = divmod(h, 4)
                    units[0 if lat else 1].append(dict(
                        qk=[(q_t[:, a, b, i * P:(i + 1) * P], k_t[:, k0:2 * S])],
                        v=[proj[:, j, 640 + 64 * a:704 + 64 * a] for j in range(k0 // P, T_ALL)],
                        mask=mask[:, i, :] if lat else None, sink=sink[:, h:h + 1],
                        minus_sink=minus_sink[:, h:h + 1], out=o[:, i, 64 * h:64 * h + 64]))
            modulate(0, (1,))
            attention(k, "swa", units[0], 64 ** -0.5, 2 * S, 64)
            modulate(0, (2,))
            attention(k, "swac", units[1], 64 ** -0.5, S, 64)
            modulate(1, (0,))
        stop_at("swa")
        with ExitStack() as tmp:
            q_t = h_t[0:96, :, :]
            with ExitStack() as tq:
                cq_t = sb("cq_t", [P, 2, 2 * S], where=tq)
                q = sb("mla_q", [P, T_ALL, 768], where=tq)
                norm_to_columns(k, "cq", [proj[:, i, 768:1024] for i in range(T_ALL)], 256, 1e-6, cq_t,
                                lambda kt: [(0, 2 * S, col("q_norm", kt), None)])
                banks_phase(k, project_groups(
                    k, lambda kt, r: cq_t[:, kt, r * P:(r + 1) * P], 2, [P] * T_ALL, 768,
                    lambda who, r, n0, nn, bank: copy_by(k, who, q[:, r, n0:n0 + nn], bank)))
                with ExitStack() as tr:
                    t1 = sb("mla_t1", [P, T_LAT, 8, 32], where=tr)
                    qr = sb("mla_qr", [P, T_LAT, 8, 32], where=tr)
                    rope_part = lambda i: q[:, i, :].rearrange("p (h d) -> p h d", d=96)[:, :, 64:96]

                    def steps(v):
                        yield from rope_steps(v, [(rope_part(i), qr[:, i], t1[:, i], rope32[:, i, 0, :],
                                                   rope32[:, i, 1, :], 8, 32) for i in range(T_LAT)])
                        yield [v.tensor_copy(rope_part(i), qr[:, i]) for i in range(T_LAT)]
                    vector_phase(k, steps)
                jobs = [([q[:, i, 96 * h:96 * h + 96] for i in range(T_ALL)],
                         lambda who, bank, h=h: copy_by(k, who, q_t[:, h, :], bank)) for h in range(8)]
                banks_phase(k, transpose_groups(k, jobs))
            k_t = sb("mla_k_t", [96, 8, 2 * S], where=tmp)
            kv = sb("mla_kv", [P, T_ALL, 1024], where=tmp)
            with ExitStack() as tk:
                ckv_t = sb("ckv_t", [P, 1, 2 * S], where=tk)
                norm_to_columns(k, "ckv", [proj[:, i, 1024:1152] for i in range(T_ALL)], 128, 1e-6, ckv_t,
                                lambda kt: [(0, 2 * S, col("kv_norm"), None)])
                banks_phase(k, project_groups(
                    k, lambda kt, r: ckv_t[:, kt, r * P:(r + 1) * P], 1, [P] * T_ALL, 1024,
                    lambda who, r, n0, nn, bank: copy_by(k, who, kv[:, r, n0:n0 + nn], bank)))

            jobs = [([kv[:, i, 128 * h:128 * h + 64] for i in range(T_ALL)],
                     lambda who, bank, h=h: copy_by(k, who, k_t[0:64, h, :], bank)) for h in range(8)]
            jobs += [([proj[:, i, 1088:1184] for i in range(T_ALL)],
                      lambda who, bank, h=h: copy_by(k, who, k_t[64:96, h:h + 4, :],
                                                     bank[64:96].unsqueeze(1).to_broadcast([32, 4, 2 * S])))
                     for h in (0, 4)]
            banks_phase(k, transpose_groups(k, jobs))
            units = {0: [], 1: []}
            for i in range(T_ALL):
                k0 = 0 if i < T_LAT else S
                for h in range(8):
                    units[min(1, k0)].append(dict(
                        qk=[(q_t[:, h, i * P:(i + 1) * P], k_t[:, h, k0:2 * S])],
                        v=[kv[:, j, 128 * h + 64:128 * h + 128] for j in range(k0 // P, T_ALL)],
                        mask=None, sink=None, out=o[:, i, 512 + 64 * h:576 + 64 * h]))
            attention(k, "mla", units[0], 96 ** -0.5, 2 * S, 64)
            modulate(1, (1,))
            attention(k, "mlac", units[1], 96 ** -0.5, S, 64)
        modulate(1, (2,))
        spread_gates(k, 0, mods, gates)
        gated_residual(k, "ab", o, x, gates, 0, h_t, T_ALL)


def differential(k, t, x, h_t, gates, rope64):
    nc, sb = k.nc, k.sb
    lambda_init = 0.8 - 0.6 * math.exp(-0.3)
    with ExitStack() as mix:
        k_t = sb("diff_k_t", [P, 8, 2 * S], where=mix)
        q_t = sb("diff_q_t", [P, 2, 8, S], where=mix)
        small = sb("diff_small", [P, 8], where=mix)
        lqk = sb("lqk", [P, 4, 64], where=mix)
        subln = sb("subln", [P, P], where=mix)
        k.ahead([(lqk[:, i, :], t["diff_lambda_" + n][0].partition_broadcast(P))
                 for i, n in enumerate(("q1", "k1", "q2", "k2"))]
                + [(subln[:], t["diff_subln"][0].partition_broadcast(P))])
        vt = sb("diff_v", [P, T_ALL, D], where=mix)

        def roped_to_columns(tag, n_tiles, to_columns, pool_program=None):
            with ExitStack() as tmp:
                z = sb(f"diff_{tag}", [P, n_tiles, D], where=tmp)
                t1 = sb(f"diff_t1{tag}", [P, BANK], where=tmp)

                def out_of_psum(who, r, n0, nn, bank):
                    if r < T_LAT:
                        return rope_out(k, bank, z[:, r, n0:n0 + nn], t1, rope64[:, r, 0, :], rope64[:, r, 1, :], 64)
                    return copy_by(k, who, z[:, r, n0:n0 + nn], bank)
                banks_phase(k, project_groups(
                    k, lambda kt, r: h_t[:, kt, r * P:(r + 1) * P], DK, [P] * n_tiles, D, out_of_psum,
                    lambda r, n0: "dve" if r < T_LAT else "act"))
                jobs = [([z[:, i, j * P:(j + 1) * P] for i in range(n_tiles)],
                         lambda who, bank, j=j: to_columns(who, j, bank)) for j in range(8)]
                banks_phase(k, transpose_groups(k, jobs), pool_program)
        roped_to_columns("q", T_LAT, lambda who, j, bank: copy_halves(k, who, q_t, j, bank),
                         clear_other_halves(k, q_t))
        roped_to_columns("k", T_ALL, lambda who, j, bank: copy_by(k, who, k_t[:, j, :], bank))
        banks_phase(k, project_groups(
            k, lambda kt, r: h_t[:, kt, r * P:(r + 1) * P], DK, [P] * T_ALL, D,
            lambda who, r, n0, nn, bank: copy_by(k, who, vt[:, r, n0:n0 + nn], bank)))
        a1 = sb("diff_a1", [P, T_LAT, D], where=mix)
        a2 = sb("diff_a2", [P, T_LAT, D], where=mix)
        units = []
        for i in range(T_LAT):
            for j in range(8):
                for a, dst in enumerate((a1, a2)):
                    units.append(dict(qk=[(q_t[:, a, j, i * P:(i + 1) * P], k_t[:, j, :])],
                                      v=[vt[:, m, j * P:(j + 1) * P] for m in range(T_ALL)],
                                      mask=None, sink=None, out=dst[:, i, j * P:(j + 1) * P]))
        attention(k, "diff", units, 64 ** -0.5, 2 * S, P)
        with ExitStack() as tmp:
            prod = sb("lqk_prod", [P, 64], where=tmp)
            ms = sb("diff_ms", [P, T_LAT * 8], where=tmp)
            def dots(v):
                for i in range(2):
                    yield v.tensor_tensor(prod[:], lqk[:, 2 * i, :], lqk[:, 2 * i + 1, :], ALU.mult)
                    yield v.reduce_sum(small[:, i:i + 1], prod[:], AX.X)
            vector_phase(k, dots)
            scalar_phase(k, lambda s: [s.activation(small[:, 2:4], small[:, 0:2], ACT.Exp)])
            whole = lambda a: a[:].rearrange("p t d -> p (t d)")
            per_head = lambda a: a[:].rearrange("p t (h d) -> p (t h) d", d=P)

            def combine(v):
                yield v.tensor_tensor(small[:, 4:5], small[:, 3:4], small[:, 2:3], ALU.subtract)
                yield v.tensor_scalar(small[:, 4:5], small[:, 4:5], -lambda_init, None, ALU.add)
                yield v.scalar_tensor_tensor(out=whole(a1), in0=whole(a2), scalar=small[:, 4:5], in1=whole(a1),
                                             op0=ALU.mult, op1=ALU.add)
                yield v.tensor_tensor(whole(a2), whole(a1), whole(a1), ALU.mult)
                yield v.tensor_reduce(ms[:], per_head(a2), AX.X, ALU.add)
                yield v.tensor_scalar(ms[:], ms[:], 1.0 / P, 1e-5, ALU.mult, ALU.add)
            vector_phase(k, combine)
            scalar_phase(k, lambda s: [s.activation(ms[:], ms[:], ACT.Sqrt)])

            def scaled(v):
                yield v.reciprocal(ms[:], ms[:])
                yield v.tensor_scalar(ms[:], ms[:], 1.0 - lambda_init, None, ALU.mult)
                yield v.tensor_tensor(per_head(a1), per_head(a1), ms[:].unsqueeze(2).to_broadcast([P, T_LAT * 8, P]),
                                      ALU.mult)
                yield v.tensor_tensor(per_head(a1), per_head(a1), subln[:].unsqueeze(1).to_broadcast([P, T_LAT * 8, P]),
                                      ALU.mult)
            vector_phase(k, scaled)
        gated_residual(k, "diff", a1, x, gates, 0, h_t, T_LAT)


def scalar_phase(k, steps):
    with k.nc.Block(no_gpsimd_drain=True) as block:
        @block.scalar
        def _(act):
            for ins in steps(k.nc.scalar):
                chain(act, k.act_step, ins)

        @block.sync
        def _(sp):
            k.pump(sp)


def route(k, l, h_t, n_tiles, tables, pick, weight):
    nc, sb = k.nc, k.sb
    n = n_tiles
    with ExitStack() as tmp:
        wr, br, descending = tables["router_w"], tables["router_b"], tables["descending"]
        lg = sb(f"logits{l}", [P, n, 36], where=tmp)
        one = sb(f"r_one{l}", [P, n, 4], where=tmp)
        w4 = sb(f"r_w4{l}", [P, n, 4], where=tmp)
        ex = sb(f"r_ex{l}", [P, n, 4], where=tmp)
        r1 = sb(f"r_r1{l}", [P, n, 8], where=tmp)
        em = sb(f"r_em{l}", [P, n, 32], where=tmp)
        w32 = sb(f"r_w32{l}", [P, n, 32], where=tmp)
        def fill(pe, banks):
            for i in range(n):
                for kt in range(DK):
                    mm = nc.tensor.matmul(banks[0][:, i * 36:(i + 1) * 36], h_t[:, kt, i * P:(i + 1) * P], wr[:, kt, :],
                                          start=(kt == 0), stop=(kt == DK - 1), skip_group_check=True)
            yield mm
        banks_phase(k, [(fill, [("dve", lambda bank: nc.vector.tensor_tensor(
            lg[:], bank[:, 0:n * 36].rearrange("p (i e) -> p i e", e=36), br.unsqueeze(1).to_broadcast([P, n, 36]),
            ALU.add))])])
        g, e = lg[:, :, 0:4], lg[:, :, 4:36]
        b4 = lambda a: a.to_broadcast([P, n, 4])
        b32 = lambda a: a.to_broadcast([P, n, 32])
        desc4, desc32 = descending[:, 28:32].unsqueeze(1), descending[:].unsqueeze(1)

        def first_max(v, out, vals, top, weight, desc, spread):
            yield v.tensor_reduce(top, vals, AX.X, ALU.max)
            yield v.tensor_tensor(weight, vals, spread(top), ALU.is_equal)
            yield v.tensor_tensor(weight, weight, spread(desc), ALU.mult)
            yield v.tensor_reduce(r1[:, :, 7:8], weight, AX.X, ALU.max)
            yield v.tensor_tensor(out, weight, spread(r1[:, :, 7:8]), ALU.is_equal)

        def choose(v):
            yield from first_max(v, one[:], g, r1[:, :, 0:1], w4[:], desc4, b4)
            yield v.tensor_tensor(ex[:], g, b4(r1[:, :, 0:1]), ALU.subtract)
            yield v.tensor_scalar(w4[:], one[:], -1.0, -NEG, ALU.add, ALU.mult)
            tile = lambda a, i: a[:, i, :].rearrange("p (g x) -> p g x", g=4)
            of_group = lambda a, i: a[:, i, :].unsqueeze(2).to_broadcast([P, 4, 8])
            yield [v.tensor_tensor(tile(em, i), tile(e, i), of_group(one, i), ALU.mult) for i in range(n)]
            yield [v.tensor_tensor(tile(em, i), tile(em, i), of_group(w4, i), ALU.add) for i in range(n)]
            yield from first_max(v, pick[:, :, 0, :], em[:], r1[:, :, 1:2], w32[:], desc32, b32)
            yield v.scalar_tensor_tensor(out=em[:], in0=pick[:, :, 0, :], scalar=2 * NEG, in1=em[:], op0=ALU.mult,
                                         op1=ALU.add)
            yield from first_max(v, pick[:, :, 1, :], em[:], r1[:, :, 2:3], w32[:], desc32, b32)
            yield v.tensor_tensor(r1[:, :, 3:4], r1[:, :, 2:3], r1[:, :, 1:2], ALU.subtract)
        vector_phase(k, choose)
        scalar_phase(k, lambda s: [s.activation(ex[:], ex[:], ACT.Exp),
                                   s.activation(r1[:, :, 3:4], r1[:, :, 3:4], ACT.Exp)])

        def weigh(v):
            yield v.tensor_reduce(r1[:, :, 4:5], ex[:], AX.X, ALU.add)
            yield v.tensor_scalar(r1[:, :, 5:6], r1[:, :, 3:4], 1.0, None, ALU.add)
            yield v.tensor_tensor(r1[:, :, 4:5], r1[:, :, 4:5], r1[:, :, 5:6], ALU.mult)
            yield v.reciprocal(r1[:, :, 4:5], r1[:, :, 4:5])
            yield v.tensor_copy(weight[:, :, 0:1], r1[:, :, 4:5])
            yield v.tensor_tensor(weight[:, :, 1:2], r1[:, :, 4:5], r1[:, :, 3:4], ALU.mult)
        vector_phase(k, weigh)


def place_tokens(k, l, n_tiles, tables, pick, table_at, row_at, control, n_blocks):
    nc, sb = k.nc, k.sb
    n, more = n_tiles, n_blocks - 32
    with ExitStack() as tmp:
        before, number = tables["before"], tables["number"]
        ones = sb(f"p_ones{l}", [P, P], where=tmp)
        chosen = sb(f"chosen{l}", [P, n, 32], where=tmp)
        rank = sb(f"rank{l}", [P, n, 32], where=tmp)
        blk = sb(f"blk{l}", [P, n, 32], where=tmp)
        away = sb(f"away{l}", [P, n, 32], where=tmp)
        extra = sb(f"extra{l}", [P, 32], where=tmp)
        extra_end = sb(f"extra_end{l}", [P, 32], where=tmp)
        ends = sb(f"ends{l}", [P, more, 32], where=tmp)
        ctl = sb(f"ctl{l}", [P, 16], where=tmp)
        at_f = sb(f"at_f{l}", [P, 2, n, 2], where=tmp)
        picked = sb(f"picked{l}", [P, 2, 2, n, 32], where=tmp)
        def choose(v):
            yield [v.memset(ones[:], 1.0), v.tensor_tensor(chosen[:], pick[:, :, 0, :], pick[:, :, 1, :], ALU.add)]
        vector_phase(k, choose)

        def count(pe, banks):
            for i in range(n):
                for j in range(i + 1):
                    nc.tensor.matmul(banks[0][:, i * 32:i * 32 + 32], (before if j == i else ones)[:], chosen[:, j, :],
                                     start=(j == 0), stop=(j == i), skip_group_check=True)
            for j in range(n):
                mm = nc.tensor.matmul(banks[1][:, 0:32], ones[:], chosen[:, j, :], start=(j == 0), stop=(j == n - 1))
            yield mm

        banks_phase(k, [(count, [
            ("dve", lambda bank: nc.vector.tensor_copy(rank[:].rearrange("p i e -> p (i e)"), bank[:, 0:n * 32])),
            ("dve", lambda bank: nc.vector.tensor_scalar(extra[:], bank[:, 0:32], -(SLOT + 1) / 2, 1.0 / SLOT,
                                                         ALU.add, ALU.mult))])])
        magic = 12582912.0

        def place(v):
            yield [v.tensor_scalar(extra[:], extra[:], magic, None, ALU.add),
                   v.tensor_scalar(blk[:], rank[:], -(SLOT - 1) / 2, 1.0 / SLOT, ALU.add, ALU.mult)]
            yield [v.tensor_scalar(extra[:], extra[:], -magic, 0.0, ALU.add, ALU.max),
                   v.tensor_scalar(blk[:], blk[:], magic, None, ALU.add), v.memset(ctl[:], 0.0)]
            yield [v.tensor_tensor_scan(extra_end[:], ones[:, 0:32], extra[:], 0.0, ALU.mult, ALU.add),
                   v.tensor_scalar(blk[:], blk[:], -magic, None, ALU.add)]
            yield [v.scalar_tensor_tensor(out=rank[:], in0=blk[:], scalar=-float(SLOT), in1=rank[:], op0=ALU.mult,
                                          op1=ALU.add),
                   v.tensor_tensor(extra[:], extra_end[:], extra[:], ALU.subtract),
                   v.tensor_tensor(ends[:], extra_end[:].unsqueeze(1).to_broadcast([P, more, 32]),
                                   number[:, 0:more].unsqueeze(2).to_broadcast([P, more, 32]), ALU.is_le)]
            yield [v.scalar_tensor_tensor(out=extra[:], in0=extra[:], scalar=31.0, in1=number[:], op0=ALU.add,
                                          op1=ALU.subtract),
                   v.tensor_reduce(ctl[:, 1:1 + more], ends[:], AX.X, ALU.add)]
            yield [v.tensor_tensor(away[:], blk[:], extra[:].unsqueeze(1).to_broadcast([P, n, 32]), ALU.add),
                   v.tensor_scalar(ctl[:, 1:1 + more], ctl[:, 1:1 + more], 31.0, None, ALU.min),
                   v.tensor_copy(ctl[:, 0:1], extra_end[:, 31:32])]
            yield [v.scalar_tensor_tensor(out=blk[:], in0=blk[:], scalar=0.5, in1=away[:], op0=ALU.is_ge,
                                          op1=ALU.mult),
                   v.tensor_copy(control[:], ctl[0:1, :])]
            yield v.tensor_tensor(blk[:], blk[:], number[:].unsqueeze(1).to_broadcast([P, n, 32]), ALU.add)
            yield v.scalar_tensor_tensor(out=away[:], in0=blk[:], scalar=float(SLOT), in1=rank[:], op0=ALU.mult,
                                         op1=ALU.add)
            yield v.scalar_tensor_tensor(out=rank[:], in0=rank[:], scalar=float(n_blocks), in1=blk[:], op0=ALU.mult,
                                         op1=ALU.add)
            both = [(c, which, value) for c in range(2) for which, value in enumerate((rank, away))]
            yield [v.tensor_tensor(picked[:, which, c], pick[:, :, c, :], value[:], ALU.mult)
                   for c, which, value in both]
            yield [v.tensor_reduce(at_f[:, which, :, c], picked[:, which, c], AX.X, ALU.add)
                   for c, which, value in both]
            yield [v.tensor_copy(table_at[:], at_f[:, 0]), v.tensor_copy(row_at[:], at_f[:, 1])]
        vector_phase(k, place)


def experts(k, t, l, x, h_t, gates, n_tiles, tables):
    nc, sb = k.nc, k.sb
    n_tok = n_tiles * P
    more = 2 * n_tok // (SLOT + 1)
    n_blocks = 32 + more
    h_rows = nc.dram_tensor(f"h_rows{l}", (n_tok, D), F32).ap()
    table = nc.dram_tensor(f"slot_table{l}", (SLOT * n_blocks, 1), U32).ap()
    y_rows = nc.dram_tensor(f"y_rows{l}", (SLOT * n_blocks, D), F32).ap()
    row_of = lambda ap: bass.IndirectOffsetOnAxis(ap=ap, axis=0)
    with ExitStack() as moe:
        pick = sb(f"pick{l}", [P, n_tiles, 2, 32], where=moe)
        weight = sb(f"weight{l}", [P, n_tiles, 2], where=moe)
        table_at = sb(f"table_at{l}", [P, n_tiles, 2], U32, where=moe)
        row_at = sb(f"row_at{l}", [P, n_tiles, 2], U32, where=moe)
        control = sb(f"control{l}", [1, 16], I32, where=moe)
        slots = sb(f"slots{l}", [SLOT, n_blocks], U32, where=moe)
        with ExitStack() as wide:
            k.widen(wide, l)
            with ExitStack() as tmp:
                rows = sb(f"h_row_tiles{l}", [P, n_tiles, D], where=tmp)
                groups = transpose_groups(k, [
                    ([h_t[:, kt, i * P:(i + 1) * P] for kt in range(4 * half, 4 * half + 4)],
                     lambda who, bank, i=i, half=half: copy_by(k, who, rows[:, i, half * BANK:(half + 1) * BANK], bank))
                    for i in range(n_tiles) for half in range(2)])
                banks_phase(k, groups)
                with nc.Block(no_gpsimd_drain=True) as block:
                    @block.scalar
                    def _(act):
                        k.store_done.mark(act.dma_start(h_rows.rearrange("(t p) d -> p t d", p=P), rows[:]), 16)

                    @block.sync
                    def _(sp):
                        k.pump(sp)
                route(k, l, h_t, n_tiles, tables, pick, weight)
                place_tokens(k, l, n_tiles, tables, pick, table_at, row_at, control, n_blocks)
                token = sb(f"token{l}", [P, n_tiles], U32, where=tmp)
                zeros = sb(f"slot_zeros{l}", [SLOT, n_blocks], U32, where=tmp)
                zero_row = sb(f"zero_row{l}", [SLOT, D], where=tmp)
                with nc.Block(no_gpsimd_drain=True) as block:
                    @block.vector
                    def _(dve):
                        chain(dve, k.dve_step, nc.vector.memset(zero_row[:], 0.0))

                    @block.scalar
                    def _(act):
                        act.wait_ge(k.dve_step.sem, k.dve_step.n)
                        k.store_done.mark(act.dma_start(y_rows[32 * SLOT:, :].rearrange("(b r) d -> r b d", r=SLOT),
                                                        zero_row[:].unsqueeze(1).to_broadcast([SLOT, more, D])), 16)

                    @block.gpsimd
                    def _(pool):
                        chain(pool, k.pool_step, nc.gpsimd.iota(token[:], [[P, n_tiles]], base=0, channel_multiplier=1))
                        chain(pool, k.pool_step, nc.gpsimd.memset(zeros[:], 0))
                        k.soft_done.mark(pool.dma_start(table.rearrange("(r b) o -> r (b o)", r=SLOT), zeros[:]), 16)
                        pool.wait_ge(k.soft_done.sem, k.soft_done.n)
                        for i in range(n_tiles):
                            for c in range(2):
                                k.soft_done.mark(nc.gpsimd.indirect_dma_start(table, row_of(table_at[:, i, c:c + 1]),
                                                                              token[:, i:i + 1], None), 16)
                        pool.wait_ge(k.soft_done.sem, k.soft_done.n)
                        k.soft_done.mark(pool.dma_start(slots[:], table.rearrange("(r b) o -> r (b o)", r=SLOT)), 16)
                        pool.wait_ge(k.soft_done.sem, k.soft_done.n)
                        pool.wait_ge(k.store_done.sem, k.store_done.n)

                    @block.sync
                    def _(sp):
                        k.pump(sp)
            stop_at(f"route{l}")
            with ExitStack() as tmp:
                first_blocks(k, l, tmp, h_rows, y_rows, slots, row_of)
        stop_at(f"first{l}")
        with ExitStack() as tmp:
            further_blocks(k, t, l, tmp, more, h_rows, y_rows, slots, control, row_of)
        with ExitStack() as tmp:
            got = sb(f"y_got{l}", [P, 4, D], where=tmp)
            turns_ = [(i, c) for i in range(n_tiles) for c in range(2)]
            used_at = []
            with nc.Block(no_gpsimd_drain=True) as block:
                @block.vector
                def _(dve):
                    v = nc.vector
                    for m, (i, c) in enumerate(turns_):
                        g = got[:, m % 4, :]
                        if c == 0:
                            used_at.append(None)
                            continue
                        dve.wait_ge(k.gathered[m % 4].sem, k.gathered[m % 4].n + 16 * (m // 4 + 1))
                        dve.wait_ge(k.act_step.sem, k.act_step.n + i + 1)
                        f = got[:, (m - 1) % 4, :]
                        chain(dve, k.dve_step, v.scalar_tensor_tensor(out=g, in0=g, scalar=weight[:, i, 1:2], in1=f,
                                                                      op0=ALU.mult, op1=ALU.add))
                        used_at[m - 1] = k.dve_step.n
                        chain(dve, k.dve_step, v.tensor_tensor(g, g, gates[:, 0 if i < T_LAT else 1, 1, :], ALU.mult))
                        chain(dve, k.dve_step, v.tensor_tensor(x[:, i, :], x[:, i, :], g, ALU.add))
                        used_at.append(k.dve_step.n)

                @block.scalar
                def _(act):
                    for i in range(n_tiles):
                        act.wait_ge(k.gathered[2 * i % 4].sem, k.gathered[2 * i % 4].n + 16 * (i // 2 + 1))
                        g = got[:, 2 * i % 4, :]
                        k.act_step.mark(nc.scalar.mul(g, g, weight[:, i, 0:1]))

                @block.gpsimd
                def _(pool):
                    for m, (i, c) in enumerate(turns_):
                        if m >= 4:
                            pool.wait_ge(k.dve_step.sem, used_at[m - 4])
                        k.gathered[m % 4].mark(nc.gpsimd.indirect_dma_start(got[:, m % 4, :], None, y_rows,
                                                                            row_of(row_at[:, i, c:c + 1])), 16)

                @block.sync
                def _(sp):
                    g = k.gathered[(len(turns_) - 1) % 4]
                    sp.wait_ge(g.sem, g.n)
                    k.pump(sp)


def first_blocks(k, l, tmp, h_rows, y_rows, slots, row_of):
    nc, sb = k.nc, k.sb
    xg = sb(f"x_gathered{l}", [SLOT, 3, D], where=tmp)
    xt = sb(f"x_slots_t{l}", [P, 2, DK, SLOT], where=tmp)
    silu = sb(f"silu{l}", [P, 256], where=tmp)
    hid = sb(f"hid{l}", [P, 256], where=tmp)
    hid_t = sb(f"hid_t{l}", [P, 2, P], where=tmp)
    y_sb = sb(f"y_sb{l}", [P, 2, BANK], where=tmp)
    gathered0 = [g.n for g in k.gathered]
    stored0 = [s.n for s in k.stored]
    turned_at, silu_at, y_at = {}, {}, {}
    groups = []

    def store(act, e):
        act.wait_ge(k.act_evac.sem, y_at[e])
        for half in range(2):
            k.stored[e % 2].mark(act.dma_start(y_rows[e * SLOT:(e + 1) * SLOT, half * BANK:(half + 1) * BANK],
                                               y_sb[64 * half:64 * half + SLOT, e % 2, :]), 16)

    def turn_x(e):
        def fill(pe, banks):
            pe.wait_ge(k.gathered[e % 3].sem, gathered0[e % 3] + 16 * (e // 3 + 1))
            for kt in range(DK):
                mm = nc.tensor.transpose(banks[0][:, kt * SLOT:(kt + 1) * SLOT], xg[:, e % 3, kt * P:(kt + 1) * P],
                                         k.ident[0:SLOT, 0:SLOT])
            turned_at[e] = k.tensor_done.n + 1
            yield mm
        return (fill, [("dve", lambda bank: nc.vector.tensor_copy(
            xt[:, e % 2].rearrange("p k s -> p (k s)"), bank))])

    def up(e, empty, who):
        def fill(pe, banks):
            for k0 in range(0, DK, 4):
                w = k.take(pe, 4, BANK)
                mm = hidden(nc, banks[0], xt[:, e % 2], w, k0)
                yield mm
                k.used(k.tensor_done.n)
        return (fill, [(who, empty)], True)

    def silu_out(e):
        def empty(bank):
            if e >= 1:
                store(nc.scalar, e - 1)
            silu_at[e] = k.act_evac.n + 1
            return nc.scalar.activation(silu[:], bank[:, 0:256], ACT.Silu)
        return empty

    def hid_out(e):
        def empty(bank):
            nc.vector.wait_ge(k.act_evac.sem, silu_at[e])
            return nc.vector.tensor_tensor(hid[:], silu[:], bank[:, 0:256], ALU.mult)
        return empty

    def turn_hid(e):
        def fill(pe, banks):
            for b in range(2):
                mm = nc.tensor.transpose(banks[0][:, b * P:(b + 1) * P], hid[:, b * P:(b + 1) * P], k.ident[:])
            yield mm
        return (fill, [("dve", lambda bank: nc.vector.tensor_copy(hid_t[:].rearrange("p b s -> p (b s)"),
                                                                  bank[:, 0:256]))], True)

    def down(e):
        def fill(pe, banks):
            w = [k.take(pe, 4, BANK), k.take(pe, 4, BANK)]
            yield outward(nc, banks[0], hid_t, w)
            k.used(k.tensor_done.n)
            k.used(k.tensor_done.n)

        def empty(bank):
            if e >= 2:
                nc.scalar.wait_ge(k.stored[e % 2].sem, stored0[e % 2] + 32 * (e // 2))
            y_at[e] = k.act_evac.n + 1
            return nc.scalar.copy(y_sb[:, e % 2, :], bank)
        return (fill, [("act", empty)], True)

    groups.append(turn_x(0))
    for e in range(32):
        if e + 1 < 32:
            groups.append(turn_x(e + 1))
        groups += [up(e, silu_out(e), "act"), up(e, hid_out(e), "dve"), turn_hid(e), down(e)]

    def gathers(pool):
        for e in range(32):
            if e >= 3:
                pool.wait_ge(k.tensor_done.sem, turned_at[e - 3])
            k.gathered[e % 3].mark(nc.gpsimd.indirect_dma_start(xg[:, e % 3, :], None, h_rows,
                                                                row_of(slots[:, e:e + 1])), 16)

    def last(act):
        store(act, 31)
        for s in k.stored:
            act.wait_ge(s.sem, s.n)
    k.pump_to = k.taken + 6 * 32
    banks_phase(k, groups, gathers, last)
    k.pump_to = None


def hidden(nc, bank, xt, w, k0):
    for j in range(4):
        for half in range(2):
            mm = nc.tensor.matmul(bank[64 * half:64 * half + SLOT, 0:256], xt[:, k0 + j, :],
                                  w[:, j, 256 * half:256 * half + 256], start=(k0 + j == 0), stop=(k0 + j == DK - 1))
    return mm


def outward(nc, bank, hid_t, w):
    for j in range(4):
        for half in range(2):
            mm = nc.tensor.matmul(bank[64 * half:64 * half + SLOT, :], hid_t[:, j % 2, 64 * (j // 2):64 * (j // 2) + SLOT],
                                  w[half][:, j, :], start=(j == 0), stop=(j == 3))
    return mm


def further_blocks(k, t, l, tmp, more, h_rows, y_rows, slots, control, row_of):
    nc, sb = k.nc, k.sb
    sem = lambda name: k.ctx.enter_context(nc.semaphore(f"further_{name}{l}"))
    x_in, pe_done, dve_done, act_done, y_out = (sem(s) for s in ("x", "pe", "dve", "act", "y"))
    weights_in = [sem(s) for s in ("w1", "w3", "w2")]
    w = [sb(f"fw{l}_{i}", [P, 4, BANK], where=tmp) for i in range(6)]
    xg = sb(f"fx{l}", [SLOT, D], where=tmp)
    xt = sb(f"fxt{l}", [P, DK, SLOT], where=tmp)
    silu = sb(f"fsilu{l}", [P, 256], where=tmp)
    hid = sb(f"fhid{l}", [P, 256], where=tmp)
    hid_t = sb(f"fhid_t{l}", [P, 2, P], where=tmp)
    y_sb = sb(f"fy{l}", [P, BANK], where=tmp)
    w1, w3, w2 = (t[n][l] for n in ("expert_w1", "expert_w3", "expert_w2"))
    half_rows = lambda a, k0: a[:, k0 * P:(k0 + 4) * P, :].rearrange("e (j p) n -> p (e j) n", p=P)
    bank = lambda b: k.psum[:, b, :]
    with nc.Block(no_gpsimd_drain=True) as block:
        @block.sync
        def _(sp):
            n = sp.value_load(control[0:1, 0:1], min_val=0, max_val=more)
            with ExitStack() as taken:
                for j in range(more):
                    taken.enter_context(sp.If(n > j))
                    e = bass.ds(sp.value_load(control[0:1, 1 + j:2 + j], min_val=0, max_val=31), 1)
                    if j >= 1:
                        sp.wait_ge(pe_done, 5 * j)
                    for i, src in enumerate((half_rows(w1[e], 0), half_rows(w1[e], 4), half_rows(w3[e], 0),
                                             half_rows(w3[e], 4), half_rows(w2[e], 0)[:, :, 0:BANK],
                                             half_rows(w2[e], 0)[:, :, BANK:D])):
                        sp.dma_start(w[i][:], src).then_inc(weights_in[i // 2], 16)

        @block.gpsimd
        def _(pool):
            n = pool.value_load(control[0:1, 0:1], min_val=0, max_val=more)
            with ExitStack() as taken:
                for j in range(more):
                    taken.enter_context(pool.If(n > j))
                    if j >= 1:
                        pool.wait_ge(pe_done, 5 * (j - 1) + 1)
                    nc.gpsimd.indirect_dma_start(xg[:], None, h_rows, row_of(slots[:, 32 + j:33 + j])).then_inc(x_in, 16)

        @block.tensor
        def _(pe):
            n = pe.value_load(control[0:1, 0:1], min_val=0, max_val=more)
            with ExitStack() as taken:
                for j in range(more):
                    taken.enter_context(pe.If(n > j))
                    pe.wait_ge(x_in, 16 * (j + 1))
                    for kt in range(DK):
                        mm = nc.tensor.transpose(bank(0)[:, kt * SLOT:(kt + 1) * SLOT], xg[:, kt * P:(kt + 1) * P],
                                                 k.ident[0:SLOT, 0:SLOT])
                    mm.then_inc(pe_done, 1)
                    pe.wait_ge(dve_done, 3 * j + 1)
                    for b in range(2):
                        pe.wait_ge(weights_in[b], 32 * (j + 1))
                        for half in range(2):
                            mm = hidden(nc, bank(1 + b), xt, w[2 * b + half], 4 * half)
                        mm.then_inc(pe_done, 1)
                    pe.wait_ge(dve_done, 3 * j + 2)
                    for b in range(2):
                        mm = nc.tensor.transpose(bank(3)[:, b * P:(b + 1) * P], hid[:, b * P:(b + 1) * P], k.ident[:])
                    mm.then_inc(pe_done, 1)
                    pe.wait_ge(dve_done, 3 * j + 3)
                    pe.wait_ge(weights_in[2], 32 * (j + 1))
                    outward(nc, bank(4), hid_t, w[4:6]).then_inc(pe_done, 1)

        @block.vector
        def _(dve):
            n = dve.value_load(control[0:1, 0:1], min_val=0, max_val=more)
            with ExitStack() as taken:
                for j in range(more):
                    taken.enter_context(dve.If(n > j))
                    dve.wait_ge(pe_done, 5 * j + 1)
                    nc.vector.tensor_copy(xt[:].rearrange("p k s -> p (k s)"), bank(0)).then_inc(dve_done, 1)
                    dve.wait_ge(pe_done, 5 * j + 3)
                    dve.wait_ge(act_done, 2 * j + 1)
                    nc.vector.tensor_tensor(hid[:], silu[:], bank(2)[:, 0:256], ALU.mult).then_inc(dve_done, 1)
                    dve.wait_ge(pe_done, 5 * j + 4)
                    nc.vector.tensor_copy(hid_t[:].rearrange("p b s -> p (b s)"), bank(3)[:, 0:256]).then_inc(dve_done, 1)

        @block.scalar
        def _(act):
            n = act.value_load(control[0:1, 0:1], min_val=0, max_val=more)
            with ExitStack() as taken:
                for j in range(more):
                    taken.enter_context(act.If(n > j))
                    act.wait_ge(pe_done, 5 * j + 2)
                    nc.scalar.activation(silu[:], bank(1)[:, 0:256], ACT.Silu).then_inc(act_done, 1)
                    act.wait_ge(pe_done, 5 * j + 5)
                    nc.scalar.copy(y_sb[:], bank(4)).then_inc(act_done, 1)
                    act.wait_ge(act_done, 2 * j + 2)
                    for half in range(2):
                        act.dma_start(y_rows[(32 + j) * SLOT:(33 + j) * SLOT, half * BANK:(half + 1) * BANK],
                                      y_sb[64 * half:64 * half + SLOT, :]).then_inc(y_out, 16)
                    act.wait_ge(y_out, 32 * (j + 1))


def second_block(k, t, x, h_t, col, out, late):
    nc, sb = k.nc, k.sb
    with ExitStack() as mix:
        br_t = sb("branches_t", [P, 3, 4, S], where=mix)
        tabs = sb("dil_tabs", [P, T_LAT, 2, P], where=mix)
        angle_program, sine_program = rotation_tables(k, mix, late, tabs)
        norm_to_columns(k, "pre_mix", [x[:, i, :] for i in range(T_LAT)], D, 1e-6, h_t,
                        lambda kt: [(0, S, col("pre_mix", kt), None)])
        gla_branch(k, h_t, col, br_t, late, angle_program, sine_program)
        stop_at("gla")
        dilated_branch(k, t, h_t, br_t, tabs)
        stop_at("dil")
        with ExitStack() as tmp:
            open_ = sb("branch_gates", [P, 24, S], where=tmp)
            merged = sb("merged_t", [P, DK, S], where=tmp)
            part = sb("merge_part", [P, S], where=tmp)
            gain = sb("post_mix_gain", [P, D], where=tmp)
            k.ahead([(gain[:], t["post_mix_g_2"][0].partition_broadcast(P))])
            tok = lambda kt: h_t[:, kt, 0:S]
            banks_phase(k, project_column_groups(
                k, tok, DK, S, 3 * D,
                lambda who, b, h, bank: nc.scalar.activation(open_[:, b, :], bank, ACT.Sigmoid, bias=col("b_gate", b)),
                "act"))
            groups = []
            for g in range(3):
                def merge(who, b, h, bank, g=g):
                    if g == 0:
                        return nc.vector.tensor_tensor(merged[:, b, :], bank, open_[:, b, :], ALU.mult)
                    nc.vector.wait_ge(k.dve_evac.sem, k.dve_evac.n)
                    chain(nc.vector, k.dve_step, nc.vector.tensor_tensor(part[:], bank, open_[:, 8 * g + b, :],
                                                                         ALU.mult))
                    return nc.vector.tensor_tensor(merged[:, b, :], merged[:, b, :], part[:], ALU.add)
                groups += project_column_groups(k, lambda kt, g=g: br_t[:, g, kt, :], 4, S, D, merge, "dve")
            banks_phase(k, groups)
            normed_residual(k, "mix", gain, x, lambda kt, r: merged[:, kt, r * P:(r + 1) * P], DK)
    stop_at("mix2")
    with ExitStack() as ffn:
        hid = sb("ff_hid", [P, 22, S], where=ffn)
        gain = sb("post_ffn_gain", [P, D], where=ffn)
        k.ahead([(gain[:], t["post_ffn_g_2"][0].partition_broadcast(P))])
        norm_to_columns(k, "pre_ffn", [x[:, i, :] for i in range(T_LAT)], D, 1e-6, h_t,
                        lambda kt: [(0, S, col("pre_ffn", kt), None)])
        tok = lambda kt: h_t[:, kt, 0:S]

        def conv(who, b, h, bank):
            v, o = nc.vector, hid[:, b, :]
            chain(v, k.dve_step, v.tensor_scalar(o, bank, col("ffw2", b), col("ff_b", b), ALU.mult, ALU.add))
            chain(v, k.dve_step, v.scalar_tensor_tensor(out=o[:, 1:S], in0=bank[:, 0:S - 1], scalar=col("ffw1", b),
                                                        in1=o[:, 1:S], op0=ALU.mult, op1=ALU.add))
            return v.scalar_tensor_tensor(out=o[:, 2:S], in0=bank[:, 0:S - 2], scalar=col("ffw0", b), in1=o[:, 2:S],
                                          op0=ALU.mult, op1=ALU.add)
        convolved = k.dve_evac.n

        def gelu(act):
            for b in range(22):
                act.wait_ge(k.dve_evac.sem, convolved + b + 1)
                k.act_step.mark(nc.scalar.activation(hid[:, b, :], hid[:, b, :], ACT.Gelu_apprx_tanh))
            act.wait_ge(k.act_step.sem, k.act_step.n)
        banks_phase(k, project_column_groups(k, tok, DK, S, 2816, conv, "dve"), act_last=gelu)
        banks_phase(k, project_column_groups(
            k, tok, DK, S, 2816, lambda who, b, h, bank: nc.vector.tensor_tensor(hid[:, b, :], hid[:, b, :], bank,
                                                                                 ALU.mult), "dve"))
        normed_residual(k, "ffn", gain, x, lambda kt, r: hid[:, kt, r * P:(r + 1) * P], 22)
    with nc.Block(no_gpsimd_drain=True) as block:
        @block.sync
        def _(sp):
            k.store_done.mark(sp.dma_start(out[0].rearrange("(t p) d -> p t d", p=P), x[:, 0:T_LAT, :]), 16)
            sp.wait_ge(k.store_done.sem, k.store_done.n)


def normed_residual(k, tag, g, x, lhs, k_tiles):
    nc, sb = k.nc, k.sb
    with ExitStack() as tmp:
        y = sb(f"y_{tag}_residual", [P, T_LAT, D], where=tmp)
        rs = sb(f"rs_{tag}_residual", [P, T_LAT], where=tmp)
        junk = sb(f"junk_{tag}_residual", [P, 2, D], where=tmp)
        banks_phase(k, project_groups(k, lhs, k_tiles, [P] * T_LAT, D,
                                      lambda who, r, n0, nn, bank: copy_by(k, who, y[:, r, n0:n0 + nn], bank)))
        inv_rms(k, [y[:, i, :] for i in range(T_LAT)], D, 1e-6, rs, [junk[:, 0, :], junk[:, 1, :]])

        def steps(v):
            for i in range(T_LAT):
                yield v.scalar_tensor_tensor(out=y[:, i, :], in0=y[:, i, :], scalar=rs[:, i:i + 1], in1=g[:],
                                             op0=ALU.mult, op1=ALU.mult)
                yield v.tensor_tensor(x[:, i, :], x[:, i, :], y[:, i, :], ALU.add)
        vector_phase(k, steps)


def columns_of(k, h_t, n_cols, dst, who=None):
    return project_column_groups(k, lambda kt: h_t[:, kt, 0:S], DK, S, n_cols,
                                 lambda who, b, h, bank: copy_by(k, who, dst(b, h), bank), who)


def gla_branch(k, h_t, col, br_t, late, angle_program, sine_program):
    nc, sb = k.nc, k.sb
    C, N = 16, S // 16
    with ExitStack() as gla:
        keep = lambda name, shape: sb("gla_" + name, shape, where=gla)
        qk = keep("qk", [P, 4, S])
        v_row = keep("v", [P, T_LAT, 512])
        g_t = keep("g", [P, 4, S])
        a_t = keep("a", [16, S])
        lc = keep("lc", [P, 2, S])
        lag_is, chunk_is, head_is = late["lag_is"], late["chunk_is"], late["head_is"]
        dec = keep("dec", [P, 2, N])
        states = keep("states", [P, 2, N, P])
        q_in = keep("q_in", [P, 2, 2, S])
        ones = keep("ones", [P, P])
        s_t = br_t[:, 2].rearrange("p b s -> p (b s)").rearrange("p (i h j) -> p i h j", i=T_LAT, h=4)
        four = lambda a: a.rearrange("p b (n c) -> p b n c", c=C)
        with ExitStack() as tmp:
            keep2 = lambda name, shape: sb("gla_" + name, shape, where=tmp)
            w_a, r = late["w_alpha_up"], late["within_chunk"]
            z, u = keep2("z", [P, 2, S]), keep2("u", [P, 2, S])
            k_in = keep2("k_in", [P, 2, S])
            groups = columns_of(k, h_t, 512, lambda b, h: qk[:, b, :])
            groups += project_groups(k, lambda kt, i: h_t[:, kt, i * P:(i + 1) * P], DK, [P] * T_LAT, 512,
                                     lambda who, i, n0, nn, bank: copy_by(k, who, v_row[:, i, :], bank))
            groups += columns_of(k, h_t, 528, lambda b, h: g_t[:, b, :] if b < 4 else a_t[:])
            banks_phase(k, groups, dve_first=angle_program)

            def alpha(pe, banks):
                for p in range(2):
                    mm = nc.tensor.matmul(banks[0][:, p * S:(p + 1) * S], w_a[:, p * P:(p + 1) * P], a_t[:],
                                          start=True, stop=True, skip_group_check=True)
                yield mm

            def add_b(bank):
                for p in range(2):
                    ins = nc.vector.tensor_scalar(z[:, p, :], bank[:, p * S:(p + 1) * S], col("b_alpha", p), None,
                                                  ALU.add)
                return ins
            banks_phase(k, [(alpha, [("dve", add_b)])])

            def soft(s):
                yield s.activation(u[:], z[:], ACT.Abs)
                yield s.activation(u[:], u[:], ACT.Exp, scale=-1.0)
                yield s.activation(u[:], u[:], ACT.Ln, bias=1.0)
            scalar_phase(k, soft)

            def sums(v):
                yield [v.memset(ones[:], 1.0), v.tensor_scalar(z[:], z[:], 0.0, None, ALU.min)]
                yield v.tensor_tensor(z[:], z[:], u[:], ALU.subtract)
                yield v.tensor_scalar(z[:], z[:], 1.0 / 16.0, None, ALU.mult)
                yield [v.tensor_tensor_scan(lc[:, p, :], r[:], z[:, p, :], 0.0, ALU.mult, ALU.add)
                       for p in range(2)] + [
                    v.tensor_scalar(qk[:, 0:2, :], qk[:, 0:2, :], 64 ** -0.5, None, ALU.mult)]
                yield v.tensor_tensor(four(z[:]), four(lc[:])[:, :, :, C - 1:C].to_broadcast([P, 2, N, C]),
                                      four(lc[:]), ALU.subtract)
            vector_phase(k, sums)

            def exps(s):
                yield [s.activation(z[:], z[:], ACT.Exp), s.activation(u[:], lc[:], ACT.Exp),
                       s.activation(dec[:].unsqueeze(3), four(lc[:])[:, :, :, C - 1:C], ACT.Exp)]
            scalar_phase(k, exps)

            def ins_(v):
                yield [v.tensor_tensor(k_in[:], qk[:, 2:4, :], z[:], ALU.mult)] + [
                    v.scalar_tensor_tensor(out=q_in[:, :, h, :], in0=qk[:, 0:2, :], scalar=head_is[:, 30 + h:31 + h],
                                           in1=u[:], op0=ALU.mult, op1=ALU.mult) for h in range(2)]
            vector_phase(k, ins_)
            k_row = keep2("k_row", [P, T_LAT, 2, P])
            k_pick = keep2("k_pick", [P, T_LAT, 2, 8, P])
            banks_phase(k, transpose_groups(k, [
                ([k_in[:, p, i * P:(i + 1) * P] for p in range(2)],
                 lambda who, bank, i=i: copy_by(k, who, k_row[:, i].rearrange("p b d -> p (b d)"), bank))
                for i in range(T_LAT)]))

            def pick(v):
                yield [v.tensor_tensor(k_pick[:, i, p], k_row[:, i, p, :].unsqueeze(1).to_broadcast([P, 8, P]),
                                       chunk_is[:].unsqueeze(2).to_broadcast([P, 8, P]), ALU.mult)
                       for i in range(T_LAT) for p in range(2)]
            vector_phase(k, pick)
            groups = []
            for p in range(2):
                for n in range(N - 1):
                    def fill(pe, banks, p=p, n=n):
                        i, c = divmod(n, 8)
                        yield nc.tensor.matmul(banks[0][:, 0:256], k_pick[:, i, p, c, :],
                                               v_row[:, i, 256 * p:256 * p + 256], start=True, stop=True)

                    def empty(bank, p=p, n=n, who=("act", "dve")[n % 2]):
                        copy_by(k, who, states[0:64, p, n + 1, :], bank[0:64, 0:P])
                        return copy_by(k, who, states[64:P, p, n + 1, :], bank[64:P, P:2 * P])
                    groups.append((fill, [(("act", "dve")[n % 2], empty)]))
            banks_phase(k, groups)
        with ExitStack() as tmp:
            s_lag = sb("gla_s_lag", [P, T_LAT, C, 4], where=tmp)
            with ExitStack() as tw:
                z = sb("sc_z", [P, 12, S], where=tw)
                w = sb("gla_w", [P, C, 2, S], where=tw)
                lag_groups, pool_part, act_part, dve_part = lag_sums(k, h_t, w, qk, lc, head_is, late["fold_pick"],
                                                                     s_lag)

                def act_first(act):
                    sine_program(act)
                    act_part(act)

                def dve_first(dve):
                    dve_part(dve)
                    v = nc.vector
                    for n in range(1, N - 1):
                        chain(dve, k.dve_step, [v.scalar_tensor_tensor(
                            out=states[:, p, n + 1, :], in0=states[:, p, n, :], scalar=dec[:, p, n:n + 1],
                            in1=states[:, p, n + 1, :], op0=ALU.mult, op1=ALU.add) for p in range(2)])
                banks_phase(k, columns_of(k, h_t, 1536, lambda b, h: z[:, b, :], "act") + lag_groups,
                            pool_first=pool_part, act_first=act_first, dve_first=dve_first)
                conv_branch(k, z, col, br_t)
            s_mul = sb("gla_s_mul", [P, 4, C, C], where=tmp)
            s_row = sb("gla_s_row", [P, 4, C], where=tmp)
            s_full = sb("gla_s_full", [P, 4, 8, C], where=tmp)
            for i in range(T_LAT):
                def spread(v, i=i):
                    yield [v.tensor_tensor(s_mul[:, h], s_lag[:, i, :, h].unsqueeze(1).to_broadcast([P, C, C]),
                                           lag_is[:].rearrange("p l j -> p j l"), ALU.mult) for h in range(4)]
                    yield v.tensor_reduce(s_row[:], s_mul[:], AX.X, ALU.add)
                    yield [v.tensor_tensor(s_full[:, h], s_row[:, h, :].unsqueeze(1).to_broadcast([P, 8, C]),
                                           chunk_is[:].unsqueeze(2).to_broadcast([P, 8, C]), ALU.mult)
                           for h in range(4)]
                vector_phase(k, spread)
                banks_phase(k, transpose_groups(k, [(
                    [s_full[:, h].rearrange("p n c -> p (n c)") for h in range(4)],
                    lambda who, bank, i=i: copy_by(k, who, s_t[:, i].rearrange("p h j -> p (h j)"), bank))]))
        with ExitStack() as tmp:
            o_t = sb("gla_o", [P, 4, S], where=tmp)
            sq = sb("gla_sq", [P, 4, S], where=tmp)
            groups = []
            for p in range(2):
                def fill(pe, banks, p=p):
                    both = banks[0].rearrange("p (h s) -> p h s", h=2)
                    for i in range(T_LAT):
                        for half in range(2):
                            h = 2 * p + half
                            mm = nc.tensor.matmul(both[:, half, i * P:(i + 1) * P], v_row[:, i, h * P:(h + 1) * P],
                                                  s_t[:, i, h, :], start=(i == 0 and half == 0), stop=False,
                                                  skip_group_check=True)
                    for n in range(1, N):
                        mm = nc.tensor.matmul(both[:, :, n * C:(n + 1) * C], states[:, p, n, :],
                                              q_in[:, p, :, n * C:(n + 1) * C], start=False, stop=(n == N - 1),
                                              skip_group_check=True)
                    yield mm

                who = ("act", "dve")[p]
                groups.append((fill, [(who, lambda bank, who=who, p=p: copy_by(
                    k, who, o_t[:, 2 * p:2 * p + 2, :].rearrange("p h s -> p (h s)"), bank))]))
            banks_phase(k, groups)

            def squares(s):
                yield s.activation(sq[:], o_t[:], ACT.Square)
                yield s.activation(g_t[:], g_t[:], ACT.Silu)
            scalar_phase(k, squares)
            groups = []
            for hp in range(2):
                def fill(pe, banks, hp=hp):
                    yield nc.tensor.matmul(banks[0], ones[:], sq[:, 2 * hp:2 * hp + 2, :].rearrange("p h s -> p (h s)"),
                                           start=True, stop=True)
                groups.append((fill, [("dve", lambda bank, hp=hp: nc.vector.tensor_scalar(
                    (q_in[:, 0] if hp == 0 else lc[:]).rearrange("p h s -> p (h s)"),
                    bank, 1.0 / P, 1e-6, ALU.mult, ALU.add))]))
            banks_phase(k, groups)
            scalar_phase(k, lambda s: [s.activation(a, a, ACT.Sqrt) for a in (q_in[:, 0], lc[:])])

            def finish(v):
                parts = [(a, o_t[:, 2 * hp:2 * hp + 2, :]) for hp, a in enumerate((q_in[:, 0], lc[:]))]
                yield [v.reciprocal(a, a) for a, _ in parts]
                yield [v.tensor_tensor(o, o, a, ALU.mult) for a, o in parts]
                for hp, (_, o) in enumerate(parts):
                    yield v.scalar_tensor_tensor(out=br_t[:, 0, 2 * hp:2 * hp + 2, :], in0=o, scalar=col("gla_g"),
                                                 in1=g_t[:, 2 * hp:2 * hp + 2, :], op0=ALU.mult, op1=ALU.mult)
            vector_phase(k, finish)


def lag_sums(k, h_t, w, qk, lc, head_is, fold_pick, s_lag):
    nc = k.nc
    C = 16
    AHEAD = 4
    qk_lag = lambda lag: h_t[:, 2 * (lag % AHEAD):2 * (lag % AHEAD) + 2, S:2 * S]
    four = lambda a: a.rearrange("p b (n c) -> p b n c", c=C)
    late = lambda a, lag: four(a)[:, :, :, lag:C]
    early = lambda a, lag: four(a)[:, :, :, 0:C - lag]
    sums = w[:, 0].rearrange("p b s -> p (b s)")
    counts = {}
    pool_has = {}
    qk_product = lambda engine, lag: engine.tensor_tensor(
        late(qk_lag(lag), lag), late(qk[:, 0:2, :], lag), early(qk[:, 2:4, :], lag), ALU.mult)
    dve0 = k.dve_step.n
    difference_taken = lambda lag: dve0 + lag + 1
    multiplied = lambda lag: dve0 + C + lag + 1

    def pool_part(pool):
        for lag in range(C):
            if lag >= 1:
                pool_has["zeros", lag] = k.pool_step.mark(nc.gpsimd.memset(four(w[:, lag])[:, :, :, 0:lag], 0.0))
            if lag % 2:
                continue
            if lag >= AHEAD:
                pool.wait_ge(k.dve_step.sem, multiplied(lag - AHEAD))
            pool_has[lag] = k.pool_step.mark(qk_product(nc.gpsimd, lag))
        pool.wait_ge(k.pool_step.sem, k.pool_step.n)

    def act_part(act):
        counts["exp"] = k.act_step.n
        for lag in range(C):
            act.wait_ge(k.dve_step.sem, difference_taken(lag))
            k.act_step.mark(nc.scalar.activation(late(w[:, lag], lag), late(w[:, lag], lag), ACT.Exp))

    def dve_part(dve):
        for lag in range(C):
            k.dve_step.mark(nc.vector.tensor_tensor(late(w[:, lag], lag), late(lc[:], lag), early(lc[:], lag),
                                                    ALU.subtract))
        for lag in range(C):
            if lag % 2 == 0:
                dve.wait_ge(k.pool_step.sem, pool_has[lag])
            else:
                chain(dve, k.dve_own, qk_product(nc.vector, lag))
            dve.wait_ge(k.act_step.sem, counts["exp"] + lag + 1)
            k.dve_step.mark(nc.vector.tensor_tensor(late(w[:, lag], lag), late(w[:, lag], lag),
                                                    late(qk_lag(lag), lag), ALU.mult))

    def sum_heads(pe, banks):
        for lag in range(C):
            if lag >= 1:
                pe.wait_ge(k.pool_step.sem, pool_has["zeros", lag])
            pe.wait_ge(k.dve_step.sem, multiplied(lag))
            mm = nc.tensor.matmul(banks[0][32 * (lag % 4):32 * (lag % 4) + 32, :],
                                  head_is[:, 30 - 2 * lag:62 - 2 * lag],
                                  w[:, lag].rearrange("p b s -> p (b s)"), start=(lag < 4), stop=(lag >= 12))
        yield mm

    def turn_sums(pe, banks):
        for i in range(T_LAT):
            for p in range(2):
                c = (2 * i + p) * 32
                mm = nc.tensor.matmul(banks[0][:, c:c + 32], sums[:, p * S + i * P:p * S + (i + 1) * P], fold_pick[:],
                                      start=True, stop=True, skip_group_check=True)
        yield mm

    def to_s_lag(bank):
        for i in range(T_LAT):
            ins = nc.vector.tensor_copy(s_lag[:, i].rearrange("p c (a h) -> p a c h", a=2),
                                        bank[:, 64 * i:64 * i + 64].rearrange("p (a c h) -> p a c h", a=2, h=2))
        return ins
    groups = [(sum_heads, [("dve", lambda bank: nc.vector.tensor_copy(sums, bank))]),
              (turn_sums, [("dve", to_s_lag)], True)]
    return groups, pool_part, act_part, dve_part


def conv_branch(k, z, col, br_t):
    def steps(v):
        u, o = z[:, 4:8, :], br_t[:, 1]
        yield v.tensor_tensor(u, u, z[:, 8:12, :], ALU.mult)
        yield [v.tensor_scalar(o[:, b, :], u[:, b, :], col("scw2", b), None, ALU.mult) for b in range(4)]
        for back, name in ((1, "scw1"), (2, "scw0")):
            yield [v.scalar_tensor_tensor(out=o[:, b, back:S], in0=u[:, b, 0:S - back], scalar=col(name, b),
                                          in1=o[:, b, back:S], op0=ALU.mult, op1=ALU.add) for b in range(4)]
        yield v.tensor_tensor(o, o, z[:, 0:4, :], ALU.mult)
    vector_phase(k, steps)


def rotation_tables(k, where, late, tabs):
    nc, sb = k.nc, k.sb
    pos_i, inv = late["positions"], late["inv_freq"]
    pos = sb("pos", [P, T_LAT], where=where)
    ang = sb("dil_ang", [P, T_LAT, 2, 64], where=where)
    rnd = sb("dil_rnd", [P, T_LAT, 2, 64], where=where)
    two_pi = 2.0 * math.pi
    hi = 6.28125
    lo = float(np.float32(two_pi - hi))
    magic = 12582912.0

    def angles(v):
        yield v.tensor_copy(pos[:], pos_i[:])
        for i in range(T_LAT):
            yield v.tensor_scalar(ang[:, i, 0, :], inv[:], pos[:, i:i + 1], None, ALU.mult)
            yield v.tensor_scalar(rnd[:, i, 0, :], ang[:, i, 0, :], 1.0 / two_pi, None, ALU.mult)
            yield v.tensor_scalar(rnd[:, i, 1, :], rnd[:, i, 0, :], 0.25, None, ALU.add)
        yield v.tensor_scalar(rnd[:], rnd[:], magic, None, ALU.add)
        yield v.tensor_scalar(rnd[:], rnd[:], -magic, None, ALU.add)
        for i in range(T_LAT):
            yield v.tensor_copy(ang[:, i, 1, :], ang[:, i, 0, :])
        yield v.scalar_tensor_tensor(out=ang[:], in0=rnd[:], scalar=-hi, in1=ang[:], op0=ALU.mult, op1=ALU.add)
        yield v.scalar_tensor_tensor(out=ang[:], in0=rnd[:], scalar=-lo, in1=ang[:], op0=ALU.mult, op1=ALU.add)
        for i in range(T_LAT):
            yield v.tensor_scalar(ang[:, i, 1, :], ang[:, i, 1, :], math.pi / 2, None, ALU.add)
        yield v.tensor_scalar(ang[:], ang[:], 3.1415925, -3.1415925, ALU.min, ALU.max)

    def angle_program(dve):
        for ins in angles(nc.vector):
            chain(dve, k.dve_step, ins)

    def sine_program(act):
        chain(act, k.act_step, [
            nc.scalar.activation(tabs[:, :, 1, 64:P], ang[:, :, 0, :], ACT.Sin),
            nc.scalar.activation(tabs[:, :, 1, 0:64], ang[:, :, 0, :], ACT.Sin, scale=-1.0),
            nc.scalar.activation(tabs[:, :, 0, 0:64], ang[:, :, 1, :], ACT.Sin),
            nc.scalar.activation(tabs[:, :, 0, 64:P], ang[:, :, 1, :], ACT.Sin)])
    return angle_program, sine_program


def dilated_branch(k, t, h_t, br_t, tabs):
    nc, sb = k.nc, k.sb
    with ExitStack() as dil:
        q_t = sb("dil_q_t", [P, 12, S], where=dil)
        k_t = sb("dil_k_t", [P, 12, S], where=dil)
        vv = sb("dil_v", [P, T_LAT, 1536], where=dil)
        y = sb("dil_y", [P, T_LAT, 512], where=dil)
        mask = sb("dil_mask", [P, T_LAT, 3 * S], where=dil)
        k.ahead([(mask[:], t["dil_mask"].rearrange("(t p) k -> p t k", p=P))])
        with ExitStack() as tmp:
            z = sb("dil_z", [P, T_LAT, 3072], where=tmp)
            t1 = sb("dil_t1", [P, BANK], where=tmp)

            def out_of_psum(who, r, n0, nn, bank):
                if n0 < 3072:
                    return rope_out(k, bank, z[:, r, n0:n0 + nn], t1, tabs[:, r, 0, :], tabs[:, r, 1, :], P)
                return copy_by(k, who, vv[:, r, n0 - 3072:n0 - 3072 + nn], bank)
            token_rows = lambda kt, r: h_t[:, kt, r * P:(r + 1) * P]
            banks_phase(k, project_groups(k, token_rows, DK, [P] * T_LAT, 4608, out_of_psum,
                                          lambda r, n0: "dve" if n0 < 3072 else "act"))
            jobs = []
            for half, dst in enumerate((q_t, k_t)):
                for b in range(0, 12, 2):
                    jobs.append(([z[:, i, 1536 * half + (b + a) * P:1536 * half + (b + a + 1) * P]
                                  for a in range(2) for i in range(T_LAT)],
                                 lambda who, bank, b=b, dst=dst: copy_by(
                                     k, who, dst[:, b:b + 2, :].rearrange("p b s -> p (b s)"), bank)))
            banks_phase(k, transpose_groups(k, jobs))
        units = []
        for i in range(T_LAT):
            for h in range(4):
                units.append(dict(
                    qk=[(q_t[:, 4 * g + h, i * P:(i + 1) * P], k_t[:, 4 * g + h, :]) for g in range(3)],
                    v=[vv[:, j, (4 * g + h) * P:(4 * g + h + 1) * P] for g in range(3) for j in range(T_LAT)],
                    mask=mask[:, i, :], sink=None, out=y[:, i, h * P:(h + 1) * P]))
        attention(k, "dil", units, P ** -0.5, 3 * S, P)
        banks_phase(k, transpose_groups(k, [([y[:, i, b * P:(b + 1) * P] for i in range(T_LAT)],
                                             lambda who, bank, b=b: copy_by(k, who, br_t[:, 2, b, :], bank))
                                            for b in range(4)]))


def kernel(**inputs):
    import numpy as _np
    import concourse.bacc as _bacc
    from concourse import mybir as _mybir
    from concourse.bass_utils import run_bass_kernel_spmd as _run

    nc = _bacc.Bacc("TRN2", target_bir_lowering=False, num_devices=1)
    arrays, aps = {}, {}
    for name, a in list(inputs.items()) + list(shape_constants().items()):
        a = _np.ascontiguousarray(a)
        arrays[f"in_{name}_dram"] = a
        aps[name] = nc.dram_tensor(f"in_{name}_dram", a.shape, _mybir.dt.from_np(a.dtype), kind="ExternalInput").ap()
    out = nc.dram_tensor("out_0_dram", (1, S, D), F32, kind="ExternalOutput").ap()
    two_blocks(nc, aps, out)
    r = _run(nc, [arrays], core_ids=[0])
    return r.results[0]["out_0_dram"]
```
